# Optimizing a Trainium2 kernel written in Bass

```python
import math
import jax, jax.numpy as jnp
from jax import lax
import numpy as np

D_MODEL = 1024
BATCH = 1
SEQ = 256
DEPTH = 1
DEC_BATCH = 8
DEC_SEQ = 1
PAST_LEN = 2048
PAGE_SIZE = 128

MIX_W = D_MODEL
CONV_W = MIX_W // 2
CONV_GROUPS = 4
CONV_K = 3
RET_W = MIX_W // 2
RET_HEADS = 4
RET_HD = RET_W // RET_HEADS
RET_CHUNK = 128
ROPE_BASE = 10000.0
PROJ_W = 3 * CONV_W + 4 * RET_W
N_EXPERTS = 32
TOP_K = 4
D_FF = D_MODEL
SWIGLU_LIMIT = 7.0
SWIGLU_ALPHA = 1.702
EXPERT_BLOCK = 128
RMS_EPS = 1e-6
GN_EPS = 1e-5

kernel_name = "hymba_conv_retention_moe_step"

def rmsnorm(x, g):
    xf = x.astype(jnp.float32)
    y = xf * lax.rsqrt(jnp.mean(xf * xf, axis=-1, keepdims=True) + RMS_EPS)
    return (y * g.astype(jnp.float32)).astype(x.dtype)

def rotary(x, positions):
    half = x.shape[-1] // 2
    inv = ROPE_BASE ** (-jnp.arange(half, dtype=jnp.float32) / half)
    ang = positions.astype(jnp.float32)[:, None] * inv[None, :]
    cos, sin = jnp.cos(ang), jnp.sin(ang)
    x1, x2 = x[..., :half], x[..., half:]
    return jnp.concatenate([x1 * cos - x2 * sin, x1 * sin + x2 * cos], axis=-1)

def retention_chunk(S, q, k, v, log_gamma):
    c = q.shape[2]
    pos = jnp.arange(c, dtype=jnp.float32)
    diff = pos[:, None] - pos[None, :]
    causal = diff >= 0
    lg = log_gamma[:, None, None]
    decay = jnp.where(causal, jnp.exp(lg * jnp.where(causal, diff, 0.0)), 0.0)
    scores = jnp.einsum('bhqd,bhkd->bhqk', q, k) * decay[None]
    inner = jnp.einsum('bhqk,bhkd->bhqd', scores, v)
    xi = jnp.exp(log_gamma[:, None] * (pos[None, :] + 1.0))
    cross = jnp.einsum('bhqd,bhde->bhqe', q * xi[None, :, :, None], S)
    zeta = jnp.exp(log_gamma[:, None] * (c - 1.0 - pos[None, :]))
    S_new = jnp.exp(log_gamma * c)[None, :, None, None] * S + jnp.einsum(
        'bhkd,bhke->bhde', k * zeta[None, :, :, None], v)
    return S_new, inner + cross

def retention(q, k, v, S0, log_gamma):
    B, H, L, hd = q.shape
    c = min(RET_CHUNK, L)
    n = L // c

    def to_chunks(t):
        return t.reshape(B, H, n, c, hd).transpose(2, 0, 1, 3, 4)

    S, o = lax.scan(lambda s, qkv: retention_chunk(s, qkv[0], qkv[1], qkv[2], log_gamma),
                    S0, (to_chunks(q), to_chunks(k), to_chunks(v)))
    o = o.transpose(1, 2, 0, 3, 4).reshape(B, H, L, hd)
    return o, S

def token_mixer(xn, pos_offset, conv_state, ret_state, w_in, conv_w, ret_norm, w_out):
    B, L, _ = xn.shape
    proj = xn @ w_in
    cuts = [CONV_W, 2 * CONV_W, 3 * CONV_W, 3 * CONV_W + RET_W,
            3 * CONV_W + 2 * RET_W, 3 * CONV_W + 3 * RET_W]
    xc, gb, gc, q, k, v, g = jnp.split(proj, cuts, axis=-1)

    u = gc * xc
    buf = jnp.concatenate([conv_state.astype(u.dtype), u], axis=1)
    conv_out = sum(conv_w[j] * buf[:, j:j + L] for j in range(CONV_K))
    a_out = gb * conv_out
    new_conv = buf[:, L:]

    positions = pos_offset + jnp.arange(L, dtype=jnp.int32)

    def heads(t):
        return t.astype(jnp.float32).reshape(B, L, RET_HEADS, RET_HD).transpose(0, 2, 1, 3)

    qh = rotary(heads(q), positions)
    kh = rotary(heads(k), positions) * (RET_HD ** -0.5)
    vh = heads(v)
    log_gamma = jnp.log(1.0 - 2.0 ** (-5.0 - jnp.arange(RET_HEADS, dtype=jnp.float32)))
    o, new_ret = retention(qh, kh, vh, ret_state.astype(jnp.float32), log_gamma)
    mu = jnp.mean(o, axis=-1, keepdims=True)
    var = jnp.mean((o - mu) ** 2, axis=-1, keepdims=True)
    o = (o - mu) * lax.rsqrt(var + GN_EPS)
    o = o * ret_norm.astype(jnp.float32).reshape(RET_HEADS, RET_HD)[None, :, None, :]
    o = o.transpose(0, 2, 1, 3).reshape(B, L, RET_W).astype(xn.dtype)
    r_out = jax.nn.silu(g) * o

    y = jnp.concatenate([a_out, r_out], axis=-1) @ w_out
    return y, new_conv, new_ret

def moe(xn, w_router, b_router, w_up, b_up, w_down, b_down):
    Bt, L, D = xn.shape
    x = xn.reshape(-1, D)
    T = x.shape[0]
    logits = (x @ w_router + b_router).astype(jnp.float32)
    top_vals, top_idx = lax.top_k(logits, TOP_K)
    gates = jax.nn.softmax(top_vals, axis=-1).astype(x.dtype)

    N = T * TOP_K
    flat_e = top_idx.reshape(-1).astype(jnp.int32)
    order = jnp.argsort(flat_e).astype(jnp.int32)
    sorted_e = flat_e[order]
    counts = jnp.bincount(flat_e, length=N_EXPERTS).astype(jnp.int32)
    padded = (counts + EXPERT_BLOCK - 1) // EXPERT_BLOCK * EXPERT_BLOCK
    start = jnp.cumsum(counts) - counts
    pend = jnp.cumsum(padded)
    pstart = pend - padded
    dest = pstart[sorted_e] + (jnp.arange(N, dtype=jnp.int32) - start[sorted_e])
    n_blocks = -(-N // EXPERT_BLOCK) + N_EXPERTS
    R = n_blocks * EXPERT_BLOCK
    row_token = jnp.full((R,), T, jnp.int32).at[dest].set(order // TOP_K)
    x_pad = jnp.concatenate([x, jnp.zeros((1, D), x.dtype)], axis=0)
    x_rows = x_pad[row_token].reshape(n_blocks, EXPERT_BLOCK, D)
    block_e = jnp.clip(jnp.searchsorted(pend, jnp.arange(n_blocks, dtype=jnp.int32) * EXPERT_BLOCK,
                                        side='right'), 0, N_EXPERTS - 1)

    def expert_block(args):
        xb, e = args
        h = xb @ w_up[e] + b_up[e]
        h_glu = jnp.minimum(h[:, :D_FF], SWIGLU_LIMIT)
        h_lin = jnp.clip(h[:, D_FF:], -SWIGLU_LIMIT, SWIGLU_LIMIT)
        act = h_glu * jax.nn.sigmoid(SWIGLU_ALPHA * h_glu) * (h_lin + 1.0)
        return act @ w_down[e] + b_down[e]

    y_rows = lax.map(expert_block, (x_rows, block_e)).reshape(R, D)
    dest_of_assign = jnp.zeros((N,), jnp.int32).at[order].set(dest)
    y_assign = y_rows[dest_of_assign].reshape(T, TOP_K, D)
    y = jnp.einsum('tk,tkd->td', gates, y_assign)
    return y.reshape(Bt, L, D)

def decoder_layer(x, pos_offset, conv_state, ret_state, norm_mix, w_in, conv_w, ret_norm,
                  w_out, norm_ffn, w_router, b_router, w_up, b_up, w_down, b_down):
    mix, new_conv, new_ret = token_mixer(rmsnorm(x, norm_mix), pos_offset, conv_state, ret_state,
                                         w_in, conv_w, ret_norm, w_out)
    h = x + mix
    h = h + moe(rmsnorm(h, norm_ffn), w_router, b_router, w_up, b_up, w_down, b_down)
    return h, new_conv, new_ret

def setup_inputs(seed: int = 0) -> dict:
    key = jax.random.key(seed)
    ks = jax.random.split(key, 20)
    f32 = jnp.float32
    nrm = lambda k, s, sc: jax.random.normal(k, s, f32) * sc
    return {
        "x_prompt": nrm(ks[0], (BATCH, SEQ, D_MODEL), 1.0),
        "x_sample": nrm(ks[1], (DEC_BATCH, DEC_SEQ, D_MODEL), 1.0),
        "state_conv": nrm(ks[2], (DEPTH, DEC_BATCH, CONV_K - 1, CONV_W), 1.0),
        "state_ret": nrm(ks[3], (DEPTH, DEC_BATCH, RET_HEADS, RET_HD, RET_HD), 0.5),
        "norm_mix": 1.0 + nrm(ks[4], (DEPTH, D_MODEL), 0.02),
        "w_in": nrm(ks[5], (DEPTH, D_MODEL, PROJ_W), D_MODEL ** -0.5),
        "conv_w": nrm(ks[6], (DEPTH, CONV_K, CONV_W), CONV_K ** -0.5),
        "ret_norm": 1.0 + nrm(ks[7], (DEPTH, RET_W), 0.02),
        "w_out": nrm(ks[8], (DEPTH, MIX_W, D_MODEL), MIX_W ** -0.5),
        "norm_ffn": 1.0 + nrm(ks[9], (DEPTH, D_MODEL), 0.02),
        "w_router": nrm(ks[10], (DEPTH, D_MODEL, N_EXPERTS), D_MODEL ** -0.5),
        "b_router": nrm(ks[11], (DEPTH, N_EXPERTS), 0.01),
        "w_up": nrm(ks[12], (DEPTH, N_EXPERTS, D_MODEL, 2 * D_FF), D_MODEL ** -0.5),
        "b_up": nrm(ks[13], (DEPTH, N_EXPERTS, 2 * D_FF), 0.01),
        "w_down": nrm(ks[14], (DEPTH, N_EXPERTS, D_FF, D_MODEL), D_FF ** -0.5),
        "b_down": nrm(ks[15], (DEPTH, N_EXPERTS, D_MODEL), 0.01),
        "norm_final": 1.0 + nrm(ks[16], (D_MODEL,), 0.02),
    }

def reference(x_prompt, x_sample, state_conv, state_ret, norm_mix, w_in, conv_w, ret_norm,
              w_out, norm_ffn, w_router, b_router, w_up, b_up, w_down, b_down, norm_final):
    hp, hs = x_prompt, x_sample
    conv_p, ret_p, conv_s, ret_s = [], [], [], []
    for l in range(DEPTH):
        params = (norm_mix[l], w_in[l], conv_w[l], ret_norm[l], w_out[l], norm_ffn[l],
                  w_router[l], b_router[l], w_up[l], b_up[l], w_down[l], b_down[l])
        zero_conv = jnp.zeros((hp.shape[0], CONV_K - 1, CONV_W), hp.dtype)
        zero_ret = jnp.zeros((hp.shape[0], RET_HEADS, RET_HD, RET_HD), jnp.float32)
        hp, cp, rp = decoder_layer(hp, 0, zero_conv, zero_ret, *params)
        hs, cs, rs = decoder_layer(hs, PAST_LEN, state_conv[l], state_ret[l], *params)
        conv_p.append(cp); ret_p.append(rp); conv_s.append(cs); ret_s.append(rs)
    y_prompt = rmsnorm(hp, norm_final)
    y_sample = rmsnorm(hs, norm_final)
    return (y_prompt, y_sample, jnp.stack(conv_p), jnp.stack(ret_p), jnp.stack(conv_s), jnp.stack(ret_s))


_drawn_inputs = setup_inputs


def setup_inputs(seed=0):
    import zlib

    import numpy as np

    out = dict(_drawn_inputs(seed))
    spreads = {}
    factors = {'ret_norm': 4.154, 'b_router': 2.799, 'b_up': 8.0, 'b_down': 22.117, 'norm_final': 8.176}
    for name, (base, spread) in spreads.items():
        noise = np.random.default_rng([zlib.crc32(name.encode()), seed]).standard_normal(out[name].shape)
        drawn = base * np.exp(spread * noise) if base else spread * noise
        out[name] = __import__('jax').numpy.asarray(drawn.astype(out[name].dtype))
    for name, factor in factors.items():
        out[name] = (out[name] * factor).astype(out[name].dtype)
    return out
```

```python
from contextlib import ExitStack

import concourse.bass as bass
from concourse import mybir

F32 = mybir.dt.float32
F32R = mybir.dt.float32r
I32 = mybir.dt.int32
U32 = mybir.dt.uint32
ALU = mybir.AluOpType
ACT = mybir.ActivationFunctionType
AX = mybir.AxisListType

P = 128
D = 1024
SEQ = 256
NS = 8
T = SEQ + NS
CT = 3
CONV_W = 512
HEADS = 4
HD = 128
CHUNK = 128
PROJ = 7 * 512
E = 32
TOP = 4
FF = 1024
KT = D // P
CAP = 64
OVER = -(-T // CAP)
TAB_ROWS = OVER * CAP
NOBODY = 1000000
LIMIT = 7.0
ALPHA = 1.702
RMS_EPS = 1e-6
GN_EPS = 1e-5
UC = 8
DC = 4
CPR = UC + DC
SPLIT = 3
TOK = [(0, 128), (128, 128), (256, NS)]
XC, GB, GC, Q, K, V, G = range(7)
ORDER = [K, Q, V, G, GC, XC, GB]


def hybrid_layer(nc, x_prompt, x_sample, state_conv, state_ret, norm_mix, w_in, conv_w, ret_norm, w_out,
                 norm_ffn, w_router, b_router, w_up, b_up, w_down, b_down, norm_final,
                 c_square, c_rope, c_xi, c_route, gammas,
                 y_prompt, y_sample, conv_prompt, ret_prompt, conv_sample, ret_sample):
    xn_dram = nc.dram_tensor("xn_rows", [T, D], F32, kind="Internal").ap()
    acc_dram = nc.dram_tensor("acc_rows", [T, D], F32, kind="Internal").ap()
    tab_dram = nc.dram_tensor("slot_table", [TAB_ROWS * E, 2], I32, kind="Internal").ap()
    tab_rows = tab_dram.rearrange("(s e) two -> s e two", e=E)

    w_up_v = w_up[0].rearrange("e (k p) n -> e k p n", p=P)
    w_down_v = w_down[0].rearrange("e (c k p) n -> e c p k n", p=P, k=2)

    with ExitStack() as top:
        def make(ctx):
            def sb(name, shape, dt=F32):
                return ctx.enter_context(nc.sbuf_tensor(name, shape, dt))
            return sb

        def sem(name):
            return top.enter_context(nc.semaphore(name))

        sb = make(top)
        raw_up = sb("raw_up", [P, UC, 2 * FF])
        ident = sb("ident", [P, P])
        halves = sb("halves", [P, CAP])
        tab = sb("tab", [P, E, 2], I32)
        bias_up = sb("bias_up", [P, 2 * FF // P, E])
        counts = sb("counts", [P, E], I32)
        most = sb("most", [P, 1], I32)
        bank = top.enter_context(nc.psum_tensor("bank", [P, 8, 512], F32))

        landed = [sem(f"landed{s}") for s in range(CPR)]
        acc_init = sem("acc_init")
        out_done = sem("out_done")

        with ExitStack() as ph:
            sb = make(ph)
            w_ring = sb("w_ring", [P, 2, KT, 512])
            x_tok = sb("x_tok", [P, CT, D])
            h_tok = sb("h_tok", [P, CT, D])
            xnt = sb("xnt", [P, KT, T])
            mix_in = sb("mix_in", [P, KT, T])
            kr = sb("kr", [P, HEADS, T])
            qr = sb("qr", [P, HEADS, T])
            vt = sb("vt", [P, HEADS, T])
            sg = sb("sg", [P, HEADS, T])
            tmp = sb("tmp", [P, HEADS, T])
            state = sb("state", [P, NS * HEADS, HD])
            square = sb("square", [P, 7, P])
            rope = sb("rope", [P, 2, T])
            xi = sb("xi", [P, HEADS, CHUNK])
            zeta = sb("zeta", [P, HEADS])
            route = sb("route", [P, E + CT + NS])
            rows = sb("rows", [P, P])
            vec = sb("vec", [P, 88])
            u_pad = sb("u_pad", [P, HEADS, SEQ + 2])
            u_s = sb("u_s", [P, HEADS, NS])
            k_tok = sb("k_tok", [P, 2, HEADS, HD])
            v_tok = sb("v_tok", [P, 2, HEADS, HD])
            small = sb("small", [P, 16])
            fill = sb("fill", [P, TAB_ROWS * E * 2 // P], I32)
            ks_tok = h_tok[0:NS, 0, 0:HEADS * HD]
            vs_tok = h_tok[0:NS, 1, 0:HEADS * HD]
            scores = h_tok[:, 2, :].rearrange("p (c h n) -> p c h n", c=2, h=HEADS)
            q_xi = h_tok[:, 0, 512:1024].rearrange("p (h n) -> p h n", h=HEADS)
            state1 = h_tok[:, 1, 512:1024].rearrange("p (h n) -> p h n", h=HEADS)
            nc_t = sb("nc_t", [P, HEADS, 2 + NS])
            scratch = raw_up[:, UC - 1, :]
            vd = scratch[0:NS, 0:NS * HD].rearrange("p (b e) -> p b e", b=NS)
            nc_rows = scratch[0:2 + NS, 1024:1024 + CONV_W]
            w_rt = scratch[:, 1536:1536 + KT * E].rearrange("p (k e) -> p k e", k=KT)
            b_rt = scratch[:, 1792:1792 + E]
            UPPER, MEAN, ONES, DECAY = 0, 1, 2, 3
            decay = square[:, DECAY:DECAY + HEADS, :]

            x_in = sem("x_in")
            const_in = sem("const_in")
            rows_in = sem("rows_in")
            misc_in = sem("misc_in")
            state_in = sem("state_in")
            win = [sem(f"win{s}") for s in range(2)]
            v_chain = sem("v_chain")
            a_chain = sem("a_chain")
            g_chain = sem("g_chain")
            ssq_done = sem("ssq_done")
            root_done = sem("root_done")
            x_scaled = sem("x_scaled")
            rows_t = sem("rows_t")
            vec_ready = sem("vec_ready")
            xnt_psum = sem("xnt_psum")
            xnt_ready = sem("xnt_ready")
            proj_psum = sem("proj_psum")
            proj_out = sem("proj_out")
            k_rot = sem("k_rot")
            q_rot = sem("q_rot")
            kv_tok_psum = sem("kv_tok_psum")
            kv_tok = sem("kv_tok")
            s_tok_psum = sem("s_tok_psum")
            s_tok = sem("s_tok")
            sc_psum = sem("sc_psum")
            sc_ready = sem("sc_ready")
            kv_psum = sem("kv_psum")
            s1_ready = sem("s1_ready")
            s2_ready = sem("s2_ready")
            o_psum = sem("o_psum")
            o_ready = sem("o_ready")
            vd_ready = sem("vd_ready")
            kvs_psum = sem("kvs_psum")
            snew = sem("snew")
            mean_psum = sem("mean_psum")
            dev_ready = sem("dev_ready")
            var_psum = sem("var_psum")
            std_ready = sem("std_ready")
            mix_ready = sem("mix_ready")
            ncv_ready = sem("ncv_ready")
            ncv_psum = sem("ncv_psum")
            ncv_rows = sem("ncv_rows")
            wo_psum = sem("wo_psum")
            wo_out = sem("wo_out")
            ht_psum1 = sem("ht_psum1")
            h_ready = sem("h_ready")
            ssq2 = sem("ssq2")
            root2 = sem("root2")
            xn_ready = sem("xn_ready")
            xn_stored = sem("xn_stored")
            xn2_psum = sem("xn2_psum")
            xn2_ready = sem("xn2_ready")
            lg_psum = sem("lg_psum")
            top_ready = sem("top_ready")
            exp_ready = sem("exp_ready")
            mask_ready = sem("mask_ready")
            rank_psum = sem("rank_psum")
            rec_ready = sem("rec_ready")
            gm_ready = sem("gm_ready")
            gt_psum = sem("gt_psum")
            gt_ready = sem("gt_ready")
            gb_psum = sem("gb_psum")
            acc_ready = sem("acc_ready")
            fill_done = sem("fill_done")
            filled = sem("filled")
            tabled = sem("tabled")
            tab_in = sem("tab_in")
            bu_in = sem("bu_in")
            bu_psum = sem("bu_psum")
            bu_ready = sem("bu_ready")
            bd_in = sem("bd_in")
            gffn_in = sem("gffn_in")
            eps_ready = sem("eps_ready")
            rank_read = sem("rank_read")
            state1_out = sem("state1_out")
            state_out = sem("state_out")

            rt = kr[:, :, :].rearrange("p h n -> p (h n)")
            logit = rt[:, 0:CT * E].rearrange("p (c e) -> p c e", c=CT)
            top8 = rt[:, 96:96 + CT * 8].rearrange("p (c e) -> p c e", c=CT)
            ranks = rt[:, 120:120 + CT * E].rearrange("p (c e) -> p c e", c=CT)
            gate = rt[:, 216:216 + CT * TOP].rearrange("p (c k) -> p c k", c=CT)
            idxf = rt[:, 228:228 + CT * TOP].rearrange("p (c k) -> p c k", c=CT)
            dest = rt[:, 240:240 + CT * TOP].rearrange("p (c k) -> p c k", c=CT)
            gsum = rt[:, 252:252 + CT]
            mask = rt[:, 256:256 + CT * E].rearrange("p (c e) -> p c e", c=CT)
            gmat = rt[:, 352:352 + CT * E].rearrange("p (c e) -> p c e", c=CT)
            ONEH = CT * TOP * E
            onehot = qr[:, :, :].rearrange("p h n -> p (h n)")[:, 0:ONEH].rearrange("p (c k e) -> p c k e", c=CT, k=TOP)
            prod = vt[:, :, :].rearrange("p h n -> p (h n)")[:, 0:ONEH].rearrange("p (c k e) -> p c k e", c=CT, k=TOP)
            idx8 = sb("idx8", [P, CT, 8], U32)
            dest_i = sb("dest_i", [P, CT * TOP], I32)
            rec = sb("rec", [P, CT, TOP, 2], I32)
            gt = sg[0:E, 0, :]
            g_ffn = w_ring[:, 1, 4:6, :].rearrange("p a b -> p (a b)")
            b_down_sb = w_ring[0:E, 0, 0:2, :].rearrange("p a b -> p (a b)")
            b_up_sb = w_ring[0:E, 1, 0:4, :].rearrange("p a b -> p (a b)")
            xn2 = state[:, 0:24, :].rearrange("p a b -> p (a b)").rearrange("p (c d) -> p c d", c=CT)
            junk = mix_in[:, 0:4, 0:256].rearrange("p a b -> p a b")

            block = ph.enter_context(nc.Block())

            w_in_v = w_in[0].rearrange("(k p) n -> p k n", p=P)
            w_out_v = w_out[0].rearrange("(k p) n -> p k n", p=P)

            def chunk_src(j):
                if j < len(ORDER):
                    return w_in_v[:, :, ORDER[j] * 512:(ORDER[j] + 1) * 512]
                j -= len(ORDER)
                return w_out_v[:, :, j * 512:(j + 1) * 512]

            @block.sync
            def _(sp):
                sp.dma_start(x_tok[:, 0:2, :], x_prompt[0].rearrange("(c p) d -> p c d", p=P)).then_inc(x_in, 16)
                sp.dma_start(x_tok[0:NS, 2, :], x_sample.rearrange("b s d -> (b s) d")).then_inc(x_in, 16)
                sp.dma_start(rows[0:8, :], norm_mix.rearrange("a (k p) -> (a k) p", p=P)).then_inc(rows_in, 16)
                sp.dma_start(rows[8:12, :], ret_norm.rearrange("a (k p) -> (a k) p", p=P)).then_inc(rows_in, 16)
                sp.dma_start(rows[12:24, :], conv_w[0].rearrange("j (m p) -> (j m) p", p=P)).then_inc(rows_in, 16)
                sp.dma_start(rows[24:88, :], state_conv[0].rearrange("b j (m p) -> (b j m) p", p=P)).then_inc(rows_in, 16)
                sp.dma_start(ident[:], c_square[:, 0, :]).then_inc(const_in, 16)
                sp.dma_start(halves[:], c_square[:, 1, 0:CAP]).then_inc(const_in, 16)
                sp.dma_start(square[:], c_square[:, 2:9, :]).then_inc(const_in, 16)
                sp.dma_start(rope[:], c_rope).then_inc(const_in, 16)
                sp.dma_start(xi[:], c_xi[:, 0:HEADS, :]).then_inc(const_in, 16)
                sp.dma_start(zeta[:], c_xi[:, HEADS, 0:HEADS]).then_inc(const_in, 16)
                sp.dma_start(route[:], c_route).then_inc(const_in, 16)
                for j in range(2):
                    sp.dma_start(w_ring[:, j], chunk_src(j)).then_inc(win[j], 16)
                sp.dma_start(state[:], state_ret[0].rearrange("b h d e -> d (b h) e")).then_inc(state_in, 16)
                sp.dma_start(w_rt, w_router[0].rearrange("(k p) e -> p k e", p=P)).then_inc(misc_in, 16)
                sp.dma_start(b_rt, b_router.partition_broadcast(P)[:, 0, :]).then_inc(misc_in, 16)
                sp.wait_ge(fill_done, 1)
                sp.dma_start(tab_dram.rearrange("(p s) two -> p (s two)", p=P), fill[:]).then_inc(filled, 16)
                sp.dma_start(conv_sample[0, :, 0, :], state_conv[0, :, 1, :]).then_inc(out_done, 16)
                for k in range(UC - 1):
                    sp.dma_start(raw_up[:, k, :], w_up_v[0, k]).then_inc(landed[k], 16)
                for j in range(2, 9):
                    if j - 2 < 7:
                        sp.wait_ge(proj_psum, 4 * (j - 1))
                    sp.dma_start(w_ring[:, j % 2], chunk_src(j)).then_inc(win[j % 2], 16)
                sp.wait_ge(s2_ready, 1)
                sp.dma_start(ret_prompt[0, 0].rearrange("h d e -> d h e"), state1).then_inc(state1_out, 16)
                sp.wait_ge(snew, 8)
                sp.dma_start(ret_sample[0].rearrange("b h d e -> d (b h) e"), state[:]).then_inc(state_out, 16)
                sp.wait_ge(ncv_rows, 1)
                sp.dma_start(conv_prompt[0, 0], nc_rows[0:2, :]).then_inc(out_done, 16)
                sp.dma_start(conv_sample[0, :, 1, :], nc_rows[2:2 + NS, :]).then_inc(out_done, 16)
                sp.wait_ge(wo_psum, 4)
                sp.dma_start(b_up_sb, b_up[0]).then_inc(bu_in, 16)
                sp.dma_start(g_ffn, norm_ffn.partition_broadcast(P)[:, 0, :]).then_inc(gffn_in, 16)
                sp.wait_ge(wo_psum, 8)
                sp.dma_start(b_down_sb, b_down[0]).then_inc(bd_in, 16)
                for c, (t0, n) in enumerate(TOK):
                    sp.wait_ge(xn_ready, c + 1)
                    sp.dma_start(xn_dram[t0:t0 + n, :], xn2[0:n, c, :]).then_inc(xn_stored, 16)
                for r in range(2):
                    if r == 0:
                        sp.wait_ge(tabled, 16 * CT * TOP)
                    sp.dma_start(tab[r * CAP:(r + 1) * CAP], tab_rows[0:CAP]).then_inc(tab_in, 16)
                for c, (t0, n) in enumerate(TOK):
                    sp.wait_ge(acc_ready, c + 1)
                    sp.dma_start(acc_dram[t0:t0 + n, :], h_tok[0:n, c, :]).then_inc(acc_init, 16)
                sp.wait_ge(xn_stored, 16 * CT)
                sp.wait_ge(acc_init, 16 * CT)
                sp.wait_ge(tab_in, 32)
                sp.wait_ge(state1_out, 16)
                sp.wait_ge(state_out, 16)

            @block.gpsimd
            def _(pool):
                pool.memset(fill[:], NOBODY).then_inc(fill_done, 1)
                pool.wait_ge(rec_ready, 1)
                pool.wait_ge(filled, 16)
                for c, (t0, n) in enumerate(TOK):
                    for k in range(TOP):
                        col = c * TOP + k
                        pool.indirect_dma_start(
                            tab_dram, bass.IndirectOffsetOnAxis(ap=dest_i[0:n, col:col + 1], axis=0),
                            rec[0:n, c, k, :], None, bounds_check=TAB_ROWS * E - 1, oob_is_err=False,
                        ).then_inc(tabled, 16)
                pool.wait_ge(tabled, 16 * CT * TOP)

            @block.tensor
            def _(pe):
                def turn(out, in_, n, last=None):
                    return pe.transpose(out, in_, ident[0:n, 0:n])

                pe.wait_ge(const_in, 16 * 7)
                pe.wait_ge(rows_in, 64)
                turn(bank[:, 7, 0:88], rows[0:88, :], 88).then_inc(rows_t, 1)
                for k in range(KT):
                    for c, (t0, n) in enumerate(TOK):
                        if k == 0:
                            pe.wait_ge(x_scaled, c + 1)
                        if k == 7 and c == 0:
                            pe.wait_ge(vec_ready, 1)
                        mm = turn(bank[:, k, t0:t0 + n], h_tok[0:n, c, k * P:(k + 1) * P], n)
                    mm.then_inc(xnt_psum, 1)

                def project(j):
                    pe.wait_ge(win[j % 2], 16 * (j // 2 + 1))
                    for m in range(4):
                        i = 4 * j + m
                        if i >= 4:
                            pe.wait_ge(proj_out, i - 3)
                        for k in range(KT):
                            mm = pe.matmul(bank[:, i % 4, 0:T], w_ring[:, j % 2, k, m * P:(m + 1) * P],
                                           xnt[:, k, :], start=(k == 0), stop=(k == KT - 1))
                        mm.then_inc(proj_psum, 1)
                        yield

                def run(j):
                    for _ in project(j):
                        pass

                pe.wait_ge(xnt_ready, KT)
                run(0)
                run(1)
                run(2)
                run(3)
                pe.wait_ge(k_rot, 1)
                pe.wait_ge(proj_out, 12)
                for b, (src, c) in enumerate(((kr, 0), (kr, 1), (vt, 0), (vt, 1))):
                    for h in range(HEADS):
                        mm = turn(bank[:, 4 + b, h * HD:(h + 1) * HD], src[:, h, c * P:(c + 1) * P], P)
                    mm.then_inc(kv_tok_psum, 1)
                run(4)
                pe.wait_ge(kv_tok, 4)
                for b, src in enumerate((kr, vt)):
                    for h in range(HEADS):
                        mm = turn(bank[0:NS, 4 + b, h * HD:(h + 1) * HD], src[:, h, SEQ:T], P)
                    mm.then_inc(s_tok_psum, 1)
                pe.wait_ge(q_rot, 1)
                for c in range(2):
                    for h in range(HEADS):
                        at = slice(c * CHUNK, (c + 1) * CHUNK)
                        mm = pe.matmul(bank[:, 6 + c, h * P:(h + 1) * P], kr[:, h, at], qr[:, h, at],
                                       start=True, stop=True)
                    mm.then_inc(sc_psum, 1)
                run(5)
                pe.wait_ge(sc_ready, 2)
                pe.wait_ge(s_tok, 2)
                for c in range(2):
                    for h in range(HEADS):
                        mm = pe.matmul(bank[:, 6 + c, h * P:(h + 1) * P], k_tok[:, c, h, :], v_tok[:, c, h, :],
                                       start=True, stop=True)
                    mm.then_inc(kv_psum, 1)
                for c in range(2):
                    if c == 1:
                        pe.wait_ge(s1_ready, 1)
                    for h in range(HEADS):
                        mm = pe.matmul(bank[:, 4 + c, h * P:(h + 1) * P], v_tok[:, c, h, :], scores[:, c, h, :],
                                       start=True, stop=(c == 0))
                        if c == 1:
                            mm = pe.matmul(bank[:, 4 + c, h * P:(h + 1) * P], state1[:, h, :], q_xi[:, h, :],
                                           start=False, stop=True)
                    mm.then_inc(o_psum, 1)
                pe.wait_ge(s2_ready, 1)
                for h, _ in enumerate(project(6)):
                    pe.wait_ge(vd_ready, h + 1)
                    for half in range(2):
                        if h > 0:
                            pe.wait_ge(snew, 2 * h - 1 + half)
                        pe.matmul(bank[:, 6 + half, :], ks_tok[:, h * HD:(h + 1) * HD],
                                  vd[:, half * 4:half * 4 + 4, :], start=True, stop=True).then_inc(kvs_psum, 1)
                pe.wait_ge(ncv_ready, 1)
                pe.wait_ge(o_ready, 2)
                for m in range(4):
                    mm = turn(bank[0:2 + NS, 4, m * P:(m + 1) * P], nc_t[:, m, :], P)
                mm.then_inc(ncv_psum, 1)
                pe.wait_ge(snew, 8)
                for h in range(HEADS):
                    for b in range(NS):
                        mm = pe.matmul(bank[:, 5, h * NS + b:h * NS + b + 1], state[:, b * HEADS + h, :],
                                       qr[:, h, SEQ + b:SEQ + b + 1], start=True, stop=True)
                mm.then_inc(o_psum, 1)
                pe.wait_ge(o_ready, 3)
                pe.wait_ge(ncv_rows, 1)
                for h in range(HEADS):
                    pe.matmul(bank[:, 4 + h, 0:T], square[:, MEAN, :], tmp[:, h, :],
                              start=True, stop=True).then_inc(mean_psum, 1)
                for h in range(HEADS):
                    pe.wait_ge(dev_ready, h + 1)
                    pe.matmul(bank[:, 4 + h, 0:T], square[:, MEAN, :], vt[:, h, :],
                              start=True, stop=True).then_inc(var_psum, 1)
                pe.wait_ge(proj_out, 28)
                for m in range(KT):
                    j = 7 + m // 4
                    if m % 4 == 0:
                        pe.wait_ge(win[j % 2], 16 * (j // 2 + 1))
                    if m == 4:
                        pe.wait_ge(std_ready, 4)
                    for k in range(KT):
                        if m == 0 and k == 0:
                            pe.wait_ge(mix_ready, 1)
                        if m == 0 and k == 4:
                            pe.wait_ge(mix_ready, 2)
                        mm = pe.matmul(bank[:, m, 0:T], w_ring[:, j % 2, k, (m % 4) * P:(m % 4 + 1) * P],
                                       mix_in[:, k, :], start=(k == 0), stop=(k == KT - 1))
                    mm.then_inc(wo_psum, 1)
                pe.wait_ge(wo_out, 8)
                for c, (t0, n) in enumerate(TOK):
                    for m in range(KT):
                        mm = turn(bank[0:n, 2 * c + m // 4, (m % 4) * P:(m % 4 + 1) * P], xnt[:, m, t0:t0 + n], P)
                    mm.then_inc(ht_psum1, 1)
                pe.wait_ge(bu_in, 16)
                for j in range(2 * FF // P):
                    mm = turn(bank[:, 6, j * E:(j + 1) * E], b_up_sb[:, j * P:(j + 1) * P], E)
                mm.then_inc(bu_psum, 1)
                pe.wait_ge(h_ready, 3)
                pe.wait_ge(bu_ready, 1)
                for k in range(KT):
                    for c, (t0, n) in enumerate(TOK):
                        if k == 0:
                            pe.wait_ge(xn_ready, c + 1)
                        mm = turn(bank[:, k, t0:t0 + n], xn2[0:n, c, k * P:(k + 1) * P], n)
                    mm.then_inc(xn2_psum, 1)
                pe.wait_ge(xn2_ready, KT)
                for c, (t0, n) in enumerate(TOK):
                    for k in range(KT):
                        mm = pe.matmul(bank[0:n, c, 0:E], xnt[:, k, t0:t0 + n], w_rt[:, k, :],
                                       start=(k == 0), stop=(k == KT - 1))
                    mm.then_inc(lg_psum, 1)
                pe.wait_ge(mask_ready, 1)
                for c, (t0, n) in enumerate(TOK):
                    for b in range(c):
                        pe.matmul(bank[0:n, 3, c * E:(c + 1) * E], square[:, ONES, 0:n], mask[:, b, :],
                                  start=(b == 0), stop=False)
                    pe.matmul(bank[0:n, 3, c * E:(c + 1) * E], square[0:n, UPPER, 0:n], mask[0:n, c, :],
                              start=(c == 0), stop=True)
                for c, (t0, n) in enumerate(TOK):
                    mm = pe.matmul(bank[:, 4, 0:E], square[0:n, ONES, :], mask[0:n, c, :],
                                   start=(c == 0), stop=(c == CT - 1))
                mm.then_inc(rank_psum, 1)
                pe.wait_ge(gm_ready, 1)
                for c, (t0, n) in enumerate(TOK):
                    mm = turn(bank[0:E, 5, t0:t0 + n], gmat[0:n, c, :], n)
                mm.then_inc(gt_psum, 1)
                pe.wait_ge(gt_ready, 1)
                pe.wait_ge(bd_in, 16)
                for c, (t0, n) in enumerate(TOK):
                    b0 = (6, 0, 4)[c]
                    if c == 2:
                        pe.wait_ge(rank_read, 1)
                    for half in range(2):
                        mm = pe.matmul(bank[0:n, b0 + half, :], gt[:, t0:t0 + n],
                                       b_down_sb[:, half * 512:(half + 1) * 512], start=True, stop=True)
                    mm.then_inc(gb_psum, 1)

            @block.scalar
            def _(act):
                chain = [0]

                def link(ins):
                    chain[0] += 1
                    ins.then_inc(a_chain, 1)
                    act.wait_ge(a_chain, chain[0])

                act.wait_ge(x_in, 32)
                for c, (t0, n) in enumerate(TOK):
                    if c:
                        act.wait_ge(ssq_done, c)
                    nc.scalar.activation(junk[0:n], x_tok[0:n, c, :].rearrange("p (a b) -> p a b", a=4), ACT.Square,
                                         accum_out=small[0:n, c:c + 1]).then_inc(ssq_done, 1)
                act.wait_ge(ssq_done, 3)
                act.wait_ge(eps_ready, 2)

                for c, (t0, n) in enumerate(TOK):
                    nc.scalar.activation(small[0:n, 3 + c:4 + c], small[0:n, c:c + 1], ACT.Sqrt,
                                         bias=small[0:n, 15:16], scale=1.0 / D).then_inc(root_done, 1)
                act.wait_ge(rows_t, 1)
                nc.scalar.activation(vec[:], bank[:, 7, 0:88], ACT.Copy).then_inc(vec_ready, 1)
                act.wait_ge(vec_ready, 1)
                for k in range(KT):
                    act.wait_ge(xnt_psum, k + 1)
                    nc.scalar.activation(xnt[:, k, :], bank[:, k, 0:T], ACT.Copy,
                                         scale=vec[:, k:k + 1]).then_inc(xnt_ready, 1)

                def out(j, dst, fn=ACT.Copy):
                    for m in range(4):
                        act.wait_ge(proj_psum, 4 * j + m + 1)
                        nc.scalar.activation(dst[:, m, :], bank[:, m, 0:T], fn).then_inc(proj_out, 1)

                out(0, kr)
                out(1, qr)
                out(2, vt)
                out(3, sg, ACT.Silu)
                for b, dst in ((0, k_tok), (1, k_tok), (2, v_tok), (3, v_tok)):
                    act.wait_ge(kv_tok_psum, b + 1)
                    for h in range(HEADS):
                        ins = nc.scalar.activation(dst[:, b % 2, h, :], bank[:, 4 + b, h * HD:(h + 1) * HD], ACT.Copy,
                                                   scale=zeta[:, h:h + 1] if b < 2 else 1.0)
                    ins.then_inc(kv_tok, 1)
                out(4, mix_in[:, 0:4])
                act.wait_ge(s_tok_psum, 1)
                nc.scalar.activation(ks_tok, bank[0:NS, 4, :], ACT.Copy).then_inc(s_tok, 1)
                act.wait_ge(s_tok_psum, 2)
                nc.scalar.activation(vs_tok, bank[0:NS, 5, :], ACT.Copy).then_inc(s_tok, 1)
                out(5, mix_in[:, 4:8])
                act.wait_ge(q_rot, 2)
                for c in range(2):
                    act.wait_ge(o_psum, c + 1)
                    nc.scalar.activation(tmp[:, :, c * P:(c + 1) * P],
                                         bank[:, 4 + c, :].rearrange("p (h n) -> p h n", h=HEADS),
                                         ACT.Copy).then_inc(o_ready, 1)
                act.wait_ge(ncv_ready, 1)
                out(6, mix_in[:, 4:8])
                act.wait_ge(ncv_psum, 1)
                nc.scalar.activation(nc_rows, bank[0:2 + NS, 4, :], ACT.Copy).then_inc(ncv_rows, 1)
                act.wait_ge(o_psum, 3)
                nc.scalar.activation(tmp[:, :, SEQ:T], bank[:, 5, 0:HEADS * NS].rearrange("p (h n) -> p h n", h=HEADS),
                                     ACT.Copy).then_inc(o_ready, 1)
                for h in range(HEADS):
                    act.wait_ge(var_psum, h + 1)
                    nc.scalar.activation(vt[:, h, :], bank[:, 4 + h, 0:T], ACT.Sqrt,
                                         bias=small[:, 14:15]).then_inc(std_ready, 1)
                for m in range(KT):
                    act.wait_ge(wo_psum, m + 1)
                    nc.scalar.activation(xnt[:, m, :], bank[:, m, 0:T], ACT.Copy).then_inc(wo_out, 1)
                for c, (t0, n) in enumerate(TOK):
                    act.wait_ge(h_ready, c + 1)
                    if c == 0:
                        act.wait_ge(wo_psum, 8)
                    else:
                        act.wait_ge(ssq2, c)
                    nc.scalar.activation(junk[0:n], h_tok[0:n, c, :].rearrange("p (a b) -> p a b", a=4), ACT.Square,
                                         accum_out=small[0:n, 6 + c:7 + c]).then_inc(ssq2, 1)
                act.wait_ge(ssq2, 3)
                for c, (t0, n) in enumerate(TOK):
                    nc.scalar.activation(small[0:n, 9 + c:10 + c], small[0:n, 6 + c:7 + c], ACT.Sqrt,
                                         bias=small[0:n, 15:16], scale=1.0 / D).then_inc(root2, 1)
                act.wait_ge(bu_psum, 1)
                nc.scalar.activation(bias_up[:], bank[:, 6, :].rearrange("p (j e) -> p j e", e=E),
                                     ACT.Copy).then_inc(bu_ready, 1)
                for k in range(KT):
                    act.wait_ge(xn2_psum, k + 1)
                    nc.scalar.activation(xnt[:, k, :], bank[:, k, 0:T], ACT.Copy).then_inc(xn2_ready, 1)
                act.wait_ge(top_ready, 1)
                nc.scalar.activation(gate, gate, ACT.Exp).then_inc(exp_ready, 1)
                act.wait_ge(gt_psum, 1)
                nc.scalar.activation(gt, bank[0:E, 5, 0:T], ACT.Copy).then_inc(gt_ready, 1)

            @block.vector
            def _(dve):
                chain = [0]

                def link(ins):
                    chain[0] += 1
                    ins.then_inc(v_chain, 1)
                    dve.wait_ge(v_chain, chain[0])

                tt, ts, stt = nc.vector.tensor_tensor, nc.vector.tensor_scalar, nc.vector.scalar_tensor_tensor

                nc.vector.memset(small[:, 14:15], GN_EPS).then_inc(eps_ready, 1)
                nc.vector.memset(small[:, 15:16], RMS_EPS).then_inc(eps_ready, 1)
                dve.wait_ge(root_done, 3)
                for c, (t0, n) in enumerate(TOK):
                    link(nc.vector.reciprocal(small[0:n, 3 + c:4 + c], small[0:n, 3 + c:4 + c]))
                    ts(h_tok[0:n, c, :], x_tok[0:n, c, :], small[0:n, 3 + c:4 + c], None, ALU.mult).then_inc(x_scaled, 1)

                def rotate(t, scaled, done):
                    cos = rope[:, 0:1, :].broadcast_to([P, HEADS, T])
                    sin = rope[:, 1:2, :].broadcast_to([P, HEADS, T])
                    tt(tmp[0:64], t[64:128], sin[64:128], ALU.mult).then_inc(v_chain, 1)
                    link(tt(tmp[64:128], t[0:64], sin[0:64], ALU.mult))
                    link(tt(t[:, :, :], t[:, :, :], cos, ALU.mult))
                    if scaled:
                        link(tt(t[:, :, :], t[:, :, :], tmp[:, :, :], ALU.add))
                        ts(t[:, :, :], t[:, :, :], HD ** -0.5, None, ALU.mult).then_inc(done, 1)
                        dve.wait_ge(done, 1)
                    else:
                        tt(t[:, :, :], t[:, :, :], tmp[:, :, :], ALU.add).then_inc(done, 1)
                        dve.wait_ge(done, 1)

                dve.wait_ge(const_in, 16 * 7)
                dve.wait_ge(proj_out, 4)
                chain[0] += 1
                rotate(kr, True, k_rot)
                dve.wait_ge(proj_out, 8)
                chain[0] += 1
                rotate(qr, False, q_rot)
                dve.wait_ge(xnt_psum, KT)
                tt(q_xi, qr[:, :, CHUNK:2 * CHUNK], xi[:], ALU.mult).then_inc(q_rot, 1)
                for c in range(2):
                    dve.wait_ge(sc_psum, c + 1)
                    tt(scores[:, c], bank[:, 6 + c, :].rearrange("p (h n) -> p h n", h=HEADS), decay,
                       ALU.mult).then_inc(sc_ready, 1)
                link(nc.vector.memset(u_pad[:, :, 0:2], 0.0))
                dve.wait_ge(proj_out, 24)
                dve.wait_ge(vec_ready, 1)
                link(tt(u_pad[:, :, 2:SEQ + 2], mix_in[:, 0:4, 0:SEQ], mix_in[:, 4:8, 0:SEQ], ALU.mult))
                link(tt(u_s[:], mix_in[:, 0:4, SEQ:T], mix_in[:, 4:8, SEQ:T], ALU.mult))
                link(nc.vector.tensor_copy(nc_t[:, :, 0:2], u_pad[:, :, SEQ:SEQ + 2]))
                nc.vector.tensor_copy(nc_t[:, :, 2:2 + NS], u_s[:]).then_inc(ncv_ready, 1)
                dve.wait_ge(kv_psum, 1)
                nc.vector.tensor_copy(state1, bank[:, 6, :].rearrange("p (h n) -> p h n", h=HEADS)).then_inc(s1_ready, 1)
                dve.wait_ge(o_psum, 2)
                dve.wait_ge(s1_ready, 1)
                for h in range(HEADS):
                    ins = stt(out=state1[:, h, :], in0=state1[:, h, :], scalar=float(gammas[h][1]),
                              in1=bank[:, 7, h * P:(h + 1) * P], op0=ALU.mult, op1=ALU.add)
                ins.then_inc(s2_ready, 1)
                dve.wait_ge(state_in, 16)
                dve.wait_ge(s_tok, 2)
                eye8 = route[0:NS, E + CT:E + CT + NS]
                for h in range(HEADS):
                    if h:
                        dve.wait_ge(kvs_psum, 2 * h)
                    for b in range(NS):
                        ins = ts(vd[:, b, :], vs_tok[:, h * HD:(h + 1) * HD], eye8[:, b:b + 1], None, ALU.mult)
                    ins.then_inc(vd_ready, 1)
                    for half in range(2):
                        dve.wait_ge(kvs_psum, 2 * h + half + 1)
                        at = state[:, half * 16:half * 16 + 16, :].rearrange("p (b h) e -> p b h e", h=HEADS)[:, :, h, :]
                        stt(out=at, in0=at, scalar=float(gammas[h][0]),
                            in1=bank[:, 6 + half, :].rearrange("p (b e) -> p b e", b=4),
                            op0=ALU.mult, op1=ALU.add).then_inc(snew, 1)
                cw = lambda j, m: vec[:, 12 + j * 4 + m:13 + j * 4 + m]
                past = vec[:, 24:88].rearrange("p (b j m) -> p j m b", b=NS, j=2)
                dve.wait_ge(proj_out, 28)
                for m in range(4):
                    ts(mix_in[:, m, 0:SEQ], u_pad[:, m, 0:SEQ], cw(0, m), None, ALU.mult).then_inc(v_chain, 1)
                    ts(mix_in[:, m, SEQ:T], past[:, 0, m, :], cw(0, m), None, ALU.mult).then_inc(v_chain, 1)
                chain[0] += 8
                dve.wait_ge(v_chain, chain[0])
                for j in range(1, 3):
                    for m in range(4):
                        stt(out=mix_in[:, m, 0:SEQ], in0=u_pad[:, m, j:j + SEQ], scalar=cw(j, m),
                            in1=mix_in[:, m, 0:SEQ], op0=ALU.mult, op1=ALU.add).then_inc(v_chain, 1)
                        src = past[:, 1, m, :] if j == 1 else u_s[:, m, :]
                        stt(out=mix_in[:, m, SEQ:T], in0=src, scalar=cw(j, m), in1=mix_in[:, m, SEQ:T],
                            op0=ALU.mult, op1=ALU.add).then_inc(v_chain, 1)
                    chain[0] += 8
                    dve.wait_ge(v_chain, chain[0])
                tt(mix_in[:, 0:4, :], mix_in[:, 0:4, :], mix_in[:, 4:8, :], ALU.mult).then_inc(mix_ready, 1)
                dve.wait_ge(mix_ready, 1)
                for h in range(HEADS):
                    dve.wait_ge(mean_psum, h + 1)
                    link(tt(tmp[:, h, :], tmp[:, h, :], bank[:, 4 + h, 0:T], ALU.subtract))
                    tt(vt[:, h, :], tmp[:, h, :], tmp[:, h, :], ALU.mult).then_inc(dev_ready, 1)
                for h in range(HEADS):
                    ts(sg[:, h, :], sg[:, h, :], vec[:, 8 + h:9 + h], None, ALU.mult).then_inc(v_chain, 1)
                chain[0] += HEADS
                dve.wait_ge(v_chain, chain[0])
                link(tt(tmp[:, :, :], tmp[:, :, :], sg[:, :, :], ALU.mult))
                dve.wait_ge(std_ready, HEADS)
                link(nc.vector.reciprocal(vt[:, :, :], vt[:, :, :]))
                tt(mix_in[:, 4:8, :], tmp[:, :, :], vt[:, :, :], ALU.mult).then_inc(mix_ready, 1)
                dve.wait_ge(state1_out, 16)
                for c, (t0, n) in enumerate(TOK):
                    dve.wait_ge(ht_psum1, c + 1)
                    tt(h_tok[0:n, c, :].rearrange("p (a b) -> p a b", a=2),
                       x_tok[0:n, c, :].rearrange("p (a b) -> p a b", a=2), bank[0:n, 2 * c:2 * c + 2, :],
                       ALU.add).then_inc(h_ready, 1)
                dve.wait_ge(root2, 3)
                dve.wait_ge(misc_in, 32)
                dve.wait_ge(state_out, 16)
                dve.wait_ge(gffn_in, 16)
                for c, (t0, n) in enumerate(TOK):
                    link(nc.vector.reciprocal(small[0:n, 9 + c:10 + c], small[0:n, 9 + c:10 + c]))
                    stt(out=xn2[0:n, c, :], in0=h_tok[0:n, c, :], scalar=small[0:n, 9 + c:10 + c], in1=g_ffn[0:n, :],
                        op0=ALU.mult, op1=ALU.mult).then_inc(xn_ready, 1)
                link(nc.vector.memset(rt[:, :], 0.0))
                for c, (t0, n) in enumerate(TOK):
                    dve.wait_ge(lg_psum, c + 1)
                    link(tt(logit[0:n, c, :], bank[0:n, c, 0:E], b_rt[0:n, :], ALU.add))
                for c in range(CT):
                    link(nc.vector.max(top8[:, c, :], logit[:, c, :]))
                    nc.vector.max_index(idx8[:, c, :], top8[:, c, :], logit[:, c, :]).then_inc(v_chain, 1)
                    chain[0] += 1
                top = top8[:, :, 0:TOP]
                tt(gate, top, top8[:, :, 0:1].broadcast_to([P, CT, TOP]), ALU.subtract).then_inc(top_ready, 1)
                dve.wait_ge(v_chain, chain[0])
                link(nc.vector.tensor_copy(idxf, idx8[:, :, 0:TOP]))
                iota = route[:, 0:E]
                for k in range(TOP):
                    tt(onehot[:, :, k, :], iota.rearrange("p (a e) -> p a e", a=1).broadcast_to([P, CT, E]),
                       idxf[:, :, k:k + 1].broadcast_to([P, CT, E]), ALU.is_equal).then_inc(v_chain, 1)
                chain[0] += TOP
                dve.wait_ge(v_chain, chain[0])
                nc.vector.tensor_reduce(mask, onehot.rearrange("p c k e -> p c e k"), AX.X, ALU.add).then_inc(mask_ready, 1)
                dve.wait_ge(exp_ready, 1)
                link(nc.vector.tensor_reduce(gsum, gate, AX.X, ALU.add))
                link(nc.vector.reciprocal(gsum, gsum))
                link(tt(gate, gate, gsum.rearrange("p (c a) -> p c a", a=1).broadcast_to([P, CT, TOP]), ALU.mult))
                for k in range(TOP):
                    tt(prod[:, :, k, :], onehot[:, :, k, :], gate[:, :, k:k + 1].broadcast_to([P, CT, E]),
                       ALU.mult).then_inc(v_chain, 1)
                chain[0] += TOP
                dve.wait_ge(v_chain, chain[0])
                nc.vector.tensor_reduce(gmat, prod.rearrange("p c k e -> p c e k"), AX.X, ALU.add).then_inc(gm_ready, 1)
                dve.wait_ge(gm_ready, 1)
                dve.wait_ge(rank_psum, 1)
                for c, (t0, n) in enumerate(TOK):
                    nc.vector.tensor_copy(ranks[0:n, c, :], bank[0:n, 3, c * E:(c + 1) * E]).then_inc(v_chain, 1)
                nc.vector.tensor_copy(counts[:], bank[:, 4, 0:E]).then_inc(rank_read, 1)
                dve.wait_ge(rank_read, 1)
                chain[0] += CT
                dve.wait_ge(v_chain, chain[0])
                for k in range(TOP):
                    tt(prod[:, :, k, :], onehot[:, :, k, :], ranks, ALU.mult).then_inc(v_chain, 1)
                chain[0] += TOP
                dve.wait_ge(v_chain, chain[0])
                link(nc.vector.tensor_reduce(dest, prod, AX.X, ALU.add))
                link(stt(out=dest, in0=dest, scalar=float(E), in1=idxf, op0=ALU.mult, op1=ALU.add))
                nc.vector.tensor_copy(dest_i[:], dest.rearrange("p c k -> p (c k)")).then_inc(v_chain, 1)
                nc.vector.tensor_copy(rec[:, :, :, 0], route[:, E:E + CT].rearrange("p (c a) -> p c a", a=1)
                                      .broadcast_to([P, CT, TOP])).then_inc(v_chain, 1)
                nc.vector.tensor_copy(rec[:, :, :, 1], gate.bitcast(I32)).then_inc(v_chain, 1)
                chain[0] += 3
                dve.wait_ge(v_chain, chain[0])
                nc.vector.tensor_reduce(most[:], counts[:], AX.X, ALU.max).then_inc(rec_ready, 1)
                for c, (t0, n) in enumerate(TOK):
                    b0 = (6, 0, 4)[c]
                    dve.wait_ge(gb_psum, c + 1)
                    h2 = h_tok[0:n, c, :].rearrange("p (a b) -> p a b", a=2)
                    tt(h2, h2, bank[0:n, b0:b0 + 2, :], ALU.add).then_inc(acc_ready, 1)
                dve.wait_ge(acc_ready, 3)

        with ExitStack() as ph:
            sb = make(ph)
            raw_down = sb("raw_down", [P, DC, 2 * D])
            w_high = sb("w_high", [P, SPLIT, 2 * FF], F32R)
            w_low = sb("w_low", [P, SPLIT, 2 * FF], F32R)
            xg = sb("xg", [CAP, D])
            xs = sb("xs", [P, KT, 2 * CAP], F32R)
            h_rows = sb("h_rows", [P, 2 * FF])
            hb = sb("hb", [P, 2 * FF // P, CAP])
            sig = sb("sig", [P, KT, CAP])
            av = sb("av", [P, KT, 2 * CAP], F32R)
            yl = sb("yl", [CAP, D])
            yg = sb("yg", [CAP, D])
            slot_x = sb("slot_x", [CAP, 1], I32)
            slot_y = sb("slot_y", [P, 2], I32)
            fin = sb("fin", [P, CT, D])
            g_fin = sb("g_fin", [P, D])
            st = sb("st", [P, 16])

            high_done = sem("high_done")
            low_done = sem("low_done")
            mm_done = sem("mm_done")
            slot_x_ready = sem("slot_x_ready")
            slot_y_ready = sem("slot_y_ready")
            x_landed = sem("x_landed")
            xt_psum = sem("xt_psum")
            xs_high = sem("xs_high")
            xs_ready = sem("xs_ready")
            h_copied = sem("h_copied")
            ht_psum = sem("ht_psum")
            clamped = sem("clamped")
            sig_ready = sem("sig_ready")
            lin_ready = sem("lin_ready")
            act_ready = sem("act_ready")
            act_high = sem("act_high")
            av_ready = sem("av_ready")
            yl_ready = sem("yl_ready")
            y_ready = sem("y_ready")
            scattered = sem("scattered")
            xg_zero = sem("xg_zero")
            biased = sem("biased")
            all_added = sem("all_added")
            pool_passed = sem("pool_passed")
            pe_passed = sem("pe_passed")
            slots_in = sem("slots_in")
            fin_in = sem("fin_in")
            gf_in = sem("gf_in")
            fin_chain = sem("fin_chain")
            fin_ssq = sem("fin_ssq")
            fin_root = sem("fin_root")
            fin_ready = sem("fin_ready")
            stored = sem("stored")

            block = ph.enter_context(nc.Block())
            H, HT, Y = 0, 4, 6
            LAST = E * CPR

            def up(n, k):
                if isinstance(n, int) and n == 0:
                    return k
                return CPR * n - DC + (k if k < 4 else k + DC)

            def down(n, c):
                if isinstance(n, int) and n == E:
                    return CPR * n - DC + c
                return CPR * n - DC + 4 + c

            def part(j):
                return (CPR - DC + j) % SPLIT

            def parts(n):
                return None

            def chunk_of(n, j):
                if j < 4:
                    kind, i = "up", j
                elif j < 8:
                    kind, i = "down", j - 4
                else:
                    kind, i = "up", j - 4
                pos = up(n, i) if kind == "up" else down(n, i)
                if isinstance(n, int) and n == 0:
                    buf = pos % SPLIT
                elif isinstance(n, int) and n == E:
                    buf = pos % SPLIT
                else:
                    buf = part(j)
                return kind, i, pos, buf

            def each_overflow(eng, body):
                k = eng.alloc_register(f"rounds_{eng.engine.name}")
                eng.reg_mov(k, 0)
                greatest = eng.value_load(most[0:1, 0:1], min_val=0, max_val=T)
                with eng.If(greatest > CAP):
                    with eng.Fori(1, OVER) as r:
                        with eng.Fori(0, E) as e:
                            count = eng.value_load(counts[0:1, bass.ds(e, 1)], min_val=0, max_val=T)
                            with eng.If(count > r * CAP):
                                body(r, e, eng.snap(k, min_val=0, max_val=E * OVER))
                                eng.reg_add(k, k, 1)
                return eng.snap(k, min_val=0, max_val=E * OVER)

            @block.sync
            def _(sp):
                sp.dma_start(g_fin[:], norm_final.rearrange("(a d) -> a d", a=1).partition_broadcast(P)[:, 0, :]).then_inc(gf_in, 16)

                def load(n, j, e, free):
                    kind, i, _, _ = chunk_of(n, j)
                    if free is not None:
                        sp.wait_ge(low_done, free)
                    if kind == "up":
                        sp.dma_start(raw_up[:, i, :], w_up_v[e, i]).then_inc(landed[i], 16)
                    else:
                        sp.dma_start(raw_down[:, i, :].rearrange("p (k n) -> p k n", k=2),
                                     w_down_v[e, i]).then_inc(landed[UC + i], 16)

                sp.dma_start(raw_up[:, UC - 1, :], w_up_v[0, UC - 1]).then_inc(landed[UC - 1], 16)
                for j in range(CPR):
                    if 4 <= j < 8:
                        load(1, j, 0, None)
                    else:
                        load(1, j, 1, chunk_of(0, j)[2] + 1)
                with sp.Fori(2, E) as n:
                    for j in range(CPR):
                        if 4 <= j < 8:
                            load(n, j, n - 1, CPR * n - DC - CPR + j + 1)
                        else:
                            load(n, j, n, CPR * n - DC - CPR + j + 1)
                for j in range(4, 8):
                    load(E, j, E - 1, CPR * (E - 1) - DC + j + 1)

                def overflow(r, e, k):
                    sp.wait_ge(mm_done, k * CPR + LAST)
                    for i in range(UC):
                        sp.dma_start(raw_up[:, i, :], w_up_v[e, i]).then_inc(landed[i], 16)
                    for i in range(DC):
                        sp.dma_start(raw_down[:, i, :].rearrange("p (k n) -> p k n", k=2),
                                     w_down_v[e, i]).then_inc(landed[UC + i], 16)

                each_overflow(sp, overflow)
                sp.wait_ge(all_added, 1)
                sp.dma_start(fin[:, 0:2, :], acc_dram[0:SEQ, :].rearrange("(c p) d -> p c d", p=P)).then_inc(fin_in, 16)
                sp.dma_start(fin[0:NS, 2, :], acc_dram[SEQ:T, :]).then_inc(fin_in, 16)
                for c in range(2):
                    sp.wait_ge(fin_ready, c + 1)
                    sp.dma_start(y_prompt[0, c * P:(c + 1) * P, :], fin[:, c, :]).then_inc(stored, 16)
                sp.wait_ge(fin_ready, 3)
                sp.dma_start(y_sample.rearrange("b s d -> (b s) d"), fin[0:NS, 2, :]).then_inc(stored, 16)
                sp.wait_ge(stored, 48)
                sp.wait_ge(gf_in, 16)
                sp.wait_ge(out_done, 16 * 3)

            @block.gpsimd
            def _(pool):
                rows_of = bass.IndirectOffsetOnAxis

                def carry():
                    pool.sem_inc(pool_passed, 1)

                def gather(n):
                    pool.indirect_dma_start(xg[:], None, xn_dram, rows_of(ap=slot_x[:, 0:1], axis=0),
                                            bounds_check=T - 1, oob_is_err=False).then_inc(x_landed, 16)

                def scatter():
                    pool.indirect_dma_start(acc_dram, rows_of(ap=slot_y[0:CAP, 0:1], axis=0), yg[:], None,
                                            bounds_check=T - 1, oob_is_err=False,
                                            compute_op=ALU.add).then_inc(scattered, 16)

                def take_x(n, at):
                    if not (isinstance(n, int) and n == 0):
                        pool.wait_ge(x_landed, 16 * n)
                    carry()
                    pool.tensor_copy(slot_x[:], tab[0:CAP, at, 0]).then_inc(slot_x_ready, 1)
                    if not (isinstance(n, int) and n == 0):
                        pool.wait_ge(xt_psum, n)
                    pool.wait_ge(slot_x_ready, n + 1)
                    carry()
                    gather(n)

                def add_y(n, at):
                    if not (isinstance(n, int) and n == 0):
                        pool.wait_ge(scattered, 16 * n)
                    carry()
                    pool.tensor_copy(slot_y[:], tab[:, at, :]).then_inc(slot_y_ready, 1)
                    pool.wait_ge(y_ready, n + 1)
                    pool.wait_ge(slot_y_ready, n + 1)
                    carry()
                    scatter()

                pool.memset(xg[:], 0.0).then_inc(xg_zero, 1)
                pool.wait_ge(xg_zero, 1)
                take_x(0, slice(0, 1))
                take_x(1, slice(1, 2))
                pool.wait_ge(acc_init, 16 * CT)
                take_x(2, slice(2, 3))
                add_y(0, 0)
                with pool.Fori(2, E - 1) as n:
                    take_x(n + 1, bass.ds(n + 1, 1))
                    add_y_dyn(pool, n, add_y)
                add_y(E - 2, E - 2)
                add_y(E - 1, E - 1)

                def overflow(r, e, k):
                    n = k + E
                    pool.wait_ge(scattered, 16 * n)
                    carry()
                    src = tab_rows[bass.ds(r * CAP, CAP), bass.ds(e, 1), :].rearrange("p a two -> p (a two)")
                    pool.dma_start(slot_y[0:CAP, :], src).then_inc(slots_in, 16)
                    pool.dma_start(slot_y[CAP:2 * CAP, :], src).then_inc(slots_in, 16)
                    pool.wait_ge(slots_in, k * 32 + 32)
                    carry()
                    pool.tensor_copy(slot_x[:], slot_y[0:CAP, 0:1]).then_inc(slot_x_ready, 1)
                    pool.wait_ge(slot_x_ready, n + 1)
                    carry()
                    gather(n)
                    pool.wait_ge(y_ready, n + 1)
                    carry()
                    scatter()

                k = each_overflow(pool, overflow)
                pool.wait_ge(scattered, k * 16 + 16 * E)
                carry()
                pool.memset(st[:, 15:16], RMS_EPS).then_inc(all_added, 1)

            @block.tensor
            def _(pe):
                def turn_x(n):
                    pe.wait_ge(x_landed, 16 * n + 16)
                    pe.sem_inc(pe_passed, 1)
                    for k in range(KT):
                        mm = pe.transpose(bank[:, Y, k * CAP:(k + 1) * CAP], xg[:, k * P:(k + 1) * P],
                                          ident[0:CAP, 0:CAP])
                    mm.then_inc(xt_psum, 1)

                def turn_h(n):
                    pe.wait_ge(h_copied, 4 * n + 4)
                    if not (isinstance(n, int) and n == 0):
                        pe.wait_ge(biased, n)
                    for j in range(2 * FF // P):
                        mm = pe.matmul(bank[:, HT + j // 8, (j % 8) * CAP:(j % 8 + 1) * CAP],
                                       h_rows[:, j * P:(j + 1) * P], halves[:], start=True, stop=True)
                    mm.then_inc(ht_psum, 1)

                def products(n, j):
                    kind, i, pos, buf = chunk_of(n, j)
                    first = isinstance(n, int) and n == 0
                    pe.wait_ge(high_done, pos + 1)
                    for w in (w_high, w_low):
                        if w is w_low:
                            pe.wait_ge(low_done, pos + 1)
                        for q in range(4):
                            if kind == "up":
                                if i == 0 and w is w_high and not first:
                                    pe.wait_ge(h_copied, 4 * n - 3 + q)
                                mm = pe.matmul(bank[:, H + q, :], xs[:, i, :], w[:, buf, q * 512:(q + 1) * 512],
                                               start=(i == 0 and w is w_high), stop=(i == UC - 1 and w is w_low))
                            else:
                                mm = pe.matmul(bank[:, Y + q % 2, :], av[:, 2 * i + q // 2, :],
                                               w[:, buf, q * 512:(q + 1) * 512],
                                               start=(i == 0 and w is w_high and q < 2),
                                               stop=(i == DC - 1 and w is w_low and q >= 2))
                    mm.then_inc(mm_done, 1)

                def step(n, last=False):
                    pe.wait_ge(xs_ready, n + 1)
                    products(n, 0)
                    turn_h(n - 1)
                    for j in range(1, 4):
                        products(n, j)
                    pe.wait_ge(av_ready, n)
                    for j in range(4, 11):
                        products(n, j)
                    if not last:
                        pe.wait_ge(y_ready, n)
                        turn_x(n + 1)
                    products(n, 11)

                turn_x(0)
                pe.wait_ge(xs_ready, 1)
                for j in (0, 1, 2, 3, 8, 9, 10):
                    products(0, j)
                turn_x(1)
                products(0, 11)
                with pe.Fori(1, E - 1) as n:
                    step(n)
                step(E - 1, last=True)
                turn_h(E - 1)
                pe.wait_ge(av_ready, E)
                for j in range(4, 8):
                    products(E, j)

                def overflow(r, e, k):
                    n = k + E
                    pe.wait_ge(y_ready, n)
                    turn_x(n)
                    pe.wait_ge(xs_ready, n + 1)
                    for i in range(UC):
                        pe.wait_ge(landed[i], k * 16 + 16 * (E + 1))
                        for q in range(4):
                            mm = pe.matmul(bank[:, H + q, :], xs[:, i, :].bitcast(F32),
                                           raw_up[:, i, q * 512:(q + 1) * 512], start=(i == 0), stop=(i == UC - 1))
                        mm.then_inc(mm_done, 1)
                    turn_h(n)
                    pe.wait_ge(av_ready, n + 1)
                    for i in range(DC):
                        pe.wait_ge(landed[UC + i], k * 16 + 16 * (E + 1))
                        for q in range(4):
                            mm = pe.matmul(bank[:, Y + q % 2, :], av[:, 2 * i + q // 2, :].bitcast(F32),
                                           raw_down[:, i, q * 512:(q + 1) * 512],
                                           start=(i == 0 and q < 2), stop=(i == DC - 1 and q >= 2))
                        mm.then_inc(mm_done, 1)

                each_overflow(pe, overflow)

            @block.scalar
            def _(act):
                def high(n, j):
                    kind, i, pos, buf = chunk_of(n, j)
                    src, s = (raw_up, i) if kind == "up" else (raw_down, UC + i)
                    e = n if kind == "up" else n - 1
                    act.wait_ge(landed[s], 16 * e + 16)
                    if not (isinstance(pos, int) and pos < SPLIT):
                        act.wait_ge(mm_done, pos - SPLIT + 1)
                    nc.scalar.activation(w_high[:, buf, :], src[:, i, :], ACT.Copy).then_inc(high_done, 1)

                def x_high(n, used):
                    act.wait_ge(xt_psum, n + 1)
                    if used is not None:
                        act.wait_ge(mm_done, used)
                    nc.scalar.activation(xs[:, :, 0:CAP], bank[:, Y, :].rearrange("p (k s) -> p k s", k=KT),
                                         ACT.Copy).then_inc(xs_high, 1)

                def copy_h(n, used):
                    act.wait_ge(mm_done, used)
                    if not (isinstance(n, int) and n == 0):
                        act.wait_ge(ht_psum, n)
                    for q in range(4):
                        nc.scalar.activation(h_rows[:, q * 512:(q + 1) * 512], bank[:, H + q, :],
                                             ACT.Copy).then_inc(h_copied, 1)

                def sigmoid(n):
                    act.wait_ge(clamped, n + 1)
                    nc.scalar.activation(sig[:], hb[:, 0:KT, :], ACT.Sigmoid, scale=ALPHA).then_inc(sig_ready, 1)

                def act_split(n, used):
                    act.wait_ge(act_ready, n + 1)
                    if used is not None:
                        act.wait_ge(mm_done, used)
                    nc.scalar.activation(av[:, :, 0:CAP], sig[:], ACT.Copy).then_inc(act_high, 1)

                def y_low(n, used):
                    act.wait_ge(mm_done, used)
                    act.wait_ge(slot_y_ready, n + 1) if not over else None
                    if not (isinstance(n, int) and n == 0):
                        act.wait_ge(y_ready, n)
                    nc.scalar.activation(yl[:].rearrange("p (a b) -> p a b", a=2), bank[CAP:2 * CAP, Y:Y + 2, :],
                                         ACT.Copy, scale=slot_y[CAP:2 * CAP, 1:2].bitcast(F32)).then_inc(yl_ready, 1)

                over = False

                def step(n):
                    first = isinstance(n, int) and n == 1
                    high(n, 0)
                    high(n, 1)
                    x_high(n, up(n, 0))
                    copy_h(n - 1, up(n, 0))
                    high(n, 2)
                    high(n, 3)
                    high(n, 4)
                    sigmoid(n - 1)
                    high(n, 5)
                    act_split(n - 1, None if first else up(n, 0) - 4)
                    for j in range(6, 10):
                        high(n, j)
                    y_low(n - 1, down(n, 3) + 1)
                    high(n, 10)
                    high(n, 11)

                x_high(0, None)
                for j in (0, 1, 2, 3, 8, 9, 10, 11):
                    high(0, j)
                step(1)
                with act.Fori(2, E) as n:
                    step(n)
                copy_h(E - 1, up(E, 0))
                high(E, 4)
                high(E, 5)
                sigmoid(E - 1)
                high(E, 6)
                act_split(E - 1, up(E, 0) - 4)
                high(E, 7)
                y_low(E - 1, LAST)

                over = True

                def overflow(r, e, k):
                    n = k + E
                    x_high(n, k * CPR + LAST)
                    copy_h(n, k * CPR + LAST + UC)
                    sigmoid(n)
                    act_split(n, k * CPR + LAST)
                    y_low(n, k * CPR + LAST + CPR)

                each_overflow(act, overflow)
                for c, n in enumerate((P, P, NS)):
                    act.wait_ge(fin_in, 32)
                    if c:
                        act.wait_ge(fin_ssq, c)
                    nc.scalar.activation(h_rows[0:n, 0:D], fin[0:n, c, :], ACT.Square,
                                         accum_out=st[0:n, c:c + 1]).then_inc(fin_ssq, 1)
                act.wait_ge(fin_ssq, 3)
                act.wait_ge(all_added, 1)
                for c, n in enumerate((P, P, NS)):
                    nc.scalar.activation(st[0:n, 3 + c:4 + c], st[0:n, c:c + 1], ACT.Sqrt, bias=st[0:n, 15:16],
                                         scale=1.0 / D).then_inc(fin_root, 1)

            @block.vector
            def _(dve):
                tt, ts, stt = nc.vector.tensor_tensor, nc.vector.tensor_scalar, nc.vector.scalar_tensor_tensor

                def low(n, j):
                    kind, i, pos, buf = chunk_of(n, j)
                    src = raw_up if kind == "up" else raw_down
                    dve.wait_ge(high_done, pos + 1)
                    tt(w_low[:, buf, :], src[:, i, :], w_high[:, buf, :].bitcast(F32), ALU.subtract).then_inc(low_done, 1)

                def x_low(n):
                    dve.wait_ge(xs_high, n + 1)
                    tt(xs[:, :, CAP:2 * CAP], bank[:, Y, :].rearrange("p (k s) -> p k s", k=KT),
                       xs[:, :, 0:CAP].bitcast(F32), ALU.subtract).then_inc(xs_ready, 1)

                def bias_clamp(n, e):
                    dve.wait_ge(ht_psum, n + 1)
                    if not (isinstance(n, int) and n == 0):
                        dve.wait_ge(act_ready, n)
                    tt(hb[:], bank[:, HT:HT + 2, :].rearrange("p a (j s) -> p (a j) s", s=CAP),
                       bias_up[:, :, e].broadcast_to([P, 2 * FF // P, CAP]), ALU.add).then_inc(biased, 1)
                    dve.wait_ge(biased, n + 1)
                    ts(hb[:, 0:KT, :], hb[:, 0:KT, :], LIMIT, None, ALU.min).then_inc(clamped, 1)
                    ts(hb[:, KT:, :], hb[:, KT:, :], LIMIT, -LIMIT, ALU.min, ALU.max).then_inc(lin_ready, 1)

                def activate(n):
                    dve.wait_ge(sig_ready, n + 1)
                    dve.wait_ge(clamped, n + 1)
                    dve.wait_ge(lin_ready, 2 * n + 1)
                    stt(out=hb[:, KT:, :], in0=hb[:, KT:, :], scalar=1.0, in1=hb[:, 0:KT, :],
                        op0=ALU.add, op1=ALU.mult).then_inc(lin_ready, 1)
                    dve.wait_ge(lin_ready, 2 * n + 2)
                    tt(sig[:], sig[:], hb[:, KT:, :], ALU.mult).then_inc(act_ready, 1)

                def act_low(n):
                    dve.wait_ge(act_high, n + 1)
                    dve.wait_ge(act_ready, n + 1)
                    tt(av[:, :, CAP:2 * CAP], sig[:], av[:, :, 0:CAP].bitcast(F32), ALU.subtract).then_inc(av_ready, 1)

                def y_sum(n):
                    dve.wait_ge(yl_ready, n + 1)
                    if not (isinstance(n, int) and n == 0):
                        dve.wait_ge(scattered, 16 * n)
                    stt(out=yg[:].rearrange("p (a b) -> p a b", a=2), in0=bank[0:CAP, Y:Y + 2, :],
                        scalar=slot_y[0:CAP, 1:2].bitcast(F32), in1=yl[:].rearrange("p (a b) -> p a b", a=2),
                        op0=ALU.mult, op1=ALU.add).then_inc(y_ready, 1)

                def step(n, e):
                    low(n, 0)
                    low(n, 1)
                    x_low(n)
                    low(n, 2)
                    low(n, 3)
                    bias_clamp(n - 1, e)
                    low(n, 4)
                    activate(n - 1)
                    low(n, 5)
                    act_low(n - 1)
                    for j in range(6, 10):
                        low(n, j)
                    y_sum(n - 1)
                    low(n, 10)
                    low(n, 11)

                x_low(0)
                for j in (0, 1, 2, 3, 8, 9, 10, 11):
                    low(0, j)
                step(1, slice(0, 1))
                with dve.Fori(2, E) as n:
                    step(n, bass.ds(n - 1, 1))
                low(E, 4)
                bias_clamp(E - 1, slice(E - 1, E))
                low(E, 5)
                activate(E - 1)
                low(E, 6)
                act_low(E - 1)
                low(E, 7)
                y_sum(E - 1)

                def overflow(r, e, k):
                    n = k + E
                    x_low(n)
                    bias_clamp(n, bass.ds(e, 1))
                    activate(n)
                    act_low(n)
                    y_sum(n)

                each_overflow(dve, overflow)
                dve.wait_ge(gf_in, 16)
                for c, n in enumerate((P, P, NS)):
                    dve.wait_ge(fin_root, c + 1)
                    nc.vector.reciprocal(st[0:n, 3 + c:4 + c], st[0:n, 3 + c:4 + c]).then_inc(fin_chain, 1)
                    dve.wait_ge(fin_chain, c + 1)
                    stt(out=fin[0:n, c, :], in0=fin[0:n, c, :], scalar=st[0:n, 3 + c:4 + c], in1=g_fin[0:n, :],
                        op0=ALU.mult, op1=ALU.mult).then_inc(fin_ready, 1)


def add_y_dyn(pool, n, add_y):
    add_y(n - 1, bass.ds(n - 1, 1))


def shape_constants():
    import numpy as np

    f = np.float32
    sq = np.zeros((P, 9, P), f)
    sq[:, 0] = np.eye(P)
    sq[:, 1, 0:CAP] = np.concatenate([np.eye(CAP), np.eye(CAP)])
    sq[:, 2] = np.triu(np.ones((P, P)), 1)
    sq[:, 3] = 1.0 / HD
    sq[:, 4] = 1.0
    lg = np.log(f(1.0) - f(2.0) ** (f(-5.0) - np.arange(HEADS, dtype=f)))
    pos = np.arange(CHUNK, dtype=f)
    diff = pos[None, :] - pos[:, None]
    xi = np.zeros((P, HEADS + 1, CHUNK), f)
    for h in range(HEADS):
        sq[:, 5 + h] = np.where(diff >= 0, np.exp(lg[h] * np.maximum(diff, 0)), 0)
        xi[:, h] = np.exp(lg[h] * (pos + 1))[None, :]
        xi[:, HEADS, h] = np.exp(lg[h] * (CHUNK - 1 - pos))
    half = HD // 2
    inv = (f(10000.0) ** (-np.arange(half, dtype=f) / f(half))).astype(f)
    at = np.concatenate([np.arange(SEQ), np.full(NS, 2048)]).astype(f)
    ang = (at[None, :] * inv[:, None]).astype(f)
    rope = np.zeros((P, 2, T), f)
    rope[:half, 0] = rope[half:, 0] = np.cos(ang)
    rope[:half, 1] = np.sin(ang)
    rope[half:, 1] = -np.sin(ang)
    route = np.zeros((P, E + CT + NS), f)
    route[:, :E] = np.arange(E)
    for c in range(CT):
        route[:, E + c] = np.arange(P) + c * P
    route[:NS, E + CT:] = np.eye(NS)
    gammas = [(float(np.exp(lg[h])), float(np.exp(lg[h] * f(CHUNK)))) for h in range(HEADS)]
    return {"c_square": sq, "c_rope": rope, "c_xi": xi, "c_route": route}, gammas


_INS = ["x_prompt", "x_sample", "state_conv", "state_ret", "norm_mix", "w_in", "conv_w", "ret_norm", "w_out",
        "norm_ffn", "w_router", "b_router", "w_up", "b_up", "w_down", "b_down", "norm_final"]
_OUTS = [(1, SEQ, D), (NS, 1, D), (1, 1, 2, CONV_W), (1, 1, HEADS, HD, HD), (1, NS, 2, CONV_W),
         (1, NS, HEADS, HD, HD)]


def build(nc, inputs):
    import numpy as np

    consts, gammas = shape_constants()
    arrays, args = {}, []
    for name, a in [(n, inputs[n]) for n in _INS] + list(consts.items()):
        a = np.ascontiguousarray(a)
        arrays[f"in_{name}"] = a
        args.append(nc.dram_tensor(f"in_{name}", a.shape, mybir.dt.from_np(a.dtype), kind="ExternalInput").ap())
    outs = [nc.dram_tensor(f"out_{i}", shape, F32, kind="ExternalOutput").ap() for i, shape in enumerate(_OUTS)]
    hybrid_layer(nc, *args, gammas, *outs)
    return arrays


def kernel(**inputs):
    import concourse.bacc as _bacc
    from concourse.bass_utils import run_bass_kernel_spmd as _run

    nc = _bacc.Bacc("TRN2", target_bir_lowering=False, num_devices=1)
    arrays = build(nc, inputs)
    r = _run(nc, [arrays], core_ids=[0])
    return tuple(r.results[0][f"out_{i}"] for i in range(len(_OUTS)))
```

```python
from contextlib import ExitStack

import concourse.bass as bass
from concourse import mybir

F32 = mybir.dt.float32
F32R = mybir.dt.float32r
I32 = mybir.dt.int32
U32 = mybir.dt.uint32
ALU = mybir.AluOpType
ACT = mybir.ActivationFunctionType
AX = mybir.AxisListType

P = 128
D = 1024
SEQ = 256
NS = 8
T = SEQ + NS
CT = 3
CONV_W = 512
HEADS = 4
HD = 128
CHUNK = 128
PROJ = 7 * 512
E = 32
TOP = 4
FF = 1024
KT = D // P
CAP = 64
OVER = -(-T // CAP)
NOBODY = 1 << 20
LIMIT = 7.0
ALPHA = 1.702
RMS_EPS = 1e-6
GN_EPS = 1e-5
UC = 8
DC = 4
CPR = UC + DC
SPLIT = 4
TOK = [(0, 128), (128, 128), (256, NS)]
XC, GB, GC, Q, K, V, G = range(7)
ORDER = [K, Q, V, G, GC, XC, GB]


def hybrid_layer(nc, x_prompt, x_sample, state_conv, state_ret, norm_mix, w_in, conv_w, ret_norm, w_out,
                 norm_ffn, w_router, b_router, w_up, b_up, w_down, b_down, norm_final,
                 c_square, c_rope, c_xi, c_route, c_slots, gammas,
                 y_prompt, y_sample, conv_prompt, ret_prompt, conv_sample, ret_sample):
    acc_dram = nc.dram_tensor("acc_rows", [T, D], F32, kind="Internal").ap()

    w_up_v = w_up[0].rearrange("e (k p) n -> e k p n", p=P)
    w_down_v = w_down[0].rearrange("e (c k p) n -> e c p k n", p=P, k=2)

    with ExitStack() as top:
        def make(ctx):
            def sb(name, shape, dt=F32):
                return ctx.enter_context(nc.sbuf_tensor(name, shape, dt))
            return sb

        def sem(name):
            return top.enter_context(nc.semaphore(name))

        sb = make(top)
        raw_up = sb("raw_up", [P, UC, 2 * FF])
        ident = sb("ident", [P, P])
        halves = sb("halves", [P, CAP])
        slots = sb("slots", [P, P])
        x_tok = sb("x_tok", [P, CT, D])
        rankm = sb("rankm", [P, CT, E])
        meta = sb("meta", [P, CT, E, 2])
        bias_up = sb("bias_up", [P, 2 * FF // P, E])
        counts = sb("counts", [P, E], I32)
        most = sb("most", [P, 1], I32)
        bank = top.enter_context(nc.psum_tensor("bank", [P, 8, 512], F32))

        landed = [sem(f"landed{s}") for s in range(CPR)]
        slots_in = sem("slots_in")
        acc_init = sem("acc_init")
        out_done = sem("out_done")

        with ExitStack() as ph:
            sb = make(ph)
            w_ring = sb("w_ring", [P, 2, KT, 512])
            h_tok = sb("h_tok", [P, CT, D])
            xnt = sb("xnt", [P, KT, T])
            mix_in = sb("mix_in", [P, KT, T])
            kr = sb("kr", [P, HEADS, T])
            qr = sb("qr", [P, HEADS, T])
            vt = sb("vt", [P, HEADS, T])
            sg = sb("sg", [P, HEADS, T])
            tmp = sb("tmp", [P, HEADS, T])
            state = sb("state", [P, NS * HEADS, HD])
            square = sb("square", [P, 7, P])
            rope = sb("rope", [P, 2, T])
            xi = sb("xi", [P, HEADS, CHUNK])
            zeta = sb("zeta", [P, HEADS])
            route = sb("route", [P, E + 2 * CT + NS])
            rows = sb("rows", [P, P])
            vec = sb("vec", [P, 88])
            u_pad = sb("u_pad", [P, HEADS, SEQ + 2])
            u_s = sb("u_s", [P, HEADS, NS])
            k_tok = sb("k_tok", [P, 2, HEADS, HD])
            v_tok = sb("v_tok", [P, 2, HEADS, HD])
            small = sb("small", [P, 16])
            ks_tok = h_tok[0:NS, 0, 0:HEADS * HD]
            vs_tok = h_tok[0:NS, 1, 0:HEADS * HD]
            scores = h_tok[:, 2, :].rearrange("p (c h n) -> p c h n", c=2, h=HEADS)
            q_xi = h_tok[:, 0, 512:1024].rearrange("p (h n) -> p h n", h=HEADS)
            state1 = h_tok[:, 1, 512:1024].rearrange("p (h n) -> p h n", h=HEADS)
            nc_t = sb("nc_t", [P, HEADS, 2 + NS])
            scratch = raw_up[:, UC - 1, :]
            vd = scratch[0:NS, 0:NS * HD].rearrange("p (b e) -> p b e", b=NS)
            nc_rows = scratch[0:2 + NS, 1024:1024 + CONV_W]
            w_rt = scratch[:, 1536:1536 + KT * E].rearrange("p (k e) -> p k e", k=KT)
            b_rt = scratch[:, 1792:1792 + E]
            UPPER, MEAN, ONES, DECAY = 0, 1, 2, 3
            decay = square[:, DECAY:DECAY + HEADS, :]

            x_in = sem("x_in")
            const_in = sem("const_in")
            rows_in = sem("rows_in")
            misc_in = sem("misc_in")
            state_in = sem("state_in")
            win = [sem(f"win{s}") for s in range(2)]
            v_chain = sem("v_chain")
            a_chain = sem("a_chain")
            g_chain = sem("g_chain")
            ssq_done = sem("ssq_done")
            root_done = sem("root_done")
            x_scaled = sem("x_scaled")
            rows_t = sem("rows_t")
            vec_ready = sem("vec_ready")
            xnt_psum = sem("xnt_psum")
            xnt_ready = sem("xnt_ready")
            proj_psum = sem("proj_psum")
            proj_out = sem("proj_out")
            k_rot = sem("k_rot")
            q_rot = sem("q_rot")
            kv_tok_psum = sem("kv_tok_psum")
            kv_tok = sem("kv_tok")
            s_tok_psum = sem("s_tok_psum")
            s_tok = sem("s_tok")
            sc_psum = sem("sc_psum")
            sc_ready = sem("sc_ready")
            kv_psum = sem("kv_psum")
            s1_ready = sem("s1_ready")
            s2_ready = sem("s2_ready")
            o_psum = sem("o_psum")
            o_ready = sem("o_ready")
            vd_ready = sem("vd_ready")
            kvs_psum = sem("kvs_psum")
            snew = sem("snew")
            mean_psum = sem("mean_psum")
            dev_ready = sem("dev_ready")
            var_psum = sem("var_psum")
            std_ready = sem("std_ready")
            mix_ready = sem("mix_ready")
            ncv_ready = sem("ncv_ready")
            ncv_psum = sem("ncv_psum")
            ncv_rows = sem("ncv_rows")
            wo_psum = sem("wo_psum")
            wo_out = sem("wo_out")
            ht_psum1 = sem("ht_psum1")
            h_ready = sem("h_ready")
            ssq2 = sem("ssq2")
            root2 = sem("root2")
            xn_ready = sem("xn_ready")
            xn2_psum = sem("xn2_psum")
            xn2_ready = sem("xn2_ready")
            lg_psum = sem("lg_psum")
            top_ready = sem("top_ready")
            exp_ready = sem("exp_ready")
            mask_ready = sem("mask_ready")
            rank_psum = sem("rank_psum")
            bu_in = sem("bu_in")
            bu_psum = sem("bu_psum")
            bu_ready = sem("bu_ready")
            gffn_in = sem("gffn_in")
            eps_ready = sem("eps_ready")
            x_zero = sem("x_zero")
            state1_out = sem("state1_out")
            state_out = sem("state_out")

            rt = kr[:, :, :].rearrange("p h n -> p (h n)")
            logit = rt[:, 0:CT * E].rearrange("p (c e) -> p c e", c=CT)
            top8 = rt[:, 96:96 + CT * 8].rearrange("p (c e) -> p c e", c=CT)
            ranks = rt[:, 120:120 + CT * E].rearrange("p (c e) -> p c e", c=CT)
            gate = rt[:, 216:216 + CT * TOP].rearrange("p (c k) -> p c k", c=CT)
            idxf = rt[:, 228:228 + CT * TOP].rearrange("p (c k) -> p c k", c=CT)
            dest = rt[:, 240:240 + CT * TOP].rearrange("p (c k) -> p c k", c=CT)
            gsum = rt[:, 252:252 + CT]
            mask = rt[:, 256:256 + CT * E].rearrange("p (c e) -> p c e", c=CT)
            gmat = rt[:, 352:352 + CT * E].rearrange("p (c e) -> p c e", c=CT)
            ONEH = CT * TOP * E
            onehot = qr[:, :, :].rearrange("p h n -> p (h n)")[:, 0:ONEH].rearrange("p (c k e) -> p c k e", c=CT, k=TOP)
            prod = vt[:, :, :].rearrange("p h n -> p (h n)")[:, 0:ONEH].rearrange("p (c k e) -> p c k e", c=CT, k=TOP)
            idx8 = sb("idx8", [P, CT, 8], U32)
            g_ffn = w_ring[:, 1, 4:6, :].rearrange("p a b -> p (a b)")
            b_up_sb = w_ring[0:E, 1, 0:4, :].rearrange("p a b -> p (a b)")
            xn2 = x_tok
            junk = mix_in[:, 0:4, 0:256].rearrange("p a b -> p a b")

            block = ph.enter_context(nc.Block())

            w_in_v = w_in[0].rearrange("(k p) n -> p k n", p=P)
            w_out_v = w_out[0].rearrange("(k p) n -> p k n", p=P)

            def chunk_src(j):
                if j < len(ORDER):
                    return w_in_v[:, :, ORDER[j] * 512:(ORDER[j] + 1) * 512]
                j -= len(ORDER)
                return w_out_v[:, :, j * 512:(j + 1) * 512]

            @block.sync
            def _(sp):
                sp.dma_start(x_tok[:, 0:2, :], x_prompt[0].rearrange("(c p) d -> p c d", p=P)).then_inc(x_in, 16)
                sp.wait_ge(x_zero, 1)
                sp.dma_start(x_tok[0:NS, 2, :], x_sample.rearrange("b s d -> (b s) d")).then_inc(x_in, 16)
                sp.dma_start(rows[0:8, :], norm_mix.rearrange("a (k p) -> (a k) p", p=P)).then_inc(rows_in, 16)
                sp.dma_start(rows[8:12, :], ret_norm.rearrange("a (k p) -> (a k) p", p=P)).then_inc(rows_in, 16)
                sp.dma_start(rows[12:24, :], conv_w[0].rearrange("j (m p) -> (j m) p", p=P)).then_inc(rows_in, 16)
                sp.dma_start(rows[24:88, :], state_conv[0].rearrange("b j (m p) -> (b j m) p", p=P)).then_inc(rows_in, 16)
                sp.dma_start(ident[:], c_square[:, 0, :]).then_inc(const_in, 16)
                sp.dma_start(halves[:], c_square[:, 1, 0:CAP]).then_inc(const_in, 16)
                sp.dma_start(square[:], c_square[:, 2:9, :]).then_inc(const_in, 16)
                sp.dma_start(rope[:], c_rope).then_inc(const_in, 16)
                sp.dma_start(xi[:], c_xi[:, 0:HEADS, :]).then_inc(const_in, 16)
                sp.dma_start(zeta[:], c_xi[:, HEADS, 0:HEADS]).then_inc(const_in, 16)
                sp.dma_start(route[:], c_route).then_inc(const_in, 16)
                for j in range(2):
                    sp.dma_start(w_ring[:, j], chunk_src(j)).then_inc(win[j], 16)
                sp.dma_start(slots[:], c_slots).then_inc(slots_in, 16)
                sp.dma_start(state[:], state_ret[0].rearrange("b h d e -> d (b h) e")).then_inc(state_in, 16)
                sp.dma_start(w_rt, w_router[0].rearrange("(k p) e -> p k e", p=P)).then_inc(misc_in, 16)
                sp.dma_start(b_rt, b_router.partition_broadcast(P)[:, 0, :]).then_inc(misc_in, 16)
                sp.dma_start(conv_sample[0, :, 0, :], state_conv[0, :, 1, :]).then_inc(out_done, 16)
                for k in range(UC - 1):
                    sp.dma_start(raw_up[:, k, :], w_up_v[0, k]).then_inc(landed[k], 16)
                for j in range(2, 9):
                    if j - 2 < 7:
                        sp.wait_ge(proj_psum, 4 * (j - 1))
                    sp.dma_start(w_ring[:, j % 2], chunk_src(j)).then_inc(win[j % 2], 16)
                sp.wait_ge(s2_ready, 1)
                sp.dma_start(ret_prompt[0, 0].rearrange("h d e -> d h e"), state1).then_inc(state1_out, 16)
                sp.wait_ge(snew, 8)
                sp.dma_start(ret_sample[0].rearrange("b h d e -> d (b h) e"), state[:]).then_inc(state_out, 16)
                sp.wait_ge(ncv_rows, 1)
                sp.dma_start(conv_prompt[0, 0], nc_rows[0:2, :]).then_inc(out_done, 16)
                sp.dma_start(conv_sample[0, :, 1, :], nc_rows[2:2 + NS, :]).then_inc(out_done, 16)
                sp.wait_ge(wo_psum, 4)
                sp.dma_start(b_up_sb, b_up[0]).then_inc(bu_in, 16)
                sp.dma_start(g_ffn, norm_ffn.partition_broadcast(P)[:, 0, :]).then_inc(gffn_in, 16)
                for c, (t0, n) in enumerate(TOK):
                    sp.wait_ge(h_ready, c + 1)
                    sp.dma_start(acc_dram[t0:t0 + n, :], h_tok[0:n, c, :]).then_inc(acc_init, 16)
                sp.wait_ge(acc_init, 16 * CT)
                sp.wait_ge(state1_out, 16)
                sp.wait_ge(state_out, 16)

            @block.gpsimd
            def _(pool):
                pool.memset(x_tok[:, 2, :], 0.0).then_inc(x_zero, 1)

            @block.tensor
            def _(pe):
                def turn(out, in_, n, last=None):
                    return pe.transpose(out, in_, ident[0:n, 0:n])

                pe.wait_ge(const_in, 16 * 7)
                pe.wait_ge(rows_in, 64)
                turn(bank[:, 7, 0:88], rows[0:88, :], 88).then_inc(rows_t, 1)
                for k in range(KT):
                    for c, (t0, n) in enumerate(TOK):
                        if k == 0:
                            pe.wait_ge(x_scaled, c + 1)
                        if k == 7 and c == 0:
                            pe.wait_ge(vec_ready, 1)
                        mm = turn(bank[:, k, t0:t0 + n], h_tok[0:n, c, k * P:(k + 1) * P], n)
                    mm.then_inc(xnt_psum, 1)

                def project(j):
                    pe.wait_ge(win[j % 2], 16 * (j // 2 + 1))
                    for m in range(4):
                        i = 4 * j + m
                        if i >= 4:
                            pe.wait_ge(proj_out, i - 3)
                        for k in range(KT):
                            mm = pe.matmul(bank[:, i % 4, 0:T], w_ring[:, j % 2, k, m * P:(m + 1) * P],
                                           xnt[:, k, :], start=(k == 0), stop=(k == KT - 1))
                        mm.then_inc(proj_psum, 1)
                        yield

                def run(j):
                    for _ in project(j):
                        pass

                pe.wait_ge(xnt_ready, KT)
                run(0)
                run(1)
                run(2)
                run(3)
                pe.wait_ge(k_rot, 1)
                pe.wait_ge(proj_out, 12)
                for b, (src, c) in enumerate(((kr, 0), (kr, 1), (vt, 0), (vt, 1))):
                    for h in range(HEADS):
                        mm = turn(bank[:, 4 + b, h * HD:(h + 1) * HD], src[:, h, c * P:(c + 1) * P], P)
                    mm.then_inc(kv_tok_psum, 1)
                run(4)
                pe.wait_ge(kv_tok, 4)
                for b, src in enumerate((kr, vt)):
                    for h in range(HEADS):
                        mm = turn(bank[0:NS, 4 + b, h * HD:(h + 1) * HD], src[:, h, SEQ:T], P)
                    mm.then_inc(s_tok_psum, 1)
                pe.wait_ge(q_rot, 1)
                for c in range(2):
                    for h in range(HEADS):
                        at = slice(c * CHUNK, (c + 1) * CHUNK)
                        mm = pe.matmul(bank[:, 6 + c, h * P:(h + 1) * P], kr[:, h, at], qr[:, h, at],
                                       start=True, stop=True)
                    mm.then_inc(sc_psum, 1)
                run(5)
                pe.wait_ge(sc_ready, 2)
                pe.wait_ge(s_tok, 2)
                for c in range(2):
                    for h in range(HEADS):
                        mm = pe.matmul(bank[:, 6 + c, h * P:(h + 1) * P], k_tok[:, c, h, :], v_tok[:, c, h, :],
                                       start=True, stop=True)
                    mm.then_inc(kv_psum, 1)
                for c in range(2):
                    if c == 1:
                        pe.wait_ge(s1_ready, 1)
                    for h in range(HEADS):
                        mm = pe.matmul(bank[:, 4 + c, h * P:(h + 1) * P], v_tok[:, c, h, :], scores[:, c, h, :],
                                       start=True, stop=(c == 0))
                        if c == 1:
                            mm = pe.matmul(bank[:, 4 + c, h * P:(h + 1) * P], state1[:, h, :], q_xi[:, h, :],
                                           start=False, stop=True)
                    mm.then_inc(o_psum, 1)
                pe.wait_ge(s2_ready, 1)
                for h, _ in enumerate(project(6)):
                    pe.wait_ge(vd_ready, h + 1)
                    for half in range(2):
                        if h > 0:
                            pe.wait_ge(snew, 2 * h - 1 + half)
                        pe.matmul(bank[:, 6 + half, :], ks_tok[:, h * HD:(h + 1) * HD],
                                  vd[:, half * 4:half * 4 + 4, :], start=True, stop=True).then_inc(kvs_psum, 1)
                pe.wait_ge(ncv_ready, 1)
                pe.wait_ge(o_ready, 2)
                for m in range(4):
                    mm = turn(bank[0:2 + NS, 4, m * P:(m + 1) * P], nc_t[:, m, :], P)
                mm.then_inc(ncv_psum, 1)
                pe.wait_ge(snew, 8)
                for h in range(HEADS):
                    for b in range(NS):
                        mm = pe.matmul(bank[:, 5, h * NS + b:h * NS + b + 1], state[:, b * HEADS + h, :],
                                       qr[:, h, SEQ + b:SEQ + b + 1], start=True, stop=True)
                mm.then_inc(o_psum, 1)
                pe.wait_ge(o_ready, 3)
                pe.wait_ge(ncv_rows, 1)
                for h in range(HEADS):
                    pe.matmul(bank[:, 4 + h, 0:T], square[:, MEAN, :], tmp[:, h, :],
                              start=True, stop=True).then_inc(mean_psum, 1)
                for h in range(HEADS):
                    pe.wait_ge(dev_ready, h + 1)
                    pe.matmul(bank[:, 4 + h, 0:T], square[:, MEAN, :], vt[:, h, :],
                              start=True, stop=True).then_inc(var_psum, 1)
                pe.wait_ge(proj_out, 28)
                for m in range(KT):
                    j = 7 + m // 4
                    if m % 4 == 0:
                        pe.wait_ge(win[j % 2], 16 * (j // 2 + 1))
                    if m == 4:
                        pe.wait_ge(std_ready, 4)
                    for k in range(KT):
                        if m == 0 and k == 0:
                            pe.wait_ge(mix_ready, 1)
                        if m == 0 and k == 4:
                            pe.wait_ge(mix_ready, 2)
                        mm = pe.matmul(bank[:, m, 0:T], w_ring[:, j % 2, k, (m % 4) * P:(m % 4 + 1) * P],
                                       mix_in[:, k, :], start=(k == 0), stop=(k == KT - 1))
                    mm.then_inc(wo_psum, 1)
                pe.wait_ge(wo_out, 8)
                for c, (t0, n) in enumerate(TOK):
                    for m in range(KT):
                        mm = turn(bank[0:n, 2 * c + m // 4, (m % 4) * P:(m % 4 + 1) * P], xnt[:, m, t0:t0 + n], P)
                    mm.then_inc(ht_psum1, 1)
                pe.wait_ge(bu_in, 16)
                for j in range(2 * FF // P):
                    mm = turn(bank[:, 6, j * E:(j + 1) * E], b_up_sb[:, j * P:(j + 1) * P], E)
                mm.then_inc(bu_psum, 1)
                pe.wait_ge(h_ready, 3)
                pe.wait_ge(bu_ready, 1)
                for k in range(KT):
                    for c, (t0, n) in enumerate(TOK):
                        if k == 0:
                            pe.wait_ge(xn_ready, c + 1)
                        mm = turn(bank[:, k, t0:t0 + n], xn2[0:n, c, k * P:(k + 1) * P], n)
                    mm.then_inc(xn2_psum, 1)
                pe.wait_ge(xn2_ready, KT)
                for c, (t0, n) in enumerate(TOK):
                    for k in range(KT):
                        mm = pe.matmul(bank[0:n, c, 0:E], xnt[:, k, t0:t0 + n], w_rt[:, k, :],
                                       start=(k == 0), stop=(k == KT - 1))
                    mm.then_inc(lg_psum, 1)
                pe.wait_ge(mask_ready, 1)
                for c in range(CT):
                    for b in range(c):
                        pe.matmul(bank[:, 3, c * E:(c + 1) * E], square[:, ONES, :], mask[:, b, :],
                                  start=(b == 0), stop=False)
                    pe.matmul(bank[:, 3, c * E:(c + 1) * E], square[:, UPPER, :], mask[:, c, :],
                              start=(c == 0), stop=True).then_inc(rank_psum, 1)
                for c in range(CT):
                    mm = pe.matmul(bank[:, 4, 0:E], square[:, ONES, :], mask[:, c, :],
                                   start=(c == 0), stop=(c == CT - 1))
                mm.then_inc(rank_psum, 1)

            @block.scalar
            def _(act):
                chain = [0]

                def link(ins):
                    chain[0] += 1
                    ins.then_inc(a_chain, 1)
                    act.wait_ge(a_chain, chain[0])

                act.wait_ge(x_in, 32)
                for c, (t0, n) in enumerate(TOK):
                    if c:
                        act.wait_ge(ssq_done, c)
                    nc.scalar.activation(junk[0:n], x_tok[0:n, c, :].rearrange("p (a b) -> p a b", a=4), ACT.Square,
                                         accum_out=small[0:n, c:c + 1]).then_inc(ssq_done, 1)
                act.wait_ge(ssq_done, 3)
                act.wait_ge(eps_ready, 2)

                for c, (t0, n) in enumerate(TOK):
                    nc.scalar.activation(small[0:n, 3 + c:4 + c], small[0:n, c:c + 1], ACT.Sqrt,
                                         bias=small[0:n, 15:16], scale=1.0 / D).then_inc(root_done, 1)
                act.wait_ge(rows_t, 1)
                nc.scalar.activation(vec[:], bank[:, 7, 0:88], ACT.Copy).then_inc(vec_ready, 1)
                act.wait_ge(vec_ready, 1)
                for k in range(KT):
                    act.wait_ge(xnt_psum, k + 1)
                    nc.scalar.activation(xnt[:, k, :], bank[:, k, 0:T], ACT.Copy,
                                         scale=vec[:, k:k + 1]).then_inc(xnt_ready, 1)

                def out(j, dst, fn=ACT.Copy):
                    for m in range(4):
                        act.wait_ge(proj_psum, 4 * j + m + 1)
                        nc.scalar.activation(dst[:, m, :], bank[:, m, 0:T], fn).then_inc(proj_out, 1)

                out(0, kr)
                out(1, qr)
                out(2, vt)
                out(3, sg, ACT.Silu)
                for b, dst in ((0, k_tok), (1, k_tok), (2, v_tok), (3, v_tok)):
                    act.wait_ge(kv_tok_psum, b + 1)
                    for h in range(HEADS):
                        ins = nc.scalar.activation(dst[:, b % 2, h, :], bank[:, 4 + b, h * HD:(h + 1) * HD], ACT.Copy,
                                                   scale=zeta[:, h:h + 1] if b < 2 else 1.0)
                    ins.then_inc(kv_tok, 1)
                out(4, mix_in[:, 0:4])
                act.wait_ge(s_tok_psum, 1)
                nc.scalar.activation(ks_tok, bank[0:NS, 4, :], ACT.Copy).then_inc(s_tok, 1)
                act.wait_ge(s_tok_psum, 2)
                nc.scalar.activation(vs_tok, bank[0:NS, 5, :], ACT.Copy).then_inc(s_tok, 1)
                out(5, mix_in[:, 4:8])
                act.wait_ge(q_rot, 2)
                for c in range(2):
                    act.wait_ge(o_psum, c + 1)
                    nc.scalar.activation(tmp[:, :, c * P:(c + 1) * P],
                                         bank[:, 4 + c, :].rearrange("p (h n) -> p h n", h=HEADS),
                                         ACT.Copy).then_inc(o_ready, 1)
                act.wait_ge(ncv_ready, 1)
                out(6, mix_in[:, 4:8])
                act.wait_ge(ncv_psum, 1)
                nc.scalar.activation(nc_rows, bank[0:2 + NS, 4, :], ACT.Copy).then_inc(ncv_rows, 1)
                act.wait_ge(o_psum, 3)
                nc.scalar.activation(tmp[:, :, SEQ:T], bank[:, 5, 0:HEADS * NS].rearrange("p (h n) -> p h n", h=HEADS),
                                     ACT.Copy).then_inc(o_ready, 1)
                for h in range(HEADS):
                    act.wait_ge(var_psum, h + 1)
                    nc.scalar.activation(vt[:, h, :], bank[:, 4 + h, 0:T], ACT.Sqrt,
                                         bias=small[:, 14:15]).then_inc(std_ready, 1)
                for m in range(KT):
                    act.wait_ge(wo_psum, m + 1)
                    nc.scalar.activation(xnt[:, m, :], bank[:, m, 0:T], ACT.Copy).then_inc(wo_out, 1)
                for c, (t0, n) in enumerate(TOK):
                    act.wait_ge(h_ready, c + 1)
                    if c == 0:
                        act.wait_ge(wo_psum, 8)
                    else:
                        act.wait_ge(ssq2, c)
                    nc.scalar.activation(junk[0:n], h_tok[0:n, c, :].rearrange("p (a b) -> p a b", a=4), ACT.Square,
                                         accum_out=small[0:n, 6 + c:7 + c]).then_inc(ssq2, 1)
                act.wait_ge(ssq2, 3)
                for c, (t0, n) in enumerate(TOK):
                    nc.scalar.activation(small[0:n, 9 + c:10 + c], small[0:n, 6 + c:7 + c], ACT.Sqrt,
                                         bias=small[0:n, 15:16], scale=1.0 / D).then_inc(root2, 1)
                act.wait_ge(bu_psum, 1)
                nc.scalar.activation(bias_up[:], bank[:, 6, :].rearrange("p (j e) -> p j e", e=E),
                                     ACT.Copy).then_inc(bu_ready, 1)
                for k in range(KT):
                    act.wait_ge(xn2_psum, k + 1)
                    nc.scalar.activation(xnt[:, k, :], bank[:, k, 0:T], ACT.Copy).then_inc(xn2_ready, 1)
                act.wait_ge(top_ready, 1)
                nc.scalar.activation(gate, gate, ACT.Exp).then_inc(exp_ready, 1)

            @block.vector
            def _(dve):
                chain = [0]

                def link(ins):
                    chain[0] += 1
                    ins.then_inc(v_chain, 1)
                    dve.wait_ge(v_chain, chain[0])

                tt, ts, stt = nc.vector.tensor_tensor, nc.vector.tensor_scalar, nc.vector.scalar_tensor_tensor

                nc.vector.memset(small[:, 14:15], GN_EPS).then_inc(eps_ready, 1)
                nc.vector.memset(small[:, 15:16], RMS_EPS).then_inc(eps_ready, 1)
                dve.wait_ge(root_done, 3)
                for c, (t0, n) in enumerate(TOK):
                    link(nc.vector.reciprocal(small[0:n, 3 + c:4 + c], small[0:n, 3 + c:4 + c]))
                    ts(h_tok[0:n, c, :], x_tok[0:n, c, :], small[0:n, 3 + c:4 + c], None, ALU.mult).then_inc(x_scaled, 1)

                def rotate(t, scaled, done):
                    cos = rope[:, 0:1, :].broadcast_to([P, HEADS, T])
                    sin = rope[:, 1:2, :].broadcast_to([P, HEADS, T])
                    tt(tmp[0:64], t[64:128], sin[64:128], ALU.mult).then_inc(v_chain, 1)
                    link(tt(tmp[64:128], t[0:64], sin[0:64], ALU.mult))
                    link(tt(t[:, :, :], t[:, :, :], cos, ALU.mult))
                    if scaled:
                        link(tt(t[:, :, :], t[:, :, :], tmp[:, :, :], ALU.add))
                        ts(t[:, :, :], t[:, :, :], HD ** -0.5, None, ALU.mult).then_inc(done, 1)
                        dve.wait_ge(done, 1)
                    else:
                        tt(t[:, :, :], t[:, :, :], tmp[:, :, :], ALU.add).then_inc(done, 1)
                        dve.wait_ge(done, 1)

                dve.wait_ge(const_in, 16 * 7)
                dve.wait_ge(proj_out, 4)
                chain[0] += 1
                rotate(kr, True, k_rot)
                dve.wait_ge(proj_out, 8)
                chain[0] += 1
                rotate(qr, False, q_rot)
                dve.wait_ge(xnt_psum, KT)
                tt(q_xi, qr[:, :, CHUNK:2 * CHUNK], xi[:], ALU.mult).then_inc(q_rot, 1)
                for c in range(2):
                    dve.wait_ge(sc_psum, c + 1)
                    tt(scores[:, c], bank[:, 6 + c, :].rearrange("p (h n) -> p h n", h=HEADS), decay,
                       ALU.mult).then_inc(sc_ready, 1)
                link(nc.vector.memset(u_pad[:, :, 0:2], 0.0))
                dve.wait_ge(proj_out, 24)
                dve.wait_ge(vec_ready, 1)
                link(tt(u_pad[:, :, 2:SEQ + 2], mix_in[:, 0:4, 0:SEQ], mix_in[:, 4:8, 0:SEQ], ALU.mult))
                link(tt(u_s[:], mix_in[:, 0:4, SEQ:T], mix_in[:, 4:8, SEQ:T], ALU.mult))
                link(nc.vector.tensor_copy(nc_t[:, :, 0:2], u_pad[:, :, SEQ:SEQ + 2]))
                nc.vector.tensor_copy(nc_t[:, :, 2:2 + NS], u_s[:]).then_inc(ncv_ready, 1)
                dve.wait_ge(kv_psum, 1)
                nc.vector.tensor_copy(state1, bank[:, 6, :].rearrange("p (h n) -> p h n", h=HEADS)).then_inc(s1_ready, 1)
                dve.wait_ge(o_psum, 2)
                dve.wait_ge(s1_ready, 1)
                for h in range(HEADS):
                    ins = stt(out=state1[:, h, :], in0=state1[:, h, :], scalar=float(gammas[h][1]),
                              in1=bank[:, 7, h * P:(h + 1) * P], op0=ALU.mult, op1=ALU.add)
                ins.then_inc(s2_ready, 1)
                dve.wait_ge(state_in, 16)
                dve.wait_ge(s_tok, 2)
                eye8 = route[0:NS, E + CT:E + CT + NS]
                for h in range(HEADS):
                    if h:
                        dve.wait_ge(kvs_psum, 2 * h)
                    for b in range(NS):
                        ins = ts(vd[:, b, :], vs_tok[:, h * HD:(h + 1) * HD], eye8[:, b:b + 1], None, ALU.mult)
                    ins.then_inc(vd_ready, 1)
                    for half in range(2):
                        dve.wait_ge(kvs_psum, 2 * h + half + 1)
                        at = state[:, half * 16:half * 16 + 16, :].rearrange("p (b h) e -> p b h e", h=HEADS)[:, :, h, :]
                        stt(out=at, in0=at, scalar=float(gammas[h][0]),
                            in1=bank[:, 6 + half, :].rearrange("p (b e) -> p b e", b=4),
                            op0=ALU.mult, op1=ALU.add).then_inc(snew, 1)
                cw = lambda j, m: vec[:, 12 + j * 4 + m:13 + j * 4 + m]
                past = vec[:, 24:88].rearrange("p (b j m) -> p j m b", b=NS, j=2)
                dve.wait_ge(proj_out, 28)
                for m in range(4):
                    ts(mix_in[:, m, 0:SEQ], u_pad[:, m, 0:SEQ], cw(0, m), None, ALU.mult).then_inc(v_chain, 1)
                    ts(mix_in[:, m, SEQ:T], past[:, 0, m, :], cw(0, m), None, ALU.mult).then_inc(v_chain, 1)
                chain[0] += 8
                dve.wait_ge(v_chain, chain[0])
                for j in range(1, 3):
                    for m in range(4):
                        stt(out=mix_in[:, m, 0:SEQ], in0=u_pad[:, m, j:j + SEQ], scalar=cw(j, m),
                            in1=mix_in[:, m, 0:SEQ], op0=ALU.mult, op1=ALU.add).then_inc(v_chain, 1)
                        src = past[:, 1, m, :] if j == 1 else u_s[:, m, :]
                        stt(out=mix_in[:, m, SEQ:T], in0=src, scalar=cw(j, m), in1=mix_in[:, m, SEQ:T],
                            op0=ALU.mult, op1=ALU.add).then_inc(v_chain, 1)
                    chain[0] += 8
                    dve.wait_ge(v_chain, chain[0])
                tt(mix_in[:, 0:4, :], mix_in[:, 0:4, :], mix_in[:, 4:8, :], ALU.mult).then_inc(mix_ready, 1)
                dve.wait_ge(mix_ready, 1)
                for h in range(HEADS):
                    dve.wait_ge(mean_psum, h + 1)
                    link(tt(tmp[:, h, :], tmp[:, h, :], bank[:, 4 + h, 0:T], ALU.subtract))
                    tt(vt[:, h, :], tmp[:, h, :], tmp[:, h, :], ALU.mult).then_inc(dev_ready, 1)
                for h in range(HEADS):
                    ts(sg[:, h, :], sg[:, h, :], vec[:, 8 + h:9 + h], None, ALU.mult).then_inc(v_chain, 1)
                chain[0] += HEADS
                dve.wait_ge(v_chain, chain[0])
                link(tt(tmp[:, :, :], tmp[:, :, :], sg[:, :, :], ALU.mult))
                dve.wait_ge(std_ready, HEADS)
                link(nc.vector.reciprocal(vt[:, :, :], vt[:, :, :]))
                tt(mix_in[:, 4:8, :], tmp[:, :, :], vt[:, :, :], ALU.mult).then_inc(mix_ready, 1)
                dve.wait_ge(state1_out, 16)
                for c, (t0, n) in enumerate(TOK):
                    dve.wait_ge(ht_psum1, c + 1)
                    tt(h_tok[0:n, c, :].rearrange("p (a b) -> p a b", a=2),
                       x_tok[0:n, c, :].rearrange("p (a b) -> p a b", a=2), bank[0:n, 2 * c:2 * c + 2, :],
                       ALU.add).then_inc(h_ready, 1)
                dve.wait_ge(root2, 3)
                dve.wait_ge(misc_in, 32)
                dve.wait_ge(h_ready, 3)
                dve.wait_ge(gffn_in, 16)
                for c, (t0, n) in enumerate(TOK):
                    link(nc.vector.reciprocal(small[0:n, 9 + c:10 + c], small[0:n, 9 + c:10 + c]))
                    stt(out=xn2[0:n, c, :], in0=h_tok[0:n, c, :], scalar=small[0:n, 9 + c:10 + c], in1=g_ffn[0:n, :],
                        op0=ALU.mult, op1=ALU.mult).then_inc(xn_ready, 1)
                link(nc.vector.memset(rt[:, :], 0.0))
                for c, (t0, n) in enumerate(TOK):
                    dve.wait_ge(lg_psum, c + 1)
                    link(tt(logit[0:n, c, :], bank[0:n, c, 0:E], b_rt[0:n, :], ALU.add))
                for c in range(CT):
                    link(nc.vector.max(top8[:, c, :], logit[:, c, :]))
                    nc.vector.max_index(idx8[:, c, :], top8[:, c, :], logit[:, c, :]).then_inc(v_chain, 1)
                    chain[0] += 1
                top = top8[:, :, 0:TOP]
                tt(gate, top, top8[:, :, 0:1].broadcast_to([P, CT, TOP]), ALU.subtract).then_inc(top_ready, 1)
                dve.wait_ge(v_chain, chain[0])
                link(nc.vector.tensor_copy(idxf, idx8[:, :, 0:TOP]))
                iota = route[:, 0:E]
                for k in range(TOP):
                    tt(onehot[:, :, k, :], iota.rearrange("p (a e) -> p a e", a=1).broadcast_to([P, CT, E]),
                       idxf[:, :, k:k + 1].broadcast_to([P, CT, E]), ALU.is_equal).then_inc(v_chain, 1)
                chain[0] += TOP
                dve.wait_ge(v_chain, chain[0])
                link(nc.vector.tensor_reduce(mask, onehot.rearrange("p c k e -> p c e k"), AX.X, ALU.add))
                tt(mask, mask, route[:, E + CT + NS:].rearrange("p (c a) -> p c a", a=1).broadcast_to([P, CT, E]),
                   ALU.mult).then_inc(mask_ready, 1)
                dve.wait_ge(exp_ready, 1)
                link(nc.vector.tensor_reduce(gsum, gate, AX.X, ALU.add))
                link(nc.vector.reciprocal(gsum, gsum))
                link(tt(gate, gate, gsum.rearrange("p (c a) -> p c a", a=1).broadcast_to([P, CT, TOP]), ALU.mult))
                dve.wait_ge(rank_psum, CT + 1)
                dve.wait_ge(mask_ready, 1)
                link(stt(out=rankm[:], in0=bank[:, 3, 0:CT * E].rearrange("p (c e) -> p c e", c=CT), scalar=1.0,
                         in1=mask, op0=ALU.add, op1=ALU.mult))
                link(ts(rankm[:], rankm[:], -1.0, None, ALU.add))
                link(nc.vector.tensor_copy(counts[:], bank[:, 4, 0:E]))
                link(nc.vector.tensor_reduce(most[:], counts[:], AX.X, ALU.max))
                for k in range(TOP):
                    tt(prod[:, :, k, :], onehot[:, :, k, :], gate[:, :, k:k + 1].broadcast_to([P, CT, E]),
                       ALU.mult).then_inc(v_chain, 1)
                chain[0] += TOP
                dve.wait_ge(v_chain, chain[0])
                link(nc.vector.tensor_reduce(meta[:, :, :, 1], prod.rearrange("p c k e -> p c e k"), AX.X, ALU.add))
                link(nc.vector.tensor_copy(meta[:, :, :, 0], route[:, E:E + CT].rearrange("p (c a) -> p c a", a=1)
                                           .broadcast_to([P, CT, E])))

        with ExitStack() as ph:
            sb = make(ph)
            raw_down = sb("raw_down", [P, DC, 2 * D])
            w_high = sb("w_high", [P, SPLIT, 2 * FF], F32R)
            w_low = sb("w_low", [P, SPLIT, 2 * FF], F32R)
            xs = sb("xs", [P, KT, 2 * CAP], F32R)
            h_rows = sb("h_rows", [P, 2 * FF])
            hb = sb("hb", [P, 2 * FF // P, CAP])
            sig = sb("sig", [P, KT, CAP])
            av = sb("av", [P, KT, 2 * CAP], F32R)
            yg = sb("yg", [CAP, D])
            pick = sb("pick", [P, CT, P])
            rank_now = sb("rank_now", [P, CT])
            slot_info = sb("slot_info", [P, E, 2])
            slot_row = sb("slot_row", [P, 1], I32)
            slot_gate = sb("slot_gate", [P, 1])
            nobody = sb("nobody", [P, 2])
            gt = sb("gt", [E, T])
            st = sb("st", [P, 16])
            yl = h_rows[0:CAP, 0:D]
            fin = raw_up[:, 0:2, :].rearrange("p a b -> p (a b)")[:, 0:CT * D].rearrange("p (c d) -> p c d", c=CT)
            g_fin = x_tok[:, 1, :]
            b_down_sb = x_tok[0:E, 0, :]

            high_done = sem("high_done")
            low_done = sem("low_done")
            mm_done = sem("mm_done")
            pick_ready = sem("pick_ready")
            rank_taken = sem("rank_taken")
            xt_psum = sem("xt_psum")
            xs_high = sem("xs_high")
            xs_ready = sem("xs_ready")
            info_ready = sem("info_ready")
            slot_ready = sem("slot_ready")
            h_copied = sem("h_copied")
            ht_psum = sem("ht_psum")
            biased = sem("biased")
            clamped = sem("clamped")
            lin_ready = sem("lin_ready")
            sig_ready = sem("sig_ready")
            act_ready = sem("act_ready")
            act_high = sem("act_high")
            av_ready = sem("av_ready")
            yl_ready = sem("yl_ready")
            y_ready = sem("y_ready")
            scattered = sem("scattered")
            nobody_set = sem("nobody_set")
            eps_set = sem("eps_set")
            all_added = sem("all_added")
            pool_passed = sem("pool_passed")
            pe_passed = sem("pe_passed")
            sp_passed = sem("sp_passed")
            ranks_moved = sem("ranks_moved")
            gt_psum = sem("gt_psum")
            gt_ready = sem("gt_ready")
            gb_psum = sem("gb_psum")
            bd_in = sem("bd_in")
            gf_in = sem("gf_in")
            fin_in = [sem(f"fin_in{c}") for c in range(CT)]
            fin_added = sem("fin_added")
            fin_chain = sem("fin_chain")
            fin_ssq = sem("fin_ssq")
            fin_root = sem("fin_root")
            fin_ready = sem("fin_ready")
            stored = sem("stored")

            block = ph.enter_context(nc.Block())
            H, HT, Y = 0, 4, 6
            X, INFO = HT, HT + 1
            LAST = E * CPR

            def place(n, j):
                if isinstance(n, int) and n == 0:
                    return j
                return CPR * n - DC + (j - UC if isinstance(n, int) and n == E else j)

            def ups_done(n):
                return UC if isinstance(n, int) and n == 0 else CPR * n - DC + UC

            def downs_done(n):
                return LAST if isinstance(n, int) and n == E - 1 else CPR * n + 2 * CPR - DC

            def each_overflow(eng, body, at_round=None):
                k = eng.alloc_register(f"rounds_{eng.engine.name}")
                eng.reg_mov(k, 0)
                greatest = eng.value_load(most[0:1, 0:1], min_val=0, max_val=T)
                with eng.If(greatest > CAP):
                    with eng.Fori(1, OVER) as r:
                        if at_round is not None:
                            at_round(r)
                        with eng.Fori(0, E) as e:
                            count = eng.value_load(counts[0:1, bass.ds(e, 1)], min_val=0, max_val=T)
                            with eng.If(count > r * CAP):
                                body(e, eng.snap(k, min_val=0, max_val=E * OVER))
                                eng.reg_add(k, k, 1)
                return eng.snap(k, min_val=0, max_val=E * OVER)

            @block.sync
            def _(sp):
                def load(e, j):
                    if j < UC:
                        sp.dma_start(raw_up[:, j, :], w_up_v[e, j]).then_inc(landed[j], 16)
                    else:
                        sp.dma_start(raw_down[:, j - UC, :].rearrange("p (k n) -> p k n", k=2),
                                     w_down_v[e, j - UC]).then_inc(landed[j], 16)

                load(0, UC - 1)
                for j in range(CPR):
                    if j < UC:
                        sp.wait_ge(low_done, j + 1)
                    load(1 if j < UC else 0, j)
                with sp.Fori(2, E) as n:
                    for j in range(CPR):
                        sp.wait_ge(low_done, place(n, j) - CPR + 1)
                        load(n if j < UC else n - 1, j)
                for j in range(UC, CPR):
                    sp.wait_ge(low_done, place(E - 1, j) + 1)
                    load(E - 1, j)
                def overflow(e, k):
                    sp.wait_ge(mm_done, k * CPR + LAST)
                    for j in range(CPR):
                        load(e, j)

                k = each_overflow(sp, overflow)
                sp.wait_ge(xt_psum, k + E)
                sp.sem_inc(sp_passed, 1)
                sp.dma_start(b_down_sb, b_down[0]).then_inc(bd_in, 16)
                sp.dma_start(g_fin, norm_final.rearrange("(a d) -> a d", a=1).partition_broadcast(P)[:, 0, :]).then_inc(gf_in, 16)
                sp.wait_ge(all_added, 1)
                for c, (t0, n) in enumerate(TOK):
                    sp.dma_start(fin[0:n, c, :], acc_dram[t0:t0 + n, :]).then_inc(fin_in[c], 16)
                for c in range(2):
                    sp.wait_ge(fin_ready, c + 1)
                    sp.dma_start(y_prompt[0, c * P:(c + 1) * P, :], fin[:, c, :]).then_inc(stored, 16)
                sp.wait_ge(fin_ready, 3)
                sp.dma_start(y_sample.rearrange("b s d -> (b s) d"), fin[0:NS, 2, :]).then_inc(stored, 16)
                sp.wait_ge(stored, 48)
                sp.wait_ge(out_done, 16 * 3)

            @block.gpsimd
            def _(pool):
                def carry():
                    pool.sem_inc(pool_passed, 1)

                def choose(n, e):
                    if not (isinstance(n, int) and n == 0):
                        pool.wait_ge(xt_psum, n)
                        pool.wait_ge(pick_ready, n)
                        carry()
                    pool.tensor_copy(rank_now[:], rankm[:, :, e].rearrange("p c a -> p (c a)")).then_inc(rank_taken, 1)
                    pool.wait_ge(rank_taken, n + 1)
                    carry()
                    for c in range(CT):
                        ins = pool.tensor_scalar(pick[:, c, :], slots[:], rank_now[:, c:c + 1], None, ALU.is_equal)
                    ins.then_inc(pick_ready, 1)

                def add_y(n, e):
                    if not (isinstance(n, int) and n == 0):
                        pool.wait_ge(scattered, 16 * n)
                    pool.wait_ge(info_ready, n + 1)
                    carry()
                    pool.tensor_copy(slot_row[:], slot_info[:, e, 0]).then_inc(slot_ready, 1)
                    pool.tensor_copy(slot_gate[:], slot_info[:, e, 1]).then_inc(slot_ready, 1)
                    pool.wait_ge(y_ready, n + 1)
                    pool.wait_ge(slot_ready, 2 * n + 2)
                    carry()
                    pool.indirect_dma_start(acc_dram, bass.IndirectOffsetOnAxis(ap=slot_row[0:CAP, 0:1], axis=0), yg[:],
                                            None, bounds_check=T - 1, oob_is_err=False,
                                            compute_op=ALU.add).then_inc(scattered, 16)

                pool.memset(st[:, 15:16], RMS_EPS).then_inc(eps_set, 1)
                pool.wait_ge(slots_in, 16)
                for n in range(3):
                    choose(n, slice(n, n + 1))
                pool.wait_ge(acc_init, 16 * CT)
                choose(3, slice(3, 4))
                add_y(0, slice(0, 1))
                with pool.Fori(3, E - 1) as n:
                    choose(n + 1, bass.ds(n + 1, 1))
                    add_y(n - 2, bass.ds(n - 2, 1))
                for n in range(E - 3, E):
                    add_y(n, slice(n, n + 1))

                def next_ranks(r):
                    pool.wait_ge(pick_ready, E)
                    pool.tensor_scalar(rankm[:], rankm[:], -float(CAP), None, ALU.add).then_inc(ranks_moved, 1)
                    pool.wait_ge(ranks_moved, r)
                    carry()

                def overflow(e, k):
                    choose(k + E, bass.ds(e, 1))
                    add_y(k + E, slice(0, 1))

                k = each_overflow(pool, overflow, next_ranks)
                pool.wait_ge(scattered, k * 16 + 16 * E)
                carry()
                pool.sem_inc(all_added, 1)

            @block.tensor
            def _(pe):
                def turn_x(n, e=None):
                    pe.wait_ge(pick_ready, n + 1)
                    if not (isinstance(n, int) and n < 2):
                        pe.wait_ge(biased, n - 1)
                    e = n if e is None else e
                    for k in range(KT):
                        for c in range(CT):
                            pe.matmul(bank[:, X, k * CAP:(k + 1) * CAP], x_tok[:, c, k * P:(k + 1) * P],
                                      pick[:, c, 0:CAP], start=(c == 0), stop=(c == CT - 1))
                    for c in range(CT):
                        mm = pe.matmul(bank[:, INFO, 0:2], pick[:, c, :], meta[:, c, e, :] if isinstance(e, int)
                                       else meta[:, c, bass.ds(e, 1), :].rearrange("p a two -> p (a two)"),
                                       start=(c == 0), stop=(c == CT - 1))
                    mm.then_inc(xt_psum, 1)

                def turn_h(n, gathered):
                    pe.wait_ge(h_copied, 4 * n + 4)
                    pe.wait_ge(xs_ready, gathered)
                    pe.wait_ge(info_ready, gathered)
                    for j in range(2 * FF // P):
                        mm = pe.matmul(bank[:, HT + j // 8, (j % 8) * CAP:(j % 8 + 1) * CAP],
                                       h_rows[:, j * P:(j + 1) * P], halves[:], start=True, stop=True)
                    mm.then_inc(ht_psum, 1)

                def products(n, j):
                    pos, buf = place(n, j), j % SPLIT
                    pe.wait_ge(high_done, pos + 1)
                    for w in (w_high, w_low):
                        if w is w_low:
                            pe.wait_ge(low_done, pos + 1)
                        for q in range(4):
                            if j < UC:
                                if j == 0 and w is w_high and not (isinstance(n, int) and n == 0):
                                    pe.wait_ge(h_copied, 4 * n - 3 + q)
                                mm = pe.matmul(bank[:, H + q, :], xs[:, j, :], w[:, buf, q * 512:(q + 1) * 512],
                                               start=(j == 0 and w is w_high), stop=(j == UC - 1 and w is w_low))
                            else:
                                i = j - UC
                                mm = pe.matmul(bank[:, Y + q % 2, :], av[:, 2 * i + q // 2, :],
                                               w[:, buf, q * 512:(q + 1) * 512],
                                               start=(i == 0 and w is w_high and q < 2),
                                               stop=(i == DC - 1 and w is w_low and q >= 2))
                    mm.then_inc(mm_done, 1)

                def ups(n, last=False):
                    pe.wait_ge(xs_ready, n + 1)
                    for j in range(UC):
                        products(n, j)
                        if j == 0 and not (isinstance(n, int) and n == 0):
                            turn_h(n - 1, n + 1)
                        if j == 6 and not last:
                            turn_x(n + 1)

                def downs(n):
                    pe.wait_ge(av_ready, n)
                    if not (isinstance(n, int) and n == 1):
                        pe.wait_ge(y_ready, n - 1)
                    for j in range(UC, CPR):
                        products(n, j)

                turn_x(0)
                ups(0)
                ups(1)
                downs(1)
                with pe.Fori(2, E - 1) as n:
                    ups(n)
                    downs(n)
                ups(E - 1, last=True)
                downs(E - 1)
                turn_h(E - 1, E)
                downs(E)
                for c, (t0, n) in enumerate(TOK):
                    mm = pe.transpose(bank[0:E, H, t0:t0 + n], meta[0:n, c, :, 1], ident[0:n, 0:n])
                mm.then_inc(gt_psum, 1)
                pe.wait_ge(gt_ready, 1)

                def overflow(e, k):
                    n = k + E
                    pe.wait_ge(y_ready, n)
                    turn_x(n, e)
                    pe.wait_ge(xs_ready, n + 1)
                    for i in range(UC):
                        pe.wait_ge(landed[i], k * 16 + 16 * (E + 1))
                        for q in range(4):
                            mm = pe.matmul(bank[:, H + q, :], xs[:, i, :].bitcast(F32),
                                           raw_up[:, i, q * 512:(q + 1) * 512], start=(i == 0), stop=(i == UC - 1))
                        mm.then_inc(mm_done, 1)
                    turn_h(n, n + 1)
                    pe.wait_ge(av_ready, n + 1)
                    for i in range(DC):
                        pe.wait_ge(landed[UC + i], k * 16 + 16 * (E + 1))
                        for q in range(4):
                            mm = pe.matmul(bank[:, Y + q % 2, :], av[:, 2 * i + q // 2, :].bitcast(F32),
                                           raw_down[:, i, q * 512:(q + 1) * 512],
                                           start=(i == 0 and q < 2), stop=(i == DC - 1 and q >= 2))
                        mm.then_inc(mm_done, 1)

                k = each_overflow(pe, overflow)
                pe.wait_ge(y_ready, k + E)
                pe.sem_inc(pe_passed, 1)
                pe.wait_ge(bd_in, 16)
                for c, (t0, n) in enumerate(TOK):
                    for q in range(2):
                        mm = pe.matmul(bank[0:n, 2 * c + q, :], gt[:, t0:t0 + n], b_down_sb[:, q * 512:(q + 1) * 512],
                                       start=True, stop=True)
                    mm.then_inc(gb_psum, 1)

            @block.scalar
            def _(act):
                def high(n, j):
                    pos = place(n, j)
                    src = raw_up[:, j, :] if j < UC else raw_down[:, j - UC, :]
                    e = n if j < UC else n - 1
                    act.wait_ge(landed[j], 16 * e + 16)
                    if not (isinstance(pos, int) and pos < SPLIT):
                        act.wait_ge(mm_done, pos - SPLIT + 1)
                    nc.scalar.activation(w_high[:, j % SPLIT, :], src, ACT.Copy).then_inc(high_done, 1)

                def x_high(n, used):
                    act.wait_ge(xt_psum, n + 1)
                    if used is not None:
                        act.wait_ge(mm_done, used)
                    nc.scalar.activation(xs[:, :, 0:CAP], bank[:, X, :].rearrange("p (k s) -> p k s", k=KT),
                                         ACT.Copy).then_inc(xs_high, 1)

                def copy_h(n, used):
                    act.wait_ge(mm_done, used)
                    if not (isinstance(n, int) and n < 1):
                        act.wait_ge(ht_psum, n)
                    if not (isinstance(n, int) and n < 2):
                        act.wait_ge(y_ready, n - 1)
                    for q in range(4):
                        nc.scalar.activation(h_rows[:, q * 512:(q + 1) * 512], bank[:, H + q, :],
                                             ACT.Copy).then_inc(h_copied, 1)

                def sigmoid(n):
                    act.wait_ge(clamped, n + 1)
                    nc.scalar.activation(sig[:], hb[:, 0:KT, :], ACT.Sigmoid, scale=ALPHA).then_inc(sig_ready, 1)

                def act_split(n, used):
                    act.wait_ge(act_ready, n + 1)
                    if used is not None:
                        act.wait_ge(mm_done, used)
                    nc.scalar.activation(av[:, :, 0:CAP], sig[:], ACT.Copy).then_inc(act_high, 1)

                def y_low(n, used, turned):
                    act.wait_ge(mm_done, used)
                    act.wait_ge(slot_ready, 2 * n + 2)
                    act.wait_ge(ht_psum, turned)
                    nc.scalar.activation(yl.rearrange("p (a b) -> p a b", a=2), bank[CAP:2 * CAP, Y:Y + 2, :],
                                         ACT.Copy, scale=slot_gate[CAP:2 * CAP, 0:1]).then_inc(yl_ready, 1)

                def step(n, last=False):
                    early = isinstance(n, int) and n < 2
                    for j in range(4):
                        high(n, j)
                    if not early:
                        y_low(n - 2, downs_done(n - 2), n)
                    high(n, 4)
                    sigmoid(n - 1)
                    high(n, 5)
                    act_split(n - 1, None if early else downs_done(n - 2))
                    for j in range(6, 11):
                        high(n, j)
                    if not last:
                        x_high(n + 1, ups_done(n))
                    copy_h(n, ups_done(n))
                    high(n, 11)

                x_high(0, None)
                for j in range(UC):
                    high(0, j)
                x_high(1, ups_done(0))
                copy_h(0, ups_done(0))
                step(1)
                step(2)
                with act.Fori(3, E - 1) as n:
                    step(n)
                step(E - 1, last=True)
                high(E, 8)
                high(E, 9)
                sigmoid(E - 1)
                y_low(E - 2, downs_done(E - 2), E)
                act_split(E - 1, downs_done(E - 2))
                high(E, 10)
                high(E, 11)
                act.wait_ge(y_ready, E - 1)
                y_low(E - 1, LAST, E)
                act.wait_ge(gt_psum, 1)
                nc.scalar.activation(gt[:], bank[0:E, H, 0:T], ACT.Copy).then_inc(gt_ready, 1)

                def overflow(e, k):
                    n = k + E
                    x_high(n, k * CPR + LAST)
                    act.wait_ge(y_ready, n)
                    copy_h(n, k * CPR + LAST + UC)
                    sigmoid(n)
                    act_split(n, k * CPR + LAST)
                    y_low(n, k * CPR + LAST + CPR, n + 1)

                each_overflow(act, overflow)
                for c, (t0, n) in enumerate(TOK):
                    act.wait_ge(fin_added, c + 1)
                    if c:
                        act.wait_ge(fin_ssq, c)
                    nc.scalar.activation(h_rows[0:n, 0:D], fin[0:n, c, :], ACT.Square,
                                         accum_out=st[0:n, c:c + 1]).then_inc(fin_ssq, 1)
                act.wait_ge(fin_ssq, 3)
                act.wait_ge(eps_set, 1)
                for c, (t0, n) in enumerate(TOK):
                    nc.scalar.activation(st[0:n, 3 + c:4 + c], st[0:n, c:c + 1], ACT.Sqrt, bias=st[0:n, 15:16],
                                         scale=1.0 / D).then_inc(fin_root, 1)

            @block.vector
            def _(dve):
                tt, ts, stt = nc.vector.tensor_tensor, nc.vector.tensor_scalar, nc.vector.scalar_tensor_tensor

                def low(n, j):
                    src = raw_up[:, j, :] if j < UC else raw_down[:, j - UC, :]
                    dve.wait_ge(high_done, place(n, j) + 1)
                    tt(w_low[:, j % SPLIT, :], src, w_high[:, j % SPLIT, :].bitcast(F32),
                       ALU.subtract).then_inc(low_done, 1)

                def x_low(n, e):
                    dve.wait_ge(xs_high, n + 1)
                    tt(xs[:, :, CAP:2 * CAP], bank[:, X, :].rearrange("p (k s) -> p k s", k=KT),
                       xs[:, :, 0:CAP].bitcast(F32), ALU.subtract).then_inc(xs_ready, 1)
                    tt(slot_info[:, e, :], bank[:, INFO, 0:2].rearrange("p (a b) -> p a b", a=1),
                       nobody[:].rearrange("p (a b) -> p a b", a=1), ALU.add).then_inc(info_ready, 1)

                def bias_clamp(n, e):
                    dve.wait_ge(ht_psum, n + 1)
                    if not (isinstance(n, int) and n == 0):
                        dve.wait_ge(act_ready, n)
                    tt(hb[:], bank[:, HT:HT + 2, :].rearrange("p a (j s) -> p (a j) s", s=CAP),
                       bias_up[:, :, e].broadcast_to([P, 2 * FF // P, CAP]), ALU.add).then_inc(biased, 1)
                    dve.wait_ge(biased, n + 1)
                    ts(hb[:, 0:KT, :], hb[:, 0:KT, :], LIMIT, None, ALU.min).then_inc(clamped, 1)
                    ts(hb[:, KT:, :], hb[:, KT:, :], LIMIT, -LIMIT, ALU.min, ALU.max).then_inc(lin_ready, 1)

                def activate(n):
                    dve.wait_ge(sig_ready, n + 1)
                    dve.wait_ge(clamped, n + 1)
                    dve.wait_ge(lin_ready, 2 * n + 1)
                    stt(out=hb[:, KT:, :], in0=hb[:, KT:, :], scalar=1.0, in1=hb[:, 0:KT, :],
                        op0=ALU.add, op1=ALU.mult).then_inc(lin_ready, 1)
                    dve.wait_ge(lin_ready, 2 * n + 2)
                    tt(sig[:], sig[:], hb[:, KT:, :], ALU.mult).then_inc(act_ready, 1)

                def act_low(n):
                    dve.wait_ge(act_high, n + 1)
                    dve.wait_ge(act_ready, n + 1)
                    tt(av[:, :, CAP:2 * CAP], sig[:], av[:, :, 0:CAP].bitcast(F32), ALU.subtract).then_inc(av_ready, 1)

                def y_sum(n):
                    dve.wait_ge(yl_ready, n + 1)
                    if not (isinstance(n, int) and n == 0):
                        dve.wait_ge(scattered, 16 * n)
                    stt(out=yg[:].rearrange("p (a b) -> p a b", a=2), in0=bank[0:CAP, Y:Y + 2, :],
                        scalar=slot_gate[0:CAP, 0:1], in1=yl.rearrange("p (a b) -> p a b", a=2),
                        op0=ALU.mult, op1=ALU.add).then_inc(y_ready, 1)

                def at(e):
                    return slice(e, e + 1) if isinstance(e, int) else bass.ds(e, 1)

                def step(n, last=False):
                    for j in range(4):
                        low(n, j)
                    bias_clamp(n - 1, at(n - 1))
                    if not (isinstance(n, int) and n < 2):
                        y_sum(n - 2)
                    low(n, 4)
                    activate(n - 1)
                    low(n, 5)
                    act_low(n - 1)
                    for j in range(6, 11):
                        low(n, j)
                    if not last:
                        x_low(n + 1, at(n + 1))
                    low(n, 11)

                nc.vector.memset(nobody[:, 0:1], float(NOBODY)).then_inc(nobody_set, 1)
                nc.vector.memset(nobody[:, 1:2], 0.0).then_inc(nobody_set, 1)
                dve.wait_ge(nobody_set, 2)
                x_low(0, at(0))
                for j in range(UC):
                    low(0, j)
                x_low(1, at(1))
                step(1)
                step(2)
                with dve.Fori(3, E - 1) as n:
                    step(n)
                step(E - 1, last=True)
                low(E, 8)
                low(E, 9)
                bias_clamp(E - 1, at(E - 1))
                y_sum(E - 2)
                activate(E - 1)
                act_low(E - 1)
                low(E, 10)
                low(E, 11)
                y_sum(E - 1)

                def overflow(e, k):
                    n = k + E
                    dve.wait_ge(slot_ready, 2 * n)
                    x_low(n, at(0))
                    bias_clamp(n, at(e))
                    activate(n)
                    act_low(n)
                    y_sum(n)

                each_overflow(dve, overflow)
                for c, (t0, n) in enumerate(TOK):
                    dve.wait_ge(fin_in[c], 16)
                    dve.wait_ge(gb_psum, c + 1)
                    rows = fin[0:n, c, :].rearrange("p (a b) -> p a b", a=2)
                    tt(rows, rows, bank[0:n, 2 * c:2 * c + 2, :], ALU.add).then_inc(fin_added, 1)
                dve.wait_ge(gf_in, 16)
                dve.wait_ge(fin_added, 3)
                for c, (t0, n) in enumerate(TOK):
                    dve.wait_ge(fin_root, c + 1)
                    nc.vector.reciprocal(st[0:n, 3 + c:4 + c], st[0:n, 3 + c:4 + c]).then_inc(fin_chain, 1)
                    dve.wait_ge(fin_chain, c + 1)
                    stt(out=fin[0:n, c, :], in0=fin[0:n, c, :], scalar=st[0:n, 3 + c:4 + c], in1=g_fin[0:n, :],
                        op0=ALU.mult, op1=ALU.mult).then_inc(fin_ready, 1)


def shape_constants():
    import numpy as np

    f = np.float32
    sq = np.zeros((P, 9, P), f)
    sq[:, 0] = np.eye(P)
    sq[:, 1, 0:CAP] = np.concatenate([np.eye(CAP), np.eye(CAP)])
    sq[:, 2] = np.triu(np.ones((P, P)), 1)
    sq[:, 3] = 1.0 / HD
    sq[:, 4] = 1.0
    lg = np.log(f(1.0) - f(2.0) ** (f(-5.0) - np.arange(HEADS, dtype=f)))
    pos = np.arange(CHUNK, dtype=f)
    diff = pos[None, :] - pos[:, None]
    xi = np.zeros((P, HEADS + 1, CHUNK), f)
    for h in range(HEADS):
        sq[:, 5 + h] = np.where(diff >= 0, np.exp(lg[h] * np.maximum(diff, 0)), 0)
        xi[:, h] = np.exp(lg[h] * (pos + 1))[None, :]
        xi[:, HEADS, h] = np.exp(lg[h] * (CHUNK - 1 - pos))
    half = HD // 2
    inv = (f(10000.0) ** (-np.arange(half, dtype=f) / f(half))).astype(f)
    at = np.concatenate([np.arange(SEQ), np.full(NS, 2048)]).astype(f)
    ang = (at[None, :] * inv[:, None]).astype(f)
    rope = np.zeros((P, 2, T), f)
    rope[:half, 0] = rope[half:, 0] = np.cos(ang)
    rope[:half, 1] = np.sin(ang)
    rope[half:, 1] = -np.sin(ang)
    route = np.zeros((P, E + 2 * CT + NS), f)
    route[:, :E] = np.arange(E)
    for c in range(CT):
        route[:, E + c] = np.arange(P) + c * P - NOBODY
        route[:, E + CT + NS + c] = np.arange(P) + c * P < T
    route[:NS, E + CT:E + CT + NS] = np.eye(NS)
    slots = np.tile(np.arange(P, dtype=f) % CAP, (P, 1))
    gammas = [(float(np.exp(lg[h])), float(np.exp(lg[h] * f(CHUNK)))) for h in range(HEADS)]
    return {"c_square": sq, "c_rope": rope, "c_xi": xi, "c_route": route, "c_slots": slots}, gammas


_INS = ["x_prompt", "x_sample", "state_conv", "state_ret", "norm_mix", "w_in", "conv_w", "ret_norm", "w_out",
        "norm_ffn", "w_router", "b_router", "w_up", "b_up", "w_down", "b_down", "norm_final"]
_OUTS = [(1, SEQ, D), (NS, 1, D), (1, 1, 2, CONV_W), (1, 1, HEADS, HD, HD), (1, NS, 2, CONV_W),
         (1, NS, HEADS, HD, HD)]


def build(nc, inputs):
    import numpy as np

    consts, gammas = shape_constants()
    arrays, args = {}, []
    for name, a in [(n, inputs[n]) for n in _INS] + list(consts.items()):
        a = np.ascontiguousarray(a)
        arrays[f"in_{name}"] = a
        args.append(nc.dram_tensor(f"in_{name}", a.shape, mybir.dt.from_np(a.dtype), kind="ExternalInput").ap())
    outs = [nc.dram_tensor(f"out_{i}", shape, F32, kind="ExternalOutput").ap() for i, shape in enumerate(_OUTS)]
    hybrid_layer(nc, *args, gammas, *outs)
    return arrays


def kernel(**inputs):
    import concourse.bacc as _bacc
    from concourse.bass_utils import run_bass_kernel_spmd as _run

    nc = _bacc.Bacc("TRN2", target_bir_lowering=False, num_devices=1)
    arrays = build(nc, inputs)
    r = _run(nc, [arrays], core_ids=[0])
    return tuple(r.results[0][f"out_{i}"] for i in range(len(_OUTS)))
```

```python
from contextlib import ExitStack

import concourse.bass as bass
from concourse import mybir

F32 = mybir.dt.float32
F32R = mybir.dt.float32r
I32 = mybir.dt.int32
U32 = mybir.dt.uint32
ALU = mybir.AluOpType
ACT = mybir.ActivationFunctionType
AX = mybir.AxisListType

P = 128
D = 1024
SEQ = 256
NS = 8
T = SEQ + NS
CT = 3
CONV_W = 512
HEADS = 4
HD = 128
CHUNK = 128
PROJ = 7 * 512
E = 32
TOP = 4
FF = 1024
KT = D // P
CAP = 64
OVER = -(-T // CAP)
NOBODY = 1 << 20
LIMIT = 7.0
ALPHA = 1.702
RMS_EPS = 1e-6
GN_EPS = 1e-5
W = 256
UC = 8
DC = 4
CPR = UC + DC
SPLIT = 4
TOK = [(0, 128), (128, 128), (256, NS)]
XC, GB, GC, Q, K, V, G = range(7)
ORDER = [K, Q, V, GC, XC, G, GB]


def hybrid_layer(nc, x_prompt, x_sample, state_conv, state_ret, norm_mix, w_in, conv_w, ret_norm, w_out,
                 norm_ffn, w_router, b_router, w_up, b_up, w_down, b_down, norm_final,
                 c_square, c_rope, c_xi, c_route, c_slots, gammas,
                 y_prompt, y_sample, conv_prompt, ret_prompt, conv_sample, ret_sample):
    acc_dram = nc.dram_tensor("acc_rows", [T, D], F32, kind="Internal").ap()

    w_up_v = w_up[0].rearrange("e (k p) n -> e k p n", p=P)
    w_down_v = w_down[0].rearrange("e (c k p) n -> e c p k n", p=P, k=2)

    with ExitStack() as top:
        def make(ctx):
            def sb(name, shape, dt=F32):
                return ctx.enter_context(nc.sbuf_tensor(name, shape, dt))
            return sb

        def sem(name):
            return top.enter_context(nc.semaphore(name))

        sb = make(top)
        raw_up = sb("raw_up", [P, UC, 2 * FF])
        raw_down = sb("raw_down", [P, DC, 2 * D])
        ident = sb("ident", [P, P])
        halves = sb("halves", [P, CAP])
        slots = sb("slots", [P, P])
        minus_half = sb("minus_half", [P, 1])
        x_tok = sb("x_tok", [P, CT, D])
        pick = sb("pick", [P, CT, P])
        rankm = sb("rankm", [P, CT, E])
        meta = sb("meta", [P, CT, E, 2])
        bias_up = sb("bias_up", [P, 2 * FF // P, E])
        counts = sb("counts", [P, E], I32)
        most = sb("most", [P, 1], I32)
        bank = top.enter_context(nc.psum_tensor("bank", [P, 8, 512], F32))

        landed = [sem(f"landed{s}") for s in range(CPR)]
        slots_in = sem("slots_in")
        pick_ready = sem("pick_ready")
        acc_init = sem("acc_init")
        out_done = sem("out_done")

        def load_down(sp, e, i):
            sp.dma_start(raw_down[:, i, :].rearrange("p (k n) -> p k n", k=2), w_down_v[e, i]).then_inc(landed[UC + i], 16)

        with ExitStack() as ph:
            sb = make(ph)
            w_ring = sb("w_ring", [P, 2, KT, W])
            h_tok = sb("h_tok", [P, CT, D])
            xnt = sb("xnt", [P, KT, T])
            mix_in = sb("mix_in", [P, KT, T])
            kr = sb("kr", [P, HEADS, T])
            qr = sb("qr", [P, HEADS, T])
            vt = sb("vt", [P, HEADS, T])
            sg = sb("sg", [P, HEADS, T])
            tmp = sb("tmp", [P, HEADS, T])
            square = sb("square", [P, 7, P])
            rope = sb("rope", [P, 2, T])
            xi = sb("xi", [P, HEADS, CHUNK])
            zeta = sb("zeta", [P, HEADS])
            route = sb("route", [P, E + 2 * CT + NS])
            rows = sb("rows", [P, P])
            vec = sb("vec", [P, 96])
            g_ffn = sb("g_ffn", [P, D])
            u_pad = sb("u_pad", [P, HEADS, SEQ + 2])
            u_s = sb("u_s", [P, HEADS, NS])
            k_tok = sb("k_tok", [P, 2, HEADS, HD])
            v_tok = sb("v_tok", [P, 2, HEADS, HD])
            small = sb("small", [P, 16])
            state = raw_down[:, 2:4, :].rearrange("p a (b e) -> p (a b) e", e=HD)
            ks_tok = h_tok[0:NS, 0, 0:HEADS * HD]
            vs_tok = h_tok[0:NS, 1, 0:HEADS * HD]
            scores = h_tok[:, 2, :].rearrange("p (c h n) -> p c h n", c=2, h=HEADS)
            q_xi = h_tok[:, 0, 512:1024].rearrange("p (h n) -> p h n", h=HEADS)
            state1 = h_tok[:, 1, 512:1024].rearrange("p (h n) -> p h n", h=HEADS)
            nc_t = sb("nc_t", [P, HEADS, 2 + NS])
            vd = raw_up[0:NS, UC - 1, 0:NS * HD].rearrange("p (b e) -> p b e", b=NS)
            nc_rows = v_tok[0:2 + NS, 0, :, :].rearrange("p h e -> p (h e)")
            w_rt = sb("w_rt", [P, KT, E])
            b_rt = sb("b_rt", [P, E])
            qk = sb("qk", [P, HEADS, NS])
            UPPER, MEAN, ONES, DECAY = 0, 1, 2, 3
            TOKEN_BANK = ((2, 3, 4), (5, 6, 4))
            decay = square[:, DECAY:DECAY + HEADS, :]

            x_in = [sem(f"x_in{c}") for c in range(CT)]
            const_in = sem("const_in")
            ident_in = sem("ident_in")
            rows_in = sem("rows_in")
            misc_in = sem("misc_in")
            state_in = sem("state_in")
            win = [sem(f"win{s}") for s in range(2)]
            v_chain = sem("v_chain")
            g_chain = sem("g_chain")
            ssq_done = sem("ssq_done")
            x_scaled = sem("x_scaled")
            rows_t = sem("rows_t")
            vec_ready = sem("vec_ready")
            xnt_psum = sem("xnt_psum")
            xnt_ready = sem("xnt_ready")
            proj_psum = sem("proj_psum")
            proj_out = sem("proj_out")
            k_rot = sem("k_rot")
            q_rot = sem("q_rot")
            kv_tok_psum = sem("kv_tok_psum")
            kv_tok = sem("kv_tok")
            s_tok_psum = sem("s_tok_psum")
            s_tok = sem("s_tok")
            sc_psum = sem("sc_psum")
            sc_ready = sem("sc_ready")
            kv_psum = sem("kv_psum")
            s1_ready = sem("s1_ready")
            s2_ready = sem("s2_ready")
            o_psum = sem("o_psum")
            o_ready = sem("o_ready")
            vd_ready = sem("vd_ready")
            kvs_psum = sem("kvs_psum")
            snew = sem("snew")
            mean_psum = sem("mean_psum")
            dev_ready = sem("dev_ready")
            var_psum = sem("var_psum")
            std_ready = sem("std_ready")
            mix_ready = sem("mix_ready")
            ncv_ready = sem("ncv_ready")
            ncv_psum = sem("ncv_psum")
            ncv_rows = sem("ncv_rows")
            wo_psum = sem("wo_psum")
            wo_out = sem("wo_out")
            ht_psum1 = sem("ht_psum1")
            h_ready = sem("h_ready")
            ssq2 = sem("ssq2")
            lg_psum = sem("lg_psum")
            top_ready = sem("top_ready")
            exp_ready = sem("exp_ready")
            mask_ready = sem("mask_ready")
            rank_psum = sem("rank_psum")
            bu_in = sem("bu_in")
            bu_psum = sem("bu_psum")
            bu_ready = sem("bu_ready")
            gffn_in = sem("gffn_in")
            x_zero = sem("x_zero")
            xc_used = sem("xc_used")
            gated = sem("gated")
            sq_psum = sem("sq_psum")
            qk_ready = sem("qk_ready")
            qk_psum = sem("qk_psum")
            w_rt_ready = sem("w_rt_ready")
            small_zero = sem("small_zero")
            logits_read = sem("logits_read")
            lg_copied = sem("lg_copied")
            scale_ready = sem("scale_ready")
            eps_ready = sem("eps_ready")
            state1_out = sem("state1_out")
            state_out = sem("state_out")

            rt = kr[:, :, :].rearrange("p h n -> p (h n)")
            logit = rt[:, 0:CT * E].rearrange("p (c e) -> p c e", c=CT)
            top8 = rt[:, 96:96 + CT * 8].rearrange("p (c e) -> p c e", c=CT)
            gate = rt[:, 216:216 + CT * TOP].rearrange("p (c k) -> p c k", c=CT)
            idxf = rt[:, 228:228 + CT * TOP].rearrange("p (c k) -> p c k", c=CT)
            gsum = rt[:, 252:252 + CT]
            mask = rt[:, 256:256 + CT * E].rearrange("p (c e) -> p c e", c=CT)
            ONEH = CT * TOP * E
            onehot = qr[:, :, :].rearrange("p h n -> p (h n)")[:, 0:ONEH].rearrange("p (c k e) -> p c k e", c=CT, k=TOP)
            prod = vt[:, :, :].rearrange("p h n -> p (h n)")[:, 0:ONEH].rearrange("p (c k e) -> p c k e", c=CT, k=TOP)
            idx8 = sb("idx8", [P, CT, 8], U32)
            b_up_sb = raw_up[0:E, UC - 2, :]
            xn2 = x_tok
            lg_rows = sg[0:E, 0, :]
            junk = u_pad[:, :, 0:256]

            block = ph.enter_context(nc.Block())

            w_in_v = w_in[0].rearrange("(k p) n -> p k n", p=P)
            w_out_v = w_out[0].rearrange("(k p) n -> p k n", p=P)

            def chunk_src(j):
                if j < 2 * len(ORDER):
                    at = ORDER[j // 2] * 512 + j % 2 * W
                    return w_in_v[:, :, at:at + W]
                j -= 2 * len(ORDER)
                return w_out_v[:, :, j * W:(j + 1) * W]

            def store_states(sp):
                sp.wait_ge(s2_ready, 1)
                sp.dma_start(ret_prompt[0, 0].rearrange("h d e -> d h e"), state1).then_inc(state1_out, 16)
                sp.wait_ge(snew, 8)
                sp.dma_start(ret_sample[0].rearrange("b h d e -> d (b h) e"), state[:]).then_inc(state_out, 16)
                sp.wait_ge(ncv_rows, 1)
                sp.dma_start(conv_prompt[0, 0], nc_rows[0:2, :]).then_inc(out_done, 16)
                sp.dma_start(conv_sample[0, :, 1, :], nc_rows[2:2 + NS, :]).then_inc(out_done, 16)

            @block.sync
            def _(sp):
                sp.dma_start(x_tok[:, 0, :], x_prompt[0, 0:P]).then_inc(x_in[0], 16)
                sp.dma_start(ident[:], c_square[:, 0, :]).then_inc(ident_in, 16)
                sp.dma_start(x_tok[:, 1, :], x_prompt[0, P:SEQ]).then_inc(x_in[1], 16)
                sp.wait_ge(x_zero, 1)
                sp.dma_start(x_tok[0:NS, 2, :], x_sample.rearrange("b s d -> (b s) d")).then_inc(x_in[2], 16)
                sp.dma_start(rows[0:8, :], norm_mix.rearrange("a (k p) -> (a k) p", p=P)).then_inc(rows_in, 16)
                sp.dma_start(rows[8:12, :], ret_norm.rearrange("a (k p) -> (a k) p", p=P)).then_inc(rows_in, 16)
                sp.dma_start(rows[12:24, :], conv_w[0].rearrange("j (m p) -> (j m) p", p=P)).then_inc(rows_in, 16)
                sp.dma_start(rows[24:88, :], state_conv[0].rearrange("b j (m p) -> (b j m) p", p=P)).then_inc(rows_in, 16)
                sp.dma_start(rows[88:96, :], norm_ffn.rearrange("a (k p) -> (a k) p", p=P)).then_inc(rows_in, 16)
                sp.dma_start(halves[:], c_square[:, 1, 0:CAP]).then_inc(const_in, 16)
                sp.dma_start(square[:], c_square[:, 2:9, :]).then_inc(const_in, 16)
                sp.dma_start(rope[:], c_rope).then_inc(const_in, 16)
                sp.dma_start(xi[:], c_xi[:, 0:HEADS, :]).then_inc(const_in, 16)
                sp.dma_start(zeta[:], c_xi[:, HEADS, 0:HEADS]).then_inc(const_in, 16)
                sp.dma_start(route[:], c_route).then_inc(const_in, 16)
                for j in range(2):
                    sp.dma_start(w_ring[:, j], chunk_src(j)).then_inc(win[j], 16)
                sp.dma_start(slots[:], c_slots).then_inc(slots_in, 16)
                sp.dma_start(state[:], state_ret[0].rearrange("b h d e -> d (b h) e")).then_inc(state_in, 16)
                sp.dma_start(w_rt[:], w_router[0].rearrange("(k p) e -> p k e", p=P)).then_inc(misc_in, 16)
                sp.dma_start(b_rt[:], b_router.partition_broadcast(P)[:, 0, :]).then_inc(misc_in, 16)
                sp.dma_start(b_up_sb, b_up[0]).then_inc(bu_in, 16)
                sp.dma_start(g_ffn[:], norm_ffn.partition_broadcast(P)[:, 0, :]).then_inc(gffn_in, 16)
                sp.dma_start(conv_sample[0, :, 0, :], state_conv[0, :, 1, :]).then_inc(out_done, 16)
                for j in range(2, 2 * len(ORDER) + 4):
                    if j < 2 * len(ORDER) + 2:
                        sp.wait_ge(proj_psum, 2 * (j - 1))
                    else:
                        sp.wait_ge(wo_psum, 2 * (j - 2 * len(ORDER) - 1))
                    sp.dma_start(w_ring[:, j % 2], chunk_src(j)).then_inc(win[j % 2], 16)
                    if j >= 5:
                        k = j - 5
                        if k < UC - 1:
                            if k == UC - 2:
                                sp.wait_ge(bu_psum, 1)
                            sp.dma_start(raw_up[:, k, :], w_up_v[0, k]).then_inc(landed[k], 16)
                        elif k < UC + 1:
                            load_down(sp, 0, k - UC + 1)
                    if j == 2 * len(ORDER) + 1:
                        store_states(sp)
                    elif j > 2 * len(ORDER) + 1:
                        sp.wait_ge(state_out, 16)
                        load_down(sp, 0, j - 2 * len(ORDER))
                sp.dma_start(raw_up[:, UC - 1, :], w_up_v[0, UC - 1]).then_inc(landed[UC - 1], 16)
                for c, (t0, n) in enumerate(TOK):
                    sp.wait_ge(h_ready, CT + c + 1)
                    sp.dma_start(acc_dram[t0:t0 + n, :], h_tok[0:n, c, :]).then_inc(acc_init, 16)
                sp.wait_ge(acc_init, 16 * CT)
                sp.wait_ge(state1_out, 16)

            @block.gpsimd
            def _(pool):
                pool.memset(x_tok[:, 2, :], 0.0).then_inc(x_zero, 1)
                pool.memset(minus_half[:], -0.5).then_inc(g_chain, 1)
                chain = [1]

                def root(out, in_, eps, n):
                    chain[0] += 1
                    pool.tensor_scalar(out, in_, eps, None, ALU.add).then_inc(g_chain, 1)
                    pool.wait_ge(g_chain, chain[0])
                    return pool.tensor_tensor(out, out, minus_half[0:n].broadcast_to(list(out.shape)), ALU.pow)


                def scale(summed, at):
                    for c, (t0, n) in enumerate(TOK):
                        pool.wait_ge(summed, c + 1)
                        root(small[0:n, at + 3 + c:at + 4 + c], small[0:n, at + c:at + c + 1], RMS_EPS, n).then_inc(scale_ready, 1)

                scale(ssq_done, 0)
                pool.wait_ge(s_tok, 2)
                eye8 = route[0:NS, E + CT:E + CT + NS].rearrange("p (b a) -> p b a", a=1)
                for h in range(HEADS):
                    if h:
                        pool.wait_ge(kvs_psum, 2 * h)
                    pool.tensor_tensor(vd, vs_tok[:, h * HD:(h + 1) * HD].rearrange("p (a e) -> p a e", a=1)
                                       .broadcast_to([NS, NS, HD]), eye8.broadcast_to([NS, NS, HD]),
                                       ALU.mult).then_inc(vd_ready, 1)
                pool.wait_ge(ssq2, 2 * CT)
                chain[0] += 1
                pool.tensor_tensor(small[:, 9:12], small[:, 6:9], small[:, 9:12], ALU.add).then_inc(g_chain, 1)
                pool.wait_ge(g_chain, chain[0])
                root(small[:, 9:12], small[:, 9:12], RMS_EPS, P).then_inc(scale_ready, 1)

            @block.tensor
            def _(pe):
                def turn(out, in_, n):
                    return pe.transpose(out, in_, ident[0:n, 0:n])

                pe.wait_ge(ident_in, 16)
                for k in range(KT):
                    for c, (t0, n) in enumerate(TOK):
                        if k == 0:
                            pe.wait_ge(x_scaled, c + 1)
                        if k == 0 and c == 1:
                            pe.wait_ge(rows_in, 80)
                            turn(bank[:, 7, 0:96], rows[0:96, :], 96).then_inc(rows_t, 1)
                        if k == 7 and c == 0:
                            pe.wait_ge(vec_ready, 1)
                        mm = turn(bank[:, k, t0:t0 + n], h_tok[0:n, c, k * P:(k + 1) * P], n)
                    mm.then_inc(xnt_psum, 1)

                def project(j):
                    for m in range(4):
                        i = 4 * j + m
                        slot = i // 2 % 2
                        if m % 2 == 0:
                            pe.wait_ge(win[slot], 16 * (i // 4 + 1))
                        if 4 <= i < 20:
                            pe.wait_ge(proj_out, i - 3)
                        elif 20 <= i < 24:
                            pe.wait_ge(xc_used, i - 19)
                        elif i >= 24:
                            pe.wait_ge(proj_out, i - 7)
                        for k in range(KT):
                            mm = pe.matmul(bank[:, i % 4, 0:T], w_ring[:, slot, k, m % 2 * P:(m % 2 + 1) * P],
                                           xnt[:, k, :], start=(k == 0), stop=(k == KT - 1))
                        mm.then_inc(proj_psum, 1)
                        yield

                def run(j):
                    for _ in project(j):
                        pass

                pe.wait_ge(const_in, 16 * 6)
                pe.wait_ge(xnt_ready, KT)
                run(0)
                pe.wait_ge(bu_in, 16)
                for j in range(2 * FF // P):
                    mm = turn(bank[:, 6, j * E:(j + 1) * E], b_up_sb[:, j * P:(j + 1) * P], E)
                mm.then_inc(bu_psum, 1)
                run(1)
                run(2)
                pe.wait_ge(k_rot, 1)
                pe.wait_ge(proj_out, 12)
                pe.wait_ge(bu_ready, 1)
                for b, (src, c) in enumerate(((kr, 0), (kr, 1), (vt, 0), (vt, 1))):
                    for h in range(HEADS):
                        mm = turn(bank[:, 4 + b, h * HD:(h + 1) * HD], src[:, h, c * P:(c + 1) * P], P)
                    mm.then_inc(kv_tok_psum, 1)
                run(3)
                pe.wait_ge(kv_tok, 4)
                for b, src in enumerate((kr, vt)):
                    for h in range(HEADS):
                        mm = turn(bank[0:NS, 4 + b, h * HD:(h + 1) * HD], src[:, h, SEQ:T], P)
                    mm.then_inc(s_tok_psum, 1)
                pe.wait_ge(q_rot, 1)
                for c in range(2):
                    for h in range(HEADS):
                        at = slice(c * CHUNK, (c + 1) * CHUNK)
                        mm = pe.matmul(bank[:, 6 + c, h * P:(h + 1) * P], kr[:, h, at], qr[:, h, at],
                                       start=True, stop=True)
                    mm.then_inc(sc_psum, 1)
                run(4)
                pe.wait_ge(sc_ready, 2)
                pe.wait_ge(s_tok, 2)
                for c in range(2):
                    for h in range(HEADS):
                        mm = pe.matmul(bank[:, 6 + c, h * P:(h + 1) * P], k_tok[:, c, h, :], v_tok[:, c, h, :],
                                       start=True, stop=True)
                    mm.then_inc(kv_psum, 1)
                for c in range(2):
                    if c == 1:
                        pe.wait_ge(s1_ready, 1)
                    for h in range(HEADS):
                        mm = pe.matmul(bank[:, 4 + c, h * P:(h + 1) * P], v_tok[:, c, h, :], scores[:, c, h, :],
                                       start=True, stop=(c == 0))
                        if c == 1:
                            mm = pe.matmul(bank[:, 4 + c, h * P:(h + 1) * P], state1[:, h, :], q_xi[:, h, :],
                                           start=False, stop=True)
                    mm.then_inc(o_psum, 1)
                pe.wait_ge(s2_ready, 1)
                for h, _ in enumerate(project(5)):
                    pe.wait_ge(vd_ready, h + 1)
                    if h == 0:
                        pe.wait_ge(o_ready, 2)
                        pe.wait_ge(state_in, 16)
                    for b in range(NS):
                        pe.matmul(bank[:, 4, h * NS + b:h * NS + b + 1], state[:, b * HEADS + h, :],
                                  qr[:, h, SEQ + b:SEQ + b + 1], start=True, stop=True).then_inc(sq_psum, 1)
                    for half in range(2):
                        if h > 0:
                            pe.wait_ge(snew, 2 * h - 1 + half)
                        pe.matmul(bank[:, 6 + half, :], ks_tok[:, h * HD:(h + 1) * HD],
                                  vd[:, half * 4:half * 4 + 4, :], start=True, stop=True).then_inc(kvs_psum, 1)
                    if h == 0:
                        pe.wait_ge(qk_ready, 1)
                        pe.matmul(bank[:, 5, 0:HEADS * NS], square[:, ONES, :], qk[:], start=True, stop=True).then_inc(qk_psum, 1)
                last = project(6)
                next(last)
                pe.wait_ge(ncv_ready, 1)
                pe.wait_ge(o_ready, 3)
                pe.wait_ge(snew, 8)
                for h in range(HEADS):
                    pe.matmul(bank[:, 4 + h, 0:T], square[:, MEAN, :], tmp[:, h, :],
                              start=True, stop=True).then_inc(mean_psum, 1)
                next(last)
                for h in range(HEADS):
                    pe.wait_ge(dev_ready, h + 1)
                    pe.matmul(bank[:, 4 + h, 0:T], square[:, MEAN, :], vt[:, h, :],
                              start=True, stop=True).then_inc(var_psum, 1)
                next(last)
                pe.wait_ge(std_ready, 1)
                for m in range(4):
                    mm = turn(bank[0:2 + NS, 4, m * P:(m + 1) * P], nc_t[:, m, :], P)
                mm.then_inc(ncv_psum, 1)
                next(last)
                pe.wait_ge(std_ready, 4)
                pe.wait_ge(ncv_rows, 1)

                def by_token(m):
                    pe.wait_ge(wo_out, m + 1)
                    if m == 4:
                        pe.wait_ge(h_ready, 3)
                        pe.wait_ge(ssq2, 3)
                    for c, (t0, n) in enumerate(TOK):
                        turn(bank[0:n, TOKEN_BANK[m // 4][c], (m % 4) * P:(m % 4 + 1) * P], xnt[:, m, t0:t0 + n],
                             P).then_inc(ht_psum1, 1)
                    if m == 0:
                        pe.wait_ge(w_rt_ready, 1)
                    pe.matmul(bank[0:E, 7, 0:T], w_rt[:, m, :], xnt[:, m, :], start=(m == 0),
                              stop=(m == KT - 1)).then_inc(lg_psum, 1)

                for m in range(KT):
                    slot = m // 2 % 2
                    if m % 2 == 0:
                        pe.wait_ge(win[slot], 16 * (len(ORDER) + m // 4 + 1))
                    if m < 2:
                        pe.wait_ge(gated, 3 + m)
                    else:
                        pe.wait_ge(wo_out, m - 1)
                    for k in (4, 5, 6, 7, 0, 1, 2, 3):
                        for c, (t0, n) in enumerate(TOK) if k == 0 else ():
                            pe.matmul(bank[:, m % 2, t0:t0 + n], x_tok[0:n, c, m * P:(m + 1) * P], ident[0:n, 0:n],
                                      start=False, stop=False)
                        if m == 0:
                            if k >= 4:
                                pe.wait_ge(mix_ready, k - 3)
                            else:
                                pe.wait_ge(gated, k + 1)
                        mm = pe.matmul(bank[:, m % 2, 0:T], w_ring[:, slot, k, m % 2 * P:(m % 2 + 1) * P],
                                       mix_in[:, k, :], start=(k == 4), stop=(k == 3))
                    mm.then_inc(wo_psum, 1)
                    if m:
                        by_token(m - 1)
                by_token(KT - 1)
                pe.wait_ge(lg_copied, 1)
                for c, (t0, n) in enumerate(TOK):
                    mm = turn(bank[0:n, 0, c * E:(c + 1) * E], lg_rows[:, t0:t0 + n], E)
                mm.then_inc(lg_psum, 1)
                pe.wait_ge(logits_read, 1)
                pe.wait_ge(mask_ready, 1)
                flat = mask.rearrange("p c e -> p (c e)")
                pe.matmul(bank[:, 3, 0:CT * E], square[:, UPPER, :], flat, start=True, stop=False)
                for b in range(1, CT):
                    mm = pe.matmul(bank[:, 3, b * E:CT * E], square[:, ONES, :], flat[:, 0:(CT - b) * E],
                                   start=False, stop=(b == CT - 1))
                mm.then_inc(rank_psum, 1)
                for c in range(CT):
                    mm = pe.matmul(bank[:, 4, 0:E], square[:, ONES, :], mask[:, c, :],
                                   start=(c == 0), stop=(c == CT - 1))
                mm.then_inc(rank_psum, 1)

            @block.scalar
            def _(act):
                for c, (t0, n) in enumerate(TOK):
                    act.wait_ge(x_in[c], 16)
                    if c:
                        act.wait_ge(ssq_done, c)
                    nc.scalar.activation(junk[0:n], x_tok[0:n, c, :].rearrange("p (a b) -> p a b", a=4), ACT.Square,
                                         scale=D ** -0.5, accum_out=small[0:n, c:c + 1]).then_inc(ssq_done, 1)
                act.wait_ge(rows_t, 1)
                nc.scalar.activation(vec[:], bank[:, 7, 0:96], ACT.Copy).then_inc(vec_ready, 1)
                act.wait_ge(vec_ready, 1)
                for k in range(KT):
                    act.wait_ge(xnt_psum, k + 1)
                    nc.scalar.activation(xnt[:, k, :], bank[:, k, 0:T], ACT.Copy,
                                         scale=vec[:, k:k + 1]).then_inc(xnt_ready, 1)

                def out(j, dst, fn=ACT.Copy):
                    for m in range(4):
                        act.wait_ge(proj_psum, 4 * j + m + 1)
                        nc.scalar.activation(dst[:, m, :], bank[:, m, 0:T], fn).then_inc(proj_out, 1)

                out(0, kr)
                act.wait_ge(bu_psum, 1)
                nc.scalar.activation(bias_up[:], bank[:, 6, :].rearrange("p (j e) -> p j e", e=E),
                                     ACT.Copy).then_inc(bu_ready, 1)
                out(1, qr)
                out(2, vt)
                for b, dst in ((0, k_tok), (1, k_tok), (2, v_tok), (3, v_tok)):
                    act.wait_ge(kv_tok_psum, b + 1)
                    for h in range(HEADS):
                        ins = nc.scalar.activation(dst[:, b % 2, h, :], bank[:, 4 + b, h * HD:(h + 1) * HD], ACT.Copy,
                                                   scale=zeta[:, h:h + 1] if b < 2 else 1.0)
                    ins.then_inc(kv_tok, 1)
                out(3, mix_in[:, 0:4])
                act.wait_ge(s_tok_psum, 1)
                nc.scalar.activation(ks_tok, bank[0:NS, 4, :], ACT.Copy).then_inc(s_tok, 1)
                act.wait_ge(s_tok_psum, 2)
                nc.scalar.activation(vs_tok, bank[0:NS, 5, :], ACT.Copy).then_inc(s_tok, 1)
                act.wait_ge(q_rot, 2)
                for c in range(2):
                    act.wait_ge(o_psum, c + 1)
                    nc.scalar.activation(tmp[:, :, c * P:(c + 1) * P],
                                         bank[:, 4 + c, :].rearrange("p (h n) -> p h n", h=HEADS),
                                         ACT.Copy).then_inc(o_ready, 1)
                for m in range(4):
                    act.wait_ge(proj_psum, 4 * 5 + m + 1)
                    nc.scalar.activation(sg[:, m, :], bank[:, m, 0:T], ACT.Silu).then_inc(proj_out, 1)
                act.wait_ge(eps_ready, 1)
                for h in range(HEADS):
                    act.wait_ge(var_psum, h + 1)
                    nc.scalar.activation(vt[:, h, :], bank[:, 4 + h, 0:T], ACT.Sqrt,
                                         bias=small[:, 14:15]).then_inc(std_ready, 1)
                act.wait_ge(ncv_psum, 1)
                nc.scalar.activation(nc_rows, bank[0:2 + NS, 4, :], ACT.Copy).then_inc(ncv_rows, 1)

                def squares(half):
                    for c, (t0, n) in enumerate(TOK):
                        act.wait_ge(ht_psum1, 3 * (4 * half + 3) + c + 1)
                        i = CT * half + c
                        if i:
                            act.wait_ge(ssq2, i)
                        at = (6, 9)[half] + c
                        nc.scalar.activation(junk[0:n, 0:2, :], bank[0:n, TOKEN_BANK[half][c], :]
                                             .rearrange("p (a b) -> p a b", a=2), ACT.Square, scale=D ** -0.5,
                                             accum_out=small[0:n, at:at + 1]).then_inc(ssq2, 1)

                for m in range(KT):
                    act.wait_ge(wo_psum, m + 1)
                    nc.scalar.activation(xnt[:, m, :], bank[:, m % 2, 0:T], ACT.Copy).then_inc(wo_out, 1)
                    if m == 0:
                        act.wait_ge(small_zero, 1)
                    if m == 4:
                        squares(0)
                act.wait_ge(lg_psum, KT)
                nc.scalar.activation(lg_rows, bank[0:E, 7, 0:T], ACT.Copy).then_inc(lg_copied, 1)
                squares(1)
                act.wait_ge(top_ready, 1)
                nc.scalar.activation(gate, gate, ACT.Exp).then_inc(exp_ready, 1)

            @block.vector
            def _(dve):
                chain = [0]

                def link(ins):
                    chain[0] += 1
                    ins.then_inc(v_chain, 1)
                    dve.wait_ge(v_chain, chain[0])

                tt, ts, stt = nc.vector.tensor_tensor, nc.vector.tensor_scalar, nc.vector.scalar_tensor_tensor

                nc.vector.memset(small[:, 14:15], GN_EPS).then_inc(eps_ready, 1)
                nc.vector.memset(small[:, 6:12], 0.0).then_inc(small_zero, 1)
                for c, (t0, n) in enumerate(TOK):
                    dve.wait_ge(scale_ready, c + 1)
                    ts(h_tok[0:n, c, :], x_tok[0:n, c, :], small[0:n, 3 + c:4 + c], None, ALU.mult).then_inc(x_scaled, 1)
                dve.wait_ge(const_in, 16 * 6)
                dve.wait_ge(vec_ready, 1)
                dve.wait_ge(misc_in, 32)
                for k in range(KT):
                    ins = ts(w_rt[:, k, :], w_rt[:, k, :], vec[:, 88 + k:89 + k], None, ALU.mult)
                ins.then_inc(w_rt_ready, 1)

                def rotate(t, scaled, done):
                    cos = rope[:, 0:1, :].broadcast_to([P, HEADS, T])
                    sin = rope[:, 1:2, :].broadcast_to([P, HEADS, T])
                    tt(tmp[0:64], t[64:128], sin[64:128], ALU.mult).then_inc(v_chain, 1)
                    link(tt(tmp[64:128], t[0:64], sin[0:64], ALU.mult))
                    link(tt(t[:, :, :], t[:, :, :], cos, ALU.mult))
                    if scaled:
                        link(tt(t[:, :, :], t[:, :, :], tmp[:, :, :], ALU.add))
                        ts(t[:, :, :], t[:, :, :], HD ** -0.5, None, ALU.mult).then_inc(done, 1)
                        dve.wait_ge(done, 1)
                    else:
                        tt(t[:, :, :], t[:, :, :], tmp[:, :, :], ALU.add).then_inc(done, 1)
                        dve.wait_ge(done, 1)

                dve.wait_ge(proj_out, 4)
                chain[0] += 1
                rotate(kr, True, k_rot)
                dve.wait_ge(proj_out, 8)
                chain[0] += 1
                rotate(qr, False, q_rot)
                tt(q_xi, qr[:, :, CHUNK:2 * CHUNK], xi[:], ALU.mult).then_inc(q_rot, 1)
                tt(qk[:], qr[:, :, SEQ:T], kr[:, :, SEQ:T], ALU.mult).then_inc(qk_ready, 1)
                link(nc.vector.memset(u_pad[:, :, 0:2], 0.0))
                for c in range(2):
                    dve.wait_ge(sc_psum, c + 1)
                    tt(scores[:, c], bank[:, 6 + c, :].rearrange("p (h n) -> p h n", h=HEADS), decay,
                       ALU.mult).then_inc(sc_ready, 1)
                for m in range(4):
                    dve.wait_ge(proj_out, 16)
                    dve.wait_ge(proj_psum, 16 + m + 1)
                    tt(u_pad[:, m, 2:SEQ + 2], mix_in[:, m, 0:SEQ], bank[:, m, 0:SEQ], ALU.mult).then_inc(v_chain, 1)
                    tt(u_s[:, m, :], mix_in[:, m, SEQ:T], bank[:, m, SEQ:T], ALU.mult).then_inc(xc_used, 1)
                chain[0] += 4
                dve.wait_ge(v_chain, chain[0])
                dve.wait_ge(xc_used, 4)
                dve.wait_ge(kv_psum, 1)
                nc.vector.tensor_copy(state1, bank[:, 6, :].rearrange("p (h n) -> p h n", h=HEADS)).then_inc(s1_ready, 1)
                nc.vector.tensor_copy(nc_t[:, :, 0:2], u_pad[:, :, SEQ:SEQ + 2])
                nc.vector.tensor_copy(nc_t[:, :, 2:2 + NS], u_s[:]).then_inc(ncv_ready, 1)
                dve.wait_ge(o_psum, 2)
                dve.wait_ge(s1_ready, 1)
                for h in range(HEADS):
                    ins = stt(out=state1[:, h, :], in0=state1[:, h, :], scalar=float(gammas[h][1]),
                              in1=bank[:, 7, h * P:(h + 1) * P], op0=ALU.mult, op1=ALU.add)
                ins.then_inc(s2_ready, 1)
                cw = lambda j, m: vec[:, 12 + j * 4 + m:13 + j * 4 + m]
                past = vec[:, 24:88].rearrange("p (b j m) -> p j m b", b=NS, j=2)

                def tap(j):
                    for m in range(4):
                        if j == 0:
                            ts(mix_in[:, m, 0:SEQ], u_pad[:, m, 0:SEQ], cw(0, m), None, ALU.mult).then_inc(v_chain, 1)
                            ts(mix_in[:, m, SEQ:T], past[:, 0, m, :], cw(0, m), None, ALU.mult).then_inc(v_chain, 1)
                            continue
                        stt(out=mix_in[:, m, 0:SEQ], in0=u_pad[:, m, j:j + SEQ], scalar=cw(j, m),
                            in1=mix_in[:, m, 0:SEQ], op0=ALU.mult, op1=ALU.add).then_inc(v_chain, 1)
                        src = past[:, 1, m, :] if j == 1 else u_s[:, m, :]
                        stt(out=mix_in[:, m, SEQ:T], in0=src, scalar=cw(j, m), in1=mix_in[:, m, SEQ:T],
                            op0=ALU.mult, op1=ALU.add).then_inc(v_chain, 1)
                    chain[0] += 8
                    dve.wait_ge(v_chain, chain[0])

                for h in range(HEADS):
                    if h < 3:
                        tap(h)
                    dve.wait_ge(sq_psum, NS * (h + 1))
                    for half in range(2):
                        dve.wait_ge(kvs_psum, 2 * h + half + 1)
                        at = state[:, half * 16:half * 16 + 16, :].rearrange("p (b h) e -> p b h e", h=HEADS)[:, :, h, :]
                        stt(out=at, in0=at, scalar=float(gammas[h][0]),
                            in1=bank[:, 6 + half, :].rearrange("p (b e) -> p b e", b=4),
                            op0=ALU.mult, op1=ALU.add).then_inc(snew, 1)
                dve.wait_ge(qk_psum, 1)
                link(tt(tmp[:, :, SEQ:T], vt[:, :, SEQ:T], bank[:, 5, 0:HEADS * NS].rearrange("p (h b) -> p h b", h=HEADS),
                        ALU.mult))
                for h in range(HEADS):
                    ins = stt(out=tmp[:, h, SEQ:T], in0=bank[:, 4, h * NS:(h + 1) * NS], scalar=float(gammas[h][0]),
                              in1=tmp[:, h, SEQ:T], op0=ALU.mult, op1=ALU.add)
                ins.then_inc(o_ready, 1)
                dve.wait_ge(proj_out, 20)
                for h in range(HEADS):
                    ts(sg[:, h, :], sg[:, h, :], vec[:, 8 + h:9 + h], None, ALU.mult).then_inc(v_chain, 1)
                chain[0] += HEADS
                dve.wait_ge(v_chain, chain[0])

                def gate_conv(m):
                    dve.wait_ge(proj_psum, 24 + m + 1)
                    tt(mix_in[:, m, :], mix_in[:, m, :], bank[:, m, 0:T], ALU.mult).then_inc(gated, 1)

                for h in range(HEADS):
                    dve.wait_ge(mean_psum, h + 1)
                    link(tt(tmp[:, h, :], tmp[:, h, :], bank[:, 4 + h, 0:T], ALU.subtract))
                    tt(vt[:, h, :], tmp[:, h, :], tmp[:, h, :], ALU.mult).then_inc(dev_ready, 1)
                gate_conv(0)
                dve.wait_ge(dev_ready, HEADS)
                link(tt(tmp[:, :, :], tmp[:, :, :], sg[:, :, :], ALU.mult))
                gate_conv(1)
                for h in range(HEADS):
                    dve.wait_ge(std_ready, h + 1)
                    link(nc.vector.reciprocal(vt[:, h, :], vt[:, h, :]))
                    tt(mix_in[:, 4 + h, :], tmp[:, h, :], vt[:, h, :], ALU.mult).then_inc(mix_ready, 1)
                    if h == 2:
                        gate_conv(2)
                gate_conv(3)
                link(nc.vector.memset(rt[:, :], 0.0))
                dve.wait_ge(state1_out, 16)
                for half in range(2):
                    for c, (t0, n) in enumerate(TOK):
                        dve.wait_ge(ht_psum1, 3 * (4 * half + 3) + c + 1)
                        dve.wait_ge(ssq2, CT * half + c + 1)
                        nc.vector.tensor_copy(h_tok[0:n, c, half * 512:(half + 1) * 512],
                                              bank[0:n, TOKEN_BANK[half][c], :]).then_inc(h_ready, 1)
                dve.wait_ge(scale_ready, CT + 1)
                dve.wait_ge(lg_psum, KT + 1)
                for c, (t0, n) in enumerate(TOK):
                    ins = stt(out=logit[0:n, c, :], in0=bank[0:n, 0, c * E:(c + 1) * E], scalar=small[0:n, 9 + c:10 + c],
                              in1=b_rt[0:n, :], op0=ALU.mult, op1=ALU.add)
                ins.then_inc(logits_read, 1)
                dve.wait_ge(logits_read, 1)
                for c in range(CT):
                    link(nc.vector.max(top8[:, c, :], logit[:, c, :]))
                    nc.vector.max_index(idx8[:, c, :], top8[:, c, :], logit[:, c, :]).then_inc(v_chain, 1)
                    chain[0] += 1
                top = top8[:, :, 0:TOP]
                tt(gate, top, top8[:, :, 0:1].broadcast_to([P, CT, TOP]), ALU.subtract).then_inc(top_ready, 1)
                dve.wait_ge(v_chain, chain[0])
                link(nc.vector.tensor_copy(idxf, idx8[:, :, 0:TOP]))
                iota = route[:, 0:E]
                each = [P, CT * TOP, E]
                link(tt(onehot.rearrange("p c k e -> p (c k) e"), iota.rearrange("p (a e) -> p a e", a=1).broadcast_to(each),
                        idxf.rearrange("p c (k a) -> p (c k) a", a=1).broadcast_to(each), ALU.is_equal))
                link(nc.vector.tensor_reduce(mask, onehot.rearrange("p c k e -> p c e k"), AX.X, ALU.add))
                tt(mask, mask, route[:, E + CT + NS:].rearrange("p (c a) -> p c a", a=1).broadcast_to([P, CT, E]),
                   ALU.mult).then_inc(mask_ready, 1)
                dve.wait_ge(gffn_in, 16)
                dve.wait_ge(h_ready, 2 * CT)
                for c, (t0, n) in enumerate(TOK):
                    stt(out=xn2[0:n, c, :], in0=h_tok[0:n, c, :], scalar=small[0:n, 9 + c:10 + c], in1=g_ffn[0:n, :],
                        op0=ALU.mult, op1=ALU.mult)
                dve.wait_ge(rank_psum, 1)
                link(stt(out=rankm[:], in0=bank[:, 3, 0:CT * E].rearrange("p (c e) -> p c e", c=CT), scalar=1.0,
                         in1=mask, op0=ALU.add, op1=ALU.mult))
                link(ts(rankm[:], rankm[:], -1.0, None, ALU.add))
                dve.wait_ge(slots_in, 16)
                tt(pick[:], slots[:].rearrange("p (a s) -> p a s", a=1).broadcast_to([P, CT, P]),
                   rankm[:, :, 0:1].broadcast_to([P, CT, P]), ALU.is_equal).then_inc(pick_ready, 1)
                dve.wait_ge(rank_psum, 2)
                link(nc.vector.tensor_copy(counts[:], bank[:, 4, 0:E]))
                link(nc.vector.tensor_reduce(most[:], counts[:], AX.X, ALU.max))
                dve.wait_ge(exp_ready, 1)
                link(nc.vector.tensor_reduce(gsum, gate, AX.X, ALU.add))
                link(nc.vector.reciprocal(gsum, gsum))
                link(tt(gate, gate, gsum.rearrange("p (c a) -> p c a", a=1).broadcast_to([P, CT, TOP]), ALU.mult))
                link(tt(prod.rearrange("p c k e -> p (c k) e"), onehot.rearrange("p c k e -> p (c k) e"),
                        gate.rearrange("p c (k a) -> p (c k) a", a=1).broadcast_to(each), ALU.mult))
                link(nc.vector.tensor_reduce(meta[:, :, :, 1], prod.rearrange("p c k e -> p c e k"), AX.X, ALU.add))
                link(nc.vector.tensor_copy(meta[:, :, :, 0], route[:, E:E + CT].rearrange("p (c a) -> p c a", a=1)
                                           .broadcast_to([P, CT, E])))

        with ExitStack() as ph:
            sb = make(ph)
            w_high = sb("w_high", [P, SPLIT, 2 * FF], F32R)
            w_low = sb("w_low", [P, SPLIT, 2 * FF], F32R)
            xs = sb("xs", [P, KT, 2 * CAP], F32R)
            h_rows = sb("h_rows", [P, 2 * FF])
            hb = sb("hb", [P, 2 * FF // P, CAP])
            sig = sb("sig", [P, KT, CAP])
            av = sb("av", [P, KT, 2 * CAP], F32R)
            yg = sb("yg", [CAP, D])
            rank_now = sb("rank_now", [P, CT])
            slot_info = sb("slot_info", [P, E, 2])
            slot_row = sb("slot_row", [P, 1], I32)
            slot_gate = sb("slot_gate", [P, 1])
            nobody = sb("nobody", [P, 2])
            gt = sb("gt", [E, T])
            st = sb("st", [P, 16])
            yl = h_rows[0:CAP, 0:D]
            fin = raw_up[:, 0:2, :].rearrange("p a b -> p (a b)")[:, 0:CT * D].rearrange("p (c d) -> p c d", c=CT)
            g_fin = x_tok[:, 1, :]
            b_down_sb = x_tok[0:E, 0, :]

            last_landed = [sem(f"last_landed{i}") for i in range(DC)]
            high_done = sem("high_done")
            low_done = sem("low_done")
            mm_done = sem("mm_done")
            rank_taken = sem("rank_taken")
            xt_psum = sem("xt_psum")
            xs_high = sem("xs_high")
            xs_ready = sem("xs_ready")
            info_ready = sem("info_ready")
            slot_ready = sem("slot_ready")
            h_copied = sem("h_copied")
            ht_psum = sem("ht_psum")
            biased = sem("biased")
            clamped = sem("clamped")
            lin_ready = sem("lin_ready")
            sig_ready = sem("sig_ready")
            act_ready = sem("act_ready")
            act_high = sem("act_high")
            av_ready = sem("av_ready")
            yl_ready = sem("yl_ready")
            y_ready = sem("y_ready")
            scattered = sem("scattered")
            nobody_set = sem("nobody_set")
            all_added = sem("all_added")
            pool_passed = sem("pool_passed")
            pe_passed = sem("pe_passed")
            sp_passed = sem("sp_passed")
            ranks_moved = sem("ranks_moved")
            gt_psum = sem("gt_psum")
            gt_ready = sem("gt_ready")
            gb_psum = sem("gb_psum")
            bd_in = sem("bd_in")
            gf_in = sem("gf_in")
            fin_in = [sem(f"fin_in{c}") for c in range(CT)]
            fin_added = sem("fin_added")
            fin_scale = sem("fin_scale")
            fin_chain = sem("fin_chain")
            fin_ssq = sem("fin_ssq")
            fin_ready = sem("fin_ready")
            stored = sem("stored")

            block = ph.enter_context(nc.Block())
            H, HT, Y = 0, 4, 6
            X, INFO = HT, HT + 1
            LAST = E * CPR
            BIAS_BANK = (6, 2, 4)

            def place(n, j):
                if isinstance(n, int) and n == 0:
                    return j
                return CPR * n - DC + (j - UC if isinstance(n, int) and n == E else j)

            def ups_done(n):
                return UC if isinstance(n, int) and n == 0 else CPR * n - DC + UC

            def downs_done(n):
                return LAST if isinstance(n, int) and n == E - 1 else CPR * n + 2 * CPR - DC

            def y_bank(n):
                return H if isinstance(n, int) and n == E else Y

            def raw(n, j):
                if j < UC:
                    return raw_up[:, j, :]
                return (raw_up if isinstance(n, int) and n == E else raw_down)[:, j - UC, :]

            def each_overflow(eng, body, at_round=None):
                k = eng.alloc_register(f"rounds_{eng.engine.name}")
                eng.reg_mov(k, 0)
                greatest = eng.value_load(most[0:1, 0:1], min_val=0, max_val=T)
                with eng.If(greatest > CAP):
                    with eng.Fori(1, OVER) as r:
                        if at_round is not None:
                            at_round(r)
                        with eng.Fori(0, E) as e:
                            count = eng.value_load(counts[0:1, bass.ds(e, 1)], min_val=0, max_val=T)
                            with eng.If(count > r * CAP):
                                body(e, eng.snap(k, min_val=0, max_val=E * OVER))
                                eng.reg_add(k, k, 1)
                return eng.snap(k, min_val=0, max_val=E * OVER)

            @block.sync
            def _(sp):
                def load(e, j):
                    if j < UC:
                        sp.dma_start(raw_up[:, j, :], w_up_v[e, j]).then_inc(landed[j], 16)
                    else:
                        load_down(sp, e, j - UC)

                for j in range(UC):
                    sp.wait_ge(low_done, j + 1)
                    load(1, j)
                with sp.Fori(2, E) as n:
                    for j in range(CPR):
                        sp.wait_ge(low_done, place(n, j) - CPR + 1)
                        load(n if j < UC else n - 1, j)
                for i in range(DC):
                    sp.wait_ge(low_done, place(E - 1, i) + 1)
                    sp.dma_start(raw_up[:, i, :].rearrange("p (k n) -> p k n", k=2), w_down_v[E - 1, i]
                                 ).then_inc(last_landed[i], 16)
                def overflow(e, k):
                    sp.wait_ge(mm_done, k * CPR + LAST)
                    for j in range(CPR):
                        load(e, j)

                k = each_overflow(sp, overflow)
                sp.wait_ge(xt_psum, k + E)
                sp.sem_inc(sp_passed, 1)
                sp.dma_start(b_down_sb, b_down[0]).then_inc(bd_in, 16)
                sp.dma_start(g_fin, norm_final.rearrange("(a d) -> a d", a=1).partition_broadcast(P)[:, 0, :]).then_inc(gf_in, 16)
                sp.wait_ge(all_added, 1)
                for c, (t0, n) in enumerate(TOK):
                    sp.dma_start(fin[0:n, c, :], acc_dram[t0:t0 + n, :]).then_inc(fin_in[c], 16)
                for c in range(2):
                    sp.wait_ge(fin_ready, c + 1)
                    sp.dma_start(y_prompt[0, c * P:(c + 1) * P, :], fin[:, c, :]).then_inc(stored, 16)
                sp.wait_ge(fin_ready, 3)
                sp.dma_start(y_sample.rearrange("b s d -> (b s) d"), fin[0:NS, 2, :]).then_inc(stored, 16)
                sp.wait_ge(stored, 48)
                sp.wait_ge(out_done, 16 * 3)

            @block.gpsimd
            def _(pool):
                def carry():
                    pool.sem_inc(pool_passed, 1)

                def choose(n, e):
                    pool.wait_ge(xt_psum, n)
                    pool.wait_ge(pick_ready, n)
                    carry()
                    pool.tensor_copy(rank_now[:], rankm[:, :, e].rearrange("p c a -> p (c a)")).then_inc(rank_taken, 1)
                    pool.wait_ge(rank_taken, n)
                    carry()
                    for c in range(CT):
                        ins = pool.tensor_scalar(pick[:, c, :], slots[:], rank_now[:, c:c + 1], None, ALU.is_equal)
                    ins.then_inc(pick_ready, 1)

                def add_y(n, e):
                    if not (isinstance(n, int) and n == 0):
                        pool.wait_ge(scattered, 16 * n)
                    pool.wait_ge(info_ready, n + 1)
                    carry()
                    pool.tensor_copy(slot_row[:], slot_info[:, e, 0]).then_inc(slot_ready, 1)
                    pool.tensor_copy(slot_gate[:], slot_info[:, e, 1]).then_inc(slot_ready, 1)
                    pool.wait_ge(y_ready, n + 1)
                    pool.wait_ge(slot_ready, 2 * n + 2)
                    carry()
                    pool.indirect_dma_start(acc_dram, bass.IndirectOffsetOnAxis(ap=slot_row[0:CAP, 0:1], axis=0), yg[:],
                                            None, bounds_check=T - 1, oob_is_err=False,
                                            compute_op=ALU.add).then_inc(scattered, 16)

                for n in range(1, 3):
                    choose(n, slice(n, n + 1))
                pool.wait_ge(acc_init, 16 * CT)
                choose(3, slice(3, 4))
                add_y(0, slice(0, 1))
                with pool.Fori(3, E - 1) as n:
                    choose(n + 1, bass.ds(n + 1, 1))
                    add_y(n - 2, bass.ds(n - 2, 1))
                for n in range(E - 3, E):
                    add_y(n, slice(n, n + 1))

                def next_ranks(r):
                    pool.wait_ge(pick_ready, E)
                    pool.tensor_scalar(rankm[:], rankm[:], -float(CAP), None, ALU.add).then_inc(ranks_moved, 1)
                    pool.wait_ge(ranks_moved, r)
                    carry()

                def overflow(e, k):
                    choose(k + E, bass.ds(e, 1))
                    add_y(k + E, slice(0, 1))

                k = each_overflow(pool, overflow, next_ranks)
                pool.wait_ge(scattered, k * 16 + 16 * E)
                carry()
                pool.sem_inc(all_added, 1)
                for c, (t0, n) in enumerate(TOK):
                    pool.wait_ge(fin_ssq, c + 1)
                    pool.tensor_scalar(st[0:n, 3 + c:4 + c], st[0:n, c:c + 1], RMS_EPS, None, ALU.add).then_inc(fin_chain, 1)
                    pool.wait_ge(fin_chain, c + 1)
                    pool.tensor_tensor(st[0:n, 3 + c:4 + c], st[0:n, 3 + c:4 + c], minus_half[0:n], ALU.pow).then_inc(fin_scale, 1)

            @block.tensor
            def _(pe):
                def turn_x(n, e=None, part=None):
                    if not part:
                        pe.wait_ge(pick_ready, n + 1)
                        if not (isinstance(n, int) and n < 2):
                            pe.wait_ge(biased, n - 1)
                    e = n if e is None else e
                    for k in range(KT) if part is None else (2 * part, 2 * part + 1):
                        for c in range(CT):
                            pe.matmul(bank[:, X, k * CAP:(k + 1) * CAP], x_tok[:, c, k * P:(k + 1) * P],
                                      pick[:, c, 0:CAP], start=(c == 0), stop=(c == CT - 1))
                    if part is not None and part < 3:
                        return
                    for c in range(CT):
                        mm = pe.matmul(bank[:, INFO, 0:2], pick[:, c, :], meta[:, c, e, :] if isinstance(e, int)
                                       else meta[:, c, bass.ds(e, 1), :].rearrange("p a two -> p (a two)"),
                                       start=(c == 0), stop=(c == CT - 1))
                    mm.then_inc(xt_psum, 1)

                def turn_h(n, gathered):
                    pe.wait_ge(h_copied, 4 * n + 4)
                    pe.wait_ge(xs_ready, gathered)
                    pe.wait_ge(info_ready, gathered)
                    for j in range(2 * FF // P):
                        mm = pe.matmul(bank[:, HT + j // 8, (j % 8) * CAP:(j % 8 + 1) * CAP],
                                       h_rows[:, j * P:(j + 1) * P], halves[:], start=True, stop=True)
                    mm.then_inc(ht_psum, 1)

                def products(n, j):
                    pos, buf = place(n, j), j % SPLIT
                    pe.wait_ge(high_done, pos + 1)
                    for w in (w_high, w_low):
                        if w is w_low:
                            pe.wait_ge(low_done, pos + 1)
                        for q in range(4):
                            if j < UC:
                                if j == 0 and w is w_high and not (isinstance(n, int) and n == 0):
                                    pe.wait_ge(h_copied, 4 * n - 3 + q)
                                mm = pe.matmul(bank[:, H + q, :], xs[:, j, :], w[:, buf, q * 512:(q + 1) * 512],
                                               start=(j == 0 and w is w_high), stop=(j == UC - 1 and w is w_low))
                            else:
                                i = j - UC
                                mm = pe.matmul(bank[:, y_bank(n) + q % 2, :], av[:, 2 * i + q // 2, :],
                                               w[:, buf, q * 512:(q + 1) * 512],
                                               start=(i == 0 and w is w_high and q < 2),
                                               stop=(i == DC - 1 and w is w_low and q >= 2))
                    mm.then_inc(mm_done, 1)

                def ups(n, last=False):
                    pe.wait_ge(xs_ready, n + 1)
                    for j in range(UC):
                        products(n, j)
                        if j == 0 and not (isinstance(n, int) and n == 0):
                            turn_h(n - 1, n + 1)
                        if 3 <= j < 7 and not last:
                            turn_x(n + 1, part=j - 3)

                def downs(n):
                    pe.wait_ge(av_ready, n)
                    if not (isinstance(n, int) and n in (1, E)):
                        pe.wait_ge(y_ready, n - 1)
                    for j in range(UC, CPR):
                        products(n, j)
                        if j == UC and isinstance(n, int) and n == E - 1:
                            turn_h(E - 1, E)

                turn_x(0)
                ups(0)
                ups(1)
                downs(1)
                with pe.Fori(2, E - 1) as n:
                    ups(n)
                    downs(n)
                ups(E - 1, last=True)
                downs(E - 1)
                for c, (t0, n) in enumerate(TOK):
                    mm = pe.transpose(bank[0:E, H + 2, t0:t0 + n], meta[0:n, c, :, 1], ident[0:n, 0:n])
                mm.then_inc(gt_psum, 1)
                downs(E)
                pe.wait_ge(gt_ready, 1)

                def overflow(e, k):
                    n = k + E
                    pe.wait_ge(y_ready, n)
                    turn_x(n, e)
                    pe.wait_ge(xs_ready, n + 1)
                    for i in range(UC):
                        pe.wait_ge(landed[i], k * 16 + 16 * (E + 1))
                        for q in range(4):
                            mm = pe.matmul(bank[:, H + q, :], xs[:, i, :].bitcast(F32),
                                           raw_up[:, i, q * 512:(q + 1) * 512], start=(i == 0), stop=(i == UC - 1))
                        mm.then_inc(mm_done, 1)
                    turn_h(n, n + 1)
                    pe.wait_ge(av_ready, n + 1)
                    for i in range(DC):
                        pe.wait_ge(landed[UC + i], k * 16 + 16 * E)
                        for q in range(4):
                            mm = pe.matmul(bank[:, Y + q % 2, :], av[:, 2 * i + q // 2, :].bitcast(F32),
                                           raw_down[:, i, q * 512:(q + 1) * 512],
                                           start=(i == 0 and q < 2), stop=(i == DC - 1 and q >= 2))
                        mm.then_inc(mm_done, 1)
                    pe.wait_ge(y_ready, n + 1)
                    pe.sem_inc(pe_passed, 1)

                each_overflow(pe, overflow)
                pe.wait_ge(y_ready, E - 1)
                pe.wait_ge(bd_in, 16)
                for c in (1, 2, 0):
                    t0, n = TOK[c]
                    for q in range(2):
                        mm = pe.matmul(bank[0:n, BIAS_BANK[c] + q, :], gt[:, t0:t0 + n], b_down_sb[:, q * 512:(q + 1) * 512],
                                       start=True, stop=True)
                mm.then_inc(gb_psum, 1)

            @block.scalar
            def _(act):
                def high(n, j):
                    pos = place(n, j)
                    src = raw(n, j)
                    e = n if j < UC else n - 1
                    if isinstance(n, int) and n == E:
                        act.wait_ge(last_landed[j - UC], 16)
                    else:
                        act.wait_ge(landed[j], 16 * e + 16)
                    if not (isinstance(pos, int) and pos < SPLIT):
                        act.wait_ge(mm_done, pos - SPLIT + 1)
                    nc.scalar.activation(w_high[:, j % SPLIT, :], src, ACT.Copy).then_inc(high_done, 1)

                def x_high(n, used):
                    act.wait_ge(xt_psum, n + 1)
                    if used is not None:
                        act.wait_ge(mm_done, used)
                    nc.scalar.activation(xs[:, :, 0:CAP], bank[:, X, :].rearrange("p (k s) -> p k s", k=KT),
                                         ACT.Copy).then_inc(xs_high, 1)

                def copy_h(n, used):
                    act.wait_ge(mm_done, used)
                    if not (isinstance(n, int) and n < 1):
                        act.wait_ge(ht_psum, n)
                    if not (isinstance(n, int) and n < 2):
                        act.wait_ge(y_ready, n - 1)
                    for q in range(4):
                        nc.scalar.activation(h_rows[:, q * 512:(q + 1) * 512], bank[:, H + q, :],
                                             ACT.Copy).then_inc(h_copied, 1)

                def sigmoid(n):
                    act.wait_ge(clamped, n + 1)
                    nc.scalar.activation(sig[:], hb[:, 0:KT, :], ACT.Sigmoid, scale=ALPHA).then_inc(sig_ready, 1)

                def act_split(n, used):
                    act.wait_ge(act_ready, n + 1)
                    if used is not None:
                        act.wait_ge(mm_done, used)
                    nc.scalar.activation(av[:, :, 0:CAP], sig[:], ACT.Copy).then_inc(act_high, 1)

                def y_low(n, used, turned, at=Y):
                    act.wait_ge(mm_done, used)
                    act.wait_ge(slot_ready, 2 * n + 2)
                    act.wait_ge(ht_psum, turned)
                    nc.scalar.activation(yl.rearrange("p (a b) -> p a b", a=2), bank[CAP:2 * CAP, at:at + 2, :],
                                         ACT.Copy, scale=slot_gate[CAP:2 * CAP, 0:1]).then_inc(yl_ready, 1)

                def step(n, last=False, begun=0):
                    early = isinstance(n, int) and n < 2
                    for j in range(begun, 4):
                        high(n, j)
                    if not early:
                        y_low(n - 2, downs_done(n - 2), n)
                    high(n, 4)
                    sigmoid(n - 1)
                    high(n, 5)
                    act_split(n - 1, None if early else downs_done(n - 2))
                    for j in range(6, 11):
                        high(n, j)
                    if not last:
                        x_high(n + 1, ups_done(n))
                    copy_h(n, ups_done(n))
                    high(n, 11)

                for j in range(SPLIT):
                    high(0, j)
                x_high(0, None)
                for j in range(SPLIT, UC):
                    high(0, j)
                for j in range(3):
                    high(1, j)
                x_high(1, ups_done(0))
                copy_h(0, ups_done(0))
                step(1, begun=3)
                step(2)
                with act.Fori(3, E - 1) as n:
                    step(n)
                step(E - 1, last=True)
                sigmoid(E - 1)
                high(E, 8)
                act_split(E - 1, downs_done(E - 2))
                act.wait_ge(gt_psum, 1)
                nc.scalar.activation(gt[:], bank[0:E, H + 2, 0:T], ACT.Copy).then_inc(gt_ready, 1)
                high(E, 9)
                high(E, 10)
                y_low(E - 2, downs_done(E - 2), E)
                high(E, 11)
                act.wait_ge(y_ready, E - 1)
                y_low(E - 1, LAST, E, H)

                def overflow(e, k):
                    n = k + E
                    x_high(n, k * CPR + LAST)
                    act.wait_ge(y_ready, n)
                    copy_h(n, k * CPR + LAST + UC)
                    sigmoid(n)
                    act_split(n, k * CPR + LAST)
                    y_low(n, k * CPR + LAST + CPR, n + 1)

                each_overflow(act, overflow)
                for c, (t0, n) in enumerate(TOK):
                    act.wait_ge(fin_added, c + 1)
                    if c:
                        act.wait_ge(fin_ssq, c)
                    nc.scalar.activation(h_rows[0:n, 0:D], fin[0:n, c, :], ACT.Square, scale=D ** -0.5,
                                         accum_out=st[0:n, c:c + 1]).then_inc(fin_ssq, 1)

            @block.vector
            def _(dve):
                tt, ts, stt = nc.vector.tensor_tensor, nc.vector.tensor_scalar, nc.vector.scalar_tensor_tensor

                def low(n, j):
                    src = raw(n, j)
                    dve.wait_ge(high_done, place(n, j) + 1)
                    tt(w_low[:, j % SPLIT, :], src, w_high[:, j % SPLIT, :].bitcast(F32),
                       ALU.subtract).then_inc(low_done, 1)

                def x_low(n, e):
                    dve.wait_ge(xs_high, n + 1)
                    tt(xs[:, :, CAP:2 * CAP], bank[:, X, :].rearrange("p (k s) -> p k s", k=KT),
                       xs[:, :, 0:CAP].bitcast(F32), ALU.subtract).then_inc(xs_ready, 1)
                    tt(slot_info[:, e, :], bank[:, INFO, 0:2].rearrange("p (a b) -> p a b", a=1),
                       nobody[:].rearrange("p (a b) -> p a b", a=1), ALU.add).then_inc(info_ready, 1)

                def bias_clamp(n, e):
                    dve.wait_ge(ht_psum, n + 1)
                    if not (isinstance(n, int) and n == 0):
                        dve.wait_ge(act_ready, n)
                    tt(hb[:], bank[:, HT:HT + 2, :].rearrange("p a (j s) -> p (a j) s", s=CAP),
                       bias_up[:, :, e].broadcast_to([P, 2 * FF // P, CAP]), ALU.add).then_inc(biased, 1)
                    dve.wait_ge(biased, n + 1)
                    ts(hb[:, 0:KT, :], hb[:, 0:KT, :], LIMIT, None, ALU.min).then_inc(clamped, 1)
                    ts(hb[:, KT:, :], hb[:, KT:, :], LIMIT, -LIMIT, ALU.min, ALU.max).then_inc(lin_ready, 1)

                def activate(n):
                    dve.wait_ge(sig_ready, n + 1)
                    dve.wait_ge(clamped, n + 1)
                    dve.wait_ge(lin_ready, 2 * n + 1)
                    stt(out=hb[:, KT:, :], in0=hb[:, KT:, :], scalar=1.0, in1=hb[:, 0:KT, :],
                        op0=ALU.add, op1=ALU.mult).then_inc(lin_ready, 1)
                    dve.wait_ge(lin_ready, 2 * n + 2)
                    tt(sig[:], sig[:], hb[:, KT:, :], ALU.mult).then_inc(act_ready, 1)

                def act_low(n):
                    dve.wait_ge(act_high, n + 1)
                    dve.wait_ge(act_ready, n + 1)
                    tt(av[:, :, CAP:2 * CAP], sig[:], av[:, :, 0:CAP].bitcast(F32), ALU.subtract).then_inc(av_ready, 1)

                def y_sum(n, at=Y):
                    dve.wait_ge(yl_ready, n + 1)
                    if not (isinstance(n, int) and n == 0):
                        dve.wait_ge(scattered, 16 * n)
                    stt(out=yg[:].rearrange("p (a b) -> p a b", a=2), in0=bank[0:CAP, at:at + 2, :],
                        scalar=slot_gate[0:CAP, 0:1], in1=yl.rearrange("p (a b) -> p a b", a=2),
                        op0=ALU.mult, op1=ALU.add).then_inc(y_ready, 1)

                def at(e):
                    return slice(e, e + 1) if isinstance(e, int) else bass.ds(e, 1)

                def step(n, last=False, begun=0):
                    for j in range(begun, 4):
                        low(n, j)
                    bias_clamp(n - 1, at(n - 1))
                    if not (isinstance(n, int) and n < 2):
                        y_sum(n - 2)
                    low(n, 4)
                    activate(n - 1)
                    low(n, 5)
                    act_low(n - 1)
                    for j in range(6, 11):
                        low(n, j)
                    if not last:
                        x_low(n + 1, at(n + 1))
                    low(n, 11)

                nc.vector.memset(nobody[:, 0:1], float(NOBODY)).then_inc(nobody_set, 1)
                nc.vector.memset(nobody[:, 1:2], 0.0).then_inc(nobody_set, 1)
                dve.wait_ge(nobody_set, 2)
                for j in range(SPLIT):
                    low(0, j)
                x_low(0, at(0))
                for j in range(SPLIT, UC):
                    low(0, j)
                for j in range(3):
                    low(1, j)
                x_low(1, at(1))
                step(1, begun=3)
                step(2)
                with dve.Fori(3, E - 1) as n:
                    step(n)
                step(E - 1, last=True)
                bias_clamp(E - 1, at(E - 1))
                activate(E - 1)
                low(E, 8)
                act_low(E - 1)
                low(E, 9)
                low(E, 10)
                y_sum(E - 2)
                low(E, 11)
                y_sum(E - 1, H)

                def overflow(e, k):
                    n = k + E
                    dve.wait_ge(slot_ready, 2 * n)
                    x_low(n, at(0))
                    bias_clamp(n, at(e))
                    activate(n)
                    act_low(n)
                    y_sum(n)

                each_overflow(dve, overflow)
                for c, (t0, n) in enumerate(TOK):
                    dve.wait_ge(fin_in[c], 16)
                    dve.wait_ge(gb_psum, 1)
                    rows = fin[0:n, c, :].rearrange("p (a b) -> p a b", a=2)
                    tt(rows, rows, bank[0:n, BIAS_BANK[c]:BIAS_BANK[c] + 2, :], ALU.add).then_inc(fin_added, 1)
                dve.wait_ge(gf_in, 16)
                dve.wait_ge(fin_added, 3)
                for c, (t0, n) in enumerate(TOK):
                    dve.wait_ge(fin_scale, c + 1)
                    stt(out=fin[0:n, c, :], in0=fin[0:n, c, :], scalar=st[0:n, 3 + c:4 + c], in1=g_fin[0:n, :],
                        op0=ALU.mult, op1=ALU.mult).then_inc(fin_ready, 1)


def shape_constants():
    import numpy as np

    f = np.float32
    sq = np.zeros((P, 9, P), f)
    sq[:, 0] = np.eye(P)
    sq[:, 1, 0:CAP] = np.concatenate([np.eye(CAP), np.eye(CAP)])
    sq[:, 2] = np.triu(np.ones((P, P)), 1)
    sq[:, 3] = 1.0 / HD
    sq[:, 4] = 1.0
    lg = np.log(f(1.0) - f(2.0) ** (f(-5.0) - np.arange(HEADS, dtype=f)))
    pos = np.arange(CHUNK, dtype=f)
    diff = pos[None, :] - pos[:, None]
    xi = np.zeros((P, HEADS + 1, CHUNK), f)
    for h in range(HEADS):
        sq[:, 5 + h] = np.where(diff >= 0, np.exp(lg[h] * np.maximum(diff, 0)), 0)
        xi[:, h] = np.exp(lg[h] * (pos + 1))[None, :]
        xi[:, HEADS, h] = np.exp(lg[h] * (CHUNK - 1 - pos))
    half = HD // 2
    inv = (f(10000.0) ** (-np.arange(half, dtype=f) / f(half))).astype(f)
    at = np.concatenate([np.arange(SEQ), np.full(NS, 2048)]).astype(f)
    ang = (at[None, :] * inv[:, None]).astype(f)
    rope = np.zeros((P, 2, T), f)
    rope[:half, 0] = rope[half:, 0] = np.cos(ang)
    rope[:half, 1] = np.sin(ang)
    rope[half:, 1] = -np.sin(ang)
    route = np.zeros((P, E + 2 * CT + NS), f)
    route[:, :E] = np.arange(E)
    for c in range(CT):
        route[:, E + c] = np.arange(P) + c * P - NOBODY
        route[:, E + CT + NS + c] = np.arange(P) + c * P < T
    route[:NS, E + CT:E + CT + NS] = np.eye(NS)
    slots = np.tile(np.arange(P, dtype=f) % CAP, (P, 1))
    gammas = [(float(np.exp(lg[h])), float(np.exp(lg[h] * f(CHUNK)))) for h in range(HEADS)]
    return {"c_square": sq, "c_rope": rope, "c_xi": xi, "c_route": route, "c_slots": slots}, gammas


_INS = ["x_prompt", "x_sample", "state_conv", "state_ret", "norm_mix", "w_in", "conv_w", "ret_norm", "w_out",
        "norm_ffn", "w_router", "b_router", "w_up", "b_up", "w_down", "b_down", "norm_final"]
_OUTS = [(1, SEQ, D), (NS, 1, D), (1, 1, 2, CONV_W), (1, 1, HEADS, HD, HD), (1, NS, 2, CONV_W),
         (1, NS, HEADS, HD, HD)]


def build(nc, inputs):
    import numpy as np

    consts, gammas = shape_constants()
    arrays, args = {}, []
    for name, a in [(n, inputs[n]) for n in _INS] + list(consts.items()):
        a = np.ascontiguousarray(a)
        arrays[f"in_{name}"] = a
        args.append(nc.dram_tensor(f"in_{name}", a.shape, mybir.dt.from_np(a.dtype), kind="ExternalInput").ap())
    outs = [nc.dram_tensor(f"out_{i}", shape, F32, kind="ExternalOutput").ap() for i, shape in enumerate(_OUTS)]
    hybrid_layer(nc, *args, gammas, *outs)
    return arrays


def kernel(**inputs):
    import concourse.bacc as _bacc
    from concourse.bass_utils import run_bass_kernel_spmd as _run

    nc = _bacc.Bacc("TRN2", target_bir_lowering=False, num_devices=1)
    arrays = build(nc, inputs)
    r = _run(nc, [arrays], core_ids=[0])
    return tuple(r.results[0][f"out_{i}"] for i in range(len(_OUTS)))
```
